# Optimizing a Trainium2 kernel written in Bass

```python
import jax, jax.numpy as jnp
from jax import lax
import numpy as np
import math

D_MODEL = 2048
BATCH = 1
SEQ = 256
DEPTH = 2

N_MIXERS = 4
HEAD_DIM = 128
N_HEADS = D_MODEL // HEAD_DIM
N_KV_HEADS = 4
GROUP = N_HEADS // N_KV_HEADS
INNER = N_HEADS * HEAD_DIM
KV_WIDTH = N_KV_HEADS * HEAD_DIM
IDX_HEADS = 16
IDX_DIM = 64
DSA_TOPK = 256
MOBA_BLOCK = 256
MOBA_TOPK = 3
RET_HEADS = 8
RET_QK_DIM = D_MODEL // RET_HEADS
RET_V_DIM = 2 * RET_QK_DIM
RET_INNER = RET_HEADS * RET_V_DIM
RET_CHUNK = 128
Q_BLOCK = 128
ROPE_THETA = 10000.0
EPS = 1e-6
NEG = -1e30

A_WIDTHS = (INNER, KV_WIDTH, KV_WIDTH, INNER, IDX_HEADS * IDX_DIM, IDX_DIM, IDX_HEADS)
B_WIDTHS = (INNER, KV_WIDTH, KV_WIDTH, INNER)
C_WIDTHS = (RET_HEADS * RET_QK_DIM, RET_HEADS * RET_QK_DIM, RET_INNER, RET_INNER)
D_WIDTHS = (INNER, INNER, INNER, INNER, N_HEADS)


def n_layers_of(m):
    return len(range(m, DEPTH, N_MIXERS))

def split_cols(z, widths):
    cuts = [int(c) for c in np.cumsum(widths)[:-1]]
    return jnp.split(z, cuts, axis=-1)

def rms_norm(x, g):
    xf = x.astype(jnp.float32)
    y = xf * lax.rsqrt(jnp.mean(xf * xf, axis=-1, keepdims=True) + EPS)
    return (y * g.astype(jnp.float32)).astype(x.dtype)

def rope(x, pos):
    d = x.shape[-1]
    inv = ROPE_THETA ** (-jnp.arange(0, d, 2, dtype=jnp.float32) / d)
    ang = pos.astype(jnp.float32)[:, None] * inv[None, :]
    cos = jnp.cos(ang)[None, :, None, :]
    sin = jnp.sin(ang)[None, :, None, :]
    x1, x2 = jnp.split(x.astype(jnp.float32), 2, axis=-1)
    return jnp.concatenate([x1 * cos - x2 * sin, x1 * sin + x2 * cos], axis=-1).astype(x.dtype)

def sweep_query_blocks(fn, T):
    starts = jnp.arange(T // Q_BLOCK, dtype=jnp.int32) * Q_BLOCK
    out = lax.map(fn, starts)
    _, B, _, w = out.shape
    return jnp.swapaxes(out, 0, 1).reshape(B, T, w)

def batched_gather(src, idx):
    return jax.vmap(lambda s, i: s[i])(src, idx)

def dsa_mixer(h, w_in, q_g, k_g, w_out):
    B, T, _ = h.shape
    pos = jnp.arange(T, dtype=jnp.int32)
    q, k, v, gate, qi, ki, wi = split_cols(h @ w_in, A_WIDTHS)
    q = rope(rms_norm(q.reshape(B, T, N_HEADS, HEAD_DIM), q_g), pos)
    k = rope(rms_norm(k.reshape(B, T, N_KV_HEADS, HEAD_DIM), k_g), pos)
    v = v.reshape(B, T, N_KV_HEADS, HEAD_DIM)
    qi = rope(qi.reshape(B, T, IDX_HEADS, IDX_DIM), pos).astype(jnp.float32)
    ki = rope(ki.reshape(B, T, 1, IDX_DIM), pos)[:, :, 0].astype(jnp.float32)
    wi = wi.astype(jnp.float32) * IDX_HEADS ** -0.5
    n_keep = min(DSA_TOPK, T // 4)
    scale = HEAD_DIM ** -0.5

    def block(start):
        tq = start + jnp.arange(Q_BLOCK, dtype=jnp.int32)
        qib = lax.dynamic_slice_in_dim(qi, start, Q_BLOCK, axis=1)
        wib = lax.dynamic_slice_in_dim(wi, start, Q_BLOCK, axis=1)
        rel = jax.nn.relu(jnp.einsum('bqhd,bsd->bqhs', qib, ki) * IDX_DIM ** -0.5)
        score = jnp.einsum('bqh,bqhs->bqs', wib, rel)
        causal = pos[None, :] <= tq[:, None]
        score = jnp.where(causal[None], score, NEG)
        _, sel = lax.top_k(score, n_keep)
        valid = sel <= tq[None, :, None]
        k_sel = batched_gather(k, sel)
        v_sel = batched_gather(v, sel)
        qb = lax.dynamic_slice_in_dim(q, start, Q_BLOCK, axis=1).reshape(B, Q_BLOCK, N_KV_HEADS, GROUP, HEAD_DIM)
        logits = jnp.einsum('bqgrd,bqkgd->bqgrk', qb, k_sel).astype(jnp.float32) * scale
        logits = jnp.where(valid[:, :, None, None, :], logits, NEG)
        p = jax.nn.softmax(logits, axis=-1).astype(v.dtype)
        o = jnp.einsum('bqgrk,bqkgd->bqgrd', p, v_sel)
        return o.reshape(B, Q_BLOCK, INNER)

    o = sweep_query_blocks(block, T)
    return (jax.nn.silu(gate) * o) @ w_out

def moba_mixer(h, w_in, q_g, k_g, w_out):
    B, T, _ = h.shape
    pos = jnp.arange(T, dtype=jnp.int32)
    q, k, v, gate = split_cols(h @ w_in, B_WIDTHS)
    q = rope(rms_norm(q.reshape(B, T, N_HEADS, HEAD_DIM), q_g), pos)
    k = rope(rms_norm(k.reshape(B, T, N_KV_HEADS, HEAD_DIM), k_g), pos)
    v = v.reshape(B, T, N_KV_HEADS, HEAD_DIM)
    n_blocks = -(-T // MOBA_BLOCK)
    pad = n_blocks * MOBA_BLOCK - T
    kb = jnp.pad(k, ((0, 0), (0, pad), (0, 0), (0, 0))).reshape(B, n_blocks, MOBA_BLOCK, N_KV_HEADS, HEAD_DIM)
    vb = jnp.pad(v, ((0, 0), (0, pad), (0, 0), (0, 0))).reshape(B, n_blocks, MOBA_BLOCK, N_KV_HEADS, HEAD_DIM)
    k_mean = jnp.mean(kb.astype(jnp.float32), axis=2)
    kbt = kb.transpose(0, 3, 1, 2, 4)
    vbt = vb.transpose(0, 3, 1, 2, 4)
    n_sel = min(MOBA_TOPK, n_blocks - 1)
    gather2 = jax.vmap(jax.vmap(lambda s, i: s[i]))
    scale = HEAD_DIM ** -0.5

    def block(start):
        tq = start + jnp.arange(Q_BLOCK, dtype=jnp.int32)
        own = start // MOBA_BLOCK
        qb = lax.dynamic_slice_in_dim(q, start, Q_BLOCK, axis=1).reshape(B, Q_BLOCK, N_KV_HEADS, GROUP, HEAD_DIM)
        k_own = lax.dynamic_index_in_dim(kb, own, axis=1, keepdims=False)
        v_own = lax.dynamic_index_in_dim(vb, own, axis=1, keepdims=False)
        own_pos = own * MOBA_BLOCK + jnp.arange(MOBA_BLOCK, dtype=jnp.int32)
        l_own = jnp.einsum('bqgrd,bsgd->bqgrs', qb, k_own).astype(jnp.float32) * scale
        l_own = jnp.where((own_pos[None, :] <= tq[:, None])[None, :, None, None, :], l_own, NEG)
        if n_sel == 0:
            p = jax.nn.softmax(l_own, axis=-1).astype(v.dtype)
            o = jnp.einsum('bqgrs,bsgd->bqgrd', p, v_own)
        else:
            gscore = jnp.einsum('bqgrd,bngd->bqgn', qb.astype(jnp.float32), k_mean)
            past = jnp.arange(n_blocks, dtype=jnp.int32) < own
            gscore = jnp.where(past, gscore, NEG)
            _, sel = lax.top_k(gscore, n_sel)
            valid = sel < own
            sel_t = jnp.swapaxes(sel, 1, 2)
            k_sel = gather2(kbt, sel_t)
            v_sel = gather2(vbt, sel_t)
            l_sel = jnp.einsum('bqgrd,bgqnsd->bqgrns', qb, k_sel).astype(jnp.float32) * scale
            l_sel = jnp.where(valid[:, :, :, None, :, None], l_sel, NEG)
            n_k = n_sel * MOBA_BLOCK
            logits = jnp.concatenate([l_sel.reshape(B, Q_BLOCK, N_KV_HEADS, GROUP, n_k), l_own], axis=-1)
            p = jax.nn.softmax(logits, axis=-1).astype(v.dtype)
            p_sel = p[..., :n_k].reshape(B, Q_BLOCK, N_KV_HEADS, GROUP, n_sel, MOBA_BLOCK)
            p_own = p[..., n_k:]
            o = (jnp.einsum('bqgrns,bgqnsd->bqgrd', p_sel, v_sel)
                 + jnp.einsum('bqgrs,bsgd->bqgrd', p_own, v_own))
        return o.reshape(B, Q_BLOCK, INNER)

    o = sweep_query_blocks(block, T)
    return (jax.nn.silu(gate) * o) @ w_out

def retention_mixer(h, w_in, gn_g, w_out):
    B, T, _ = h.shape
    pos = jnp.arange(T, dtype=jnp.int32)
    q, k, v, gate = split_cols(h @ w_in, C_WIDTHS)
    q = rope(q.reshape(B, T, RET_HEADS, RET_QK_DIM), pos).astype(jnp.float32)
    k = rope(k.reshape(B, T, RET_HEADS, RET_QK_DIM), pos).astype(jnp.float32) * RET_QK_DIM ** -0.5
    v = v.reshape(B, T, RET_HEADS, RET_V_DIM).astype(jnp.float32)
    log_gamma = jnp.log(1.0 - 2.0 ** (-5.0 - jnp.arange(RET_HEADS, dtype=jnp.float32)))
    i = jnp.arange(RET_CHUNK, dtype=jnp.float32)
    diff = i[:, None] - i[None, :]
    decay_mask = jnp.where(diff >= 0, jnp.exp(jnp.maximum(diff, 0.0)[None] * log_gamma[:, None, None]), 0.0)
    q_decay = jnp.exp((i[:, None] + 1.0) * log_gamma[None, :])
    k_decay = jnp.exp((RET_CHUNK - 1.0 - i[:, None]) * log_gamma[None, :])
    chunk_decay = jnp.exp(RET_CHUNK * log_gamma)
    n_chunks = T // RET_CHUNK

    def to_chunks(a):
        return jnp.swapaxes(a.reshape(B, n_chunks, RET_CHUNK, *a.shape[2:]), 0, 1)

    def step(state, inp):
        qc, kc, vc = inp
        inner = jnp.einsum('bihd,bjhd->bhij', qc, kc) * decay_mask[None]
        o = (jnp.einsum('bhij,bjhv->bihv', inner, vc)
             + jnp.einsum('bihd,bhdv->bihv', qc * q_decay[None, :, :, None], state))
        state = (state * chunk_decay[None, :, None, None]
                 + jnp.einsum('bjhd,bjhv->bhdv', kc * k_decay[None, :, :, None], vc))
        return state, o

    s0 = jnp.zeros((B, RET_HEADS, RET_QK_DIM, RET_V_DIM), jnp.float32)
    _, o = lax.scan(step, s0, (to_chunks(q), to_chunks(k), to_chunks(v)))
    o = jnp.swapaxes(o, 0, 1).reshape(B, T, RET_HEADS, RET_V_DIM)
    mu = jnp.mean(o, axis=-1, keepdims=True)
    var = jnp.mean(jnp.square(o - mu), axis=-1, keepdims=True)
    o = ((o - mu) * lax.rsqrt(var + EPS)).reshape(B, T, RET_INNER) * gn_g.astype(jnp.float32)
    return (jax.nn.silu(gate) * o.astype(h.dtype)) @ w_out

def fox_mixer(h, w_in, f_bias, q_g, k_g, w_out):
    B, T, _ = h.shape
    pos = jnp.arange(T, dtype=jnp.int32)
    q, k, v, gate, f_logit = split_cols(h @ w_in, D_WIDTHS)
    q = rms_norm(q.reshape(B, T, N_HEADS, HEAD_DIM), q_g)
    k = rms_norm(k.reshape(B, T, N_HEADS, HEAD_DIM), k_g)
    v = v.reshape(B, T, N_HEADS, HEAD_DIM)
    log_f = jax.nn.log_sigmoid((f_logit + f_bias).astype(jnp.float32))
    cum_t = jnp.swapaxes(lax.cumsum(log_f, axis=1), 1, 2)
    scale = HEAD_DIM ** -0.5

    def block(start):
        tq = start + jnp.arange(Q_BLOCK, dtype=jnp.int32)
        qb = lax.dynamic_slice_in_dim(q, start, Q_BLOCK, axis=1)
        cq = lax.dynamic_slice_in_dim(cum_t, start, Q_BLOCK, axis=2)
        logits = (jnp.einsum('bqhd,bshd->bhqs', qb, k).astype(jnp.float32) * scale
                  + cq[..., None] - cum_t[:, :, None, :])
        logits = jnp.where((pos[None, :] <= tq[:, None])[None, None], logits, NEG)
        p = jax.nn.softmax(logits, axis=-1).astype(v.dtype)
        o = jnp.einsum('bhqs,bshd->bqhd', p, v)
        return o.reshape(B, Q_BLOCK, INNER)

    o = sweep_query_blocks(block, T)
    return (jax.nn.silu(gate) * o) @ w_out

def first_inputs(seed: int = 0) -> dict:
    key = jax.random.key(seed)
    ks = jax.random.split(key, 21)
    nA, nB, nC, nD = (n_layers_of(m) for m in range(N_MIXERS))

    def dense(k, shape, fan_in):
        return jax.random.normal(k, shape, jnp.float32) * fan_in ** -0.5

    def gain(k, shape):
        return 1.0 + 0.02 * jax.random.normal(k, shape, jnp.float32)

    return {
        'x': jax.random.normal(ks[0], (BATCH, SEQ, D_MODEL), jnp.float32),
        'a_norm': gain(ks[1], (nA, D_MODEL)),
        'a_w_in': dense(ks[2], (nA, D_MODEL, sum(A_WIDTHS)), D_MODEL),
        'a_q_norm': gain(ks[3], (nA, HEAD_DIM)),
        'a_k_norm': gain(ks[4], (nA, HEAD_DIM)),
        'a_w_out': dense(ks[5], (nA, INNER, D_MODEL), INNER),
        'b_norm': gain(ks[6], (nB, D_MODEL)),
        'b_w_in': dense(ks[7], (nB, D_MODEL, sum(B_WIDTHS)), D_MODEL),
        'b_q_norm': gain(ks[8], (nB, HEAD_DIM)),
        'b_k_norm': gain(ks[9], (nB, HEAD_DIM)),
        'b_w_out': dense(ks[10], (nB, INNER, D_MODEL), INNER),
        'c_norm': gain(ks[11], (nC, D_MODEL)),
        'c_w_in': dense(ks[12], (nC, D_MODEL, sum(C_WIDTHS)), D_MODEL),
        'c_gn': gain(ks[13], (nC, RET_INNER)),
        'c_w_out': dense(ks[14], (nC, RET_INNER, D_MODEL), RET_INNER),
        'd_norm': gain(ks[15], (nD, D_MODEL)),
        'd_w_in': dense(ks[16], (nD, D_MODEL, sum(D_WIDTHS)), D_MODEL),
        'd_f_bias': jax.random.uniform(ks[17], (nD, N_HEADS), jnp.float32, minval=1.0, maxval=4.0),
        'd_q_norm': gain(ks[18], (nD, HEAD_DIM)),
        'd_k_norm': gain(ks[19], (nD, HEAD_DIM)),
        'd_w_out': dense(ks[20], (nD, INNER, D_MODEL), INNER),
    }

def first_block(x, a_norm, a_w_in, a_q_norm, a_k_norm, a_w_out,
              b_norm, b_w_in, b_q_norm, b_k_norm, b_w_out,
              c_norm, c_w_in, c_gn, c_w_out,
              d_norm, d_w_in, d_f_bias, d_q_norm, d_k_norm, d_w_out):
    h = x
    for i in range(DEPTH):
        m = i % N_MIXERS
        j = i // N_MIXERS
        if m == 0:
            h = h + dsa_mixer(rms_norm(h, a_norm[j]), a_w_in[j], a_q_norm[j], a_k_norm[j], a_w_out[j])
        elif m == 1:
            h = h + moba_mixer(rms_norm(h, b_norm[j]), b_w_in[j], b_q_norm[j], b_k_norm[j], b_w_out[j])
        elif m == 2:
            h = h + retention_mixer(rms_norm(h, c_norm[j]), c_w_in[j], c_gn[j], c_w_out[j])
        else:
            h = h + fox_mixer(rms_norm(h, d_norm[j]), d_w_in[j], d_f_bias[j], d_q_norm[j], d_k_norm[j], d_w_out[j])
    return h


DEPTH_2 = 1

NSA_HEADS = 8
NSA_KV_HEADS = 2
NSA_GROUP = NSA_HEADS // NSA_KV_HEADS
NSA_DIM = NSA_HEADS * HEAD_DIM
NSA_KV_DIM = NSA_KV_HEADS * HEAD_DIM
CMP_BLOCK = 32
CMP_STRIDE = 16
SEL_BLOCK = 64
SEL_TOPK = 16
WINDOW = 512
WIN_Q_BLOCK = 128
SEL_Q_BLOCK = 64
FORCE_SCORE = 1e9
DN_HEADS = 8
DN_HEAD_DIM = 128
DN_DIM = DN_HEADS * DN_HEAD_DIM
DN_CHUNK = 64
CONV_K = 4
D_FF = -(-(8 * D_MODEL) // (3 * 256)) * 256
NORM_EPS = 1e-6
NEG_INF = -1e30
IN_SPLITS = (NSA_DIM, 6 * NSA_KV_DIM, 3 * NSA_HEADS, 3 * DN_DIM, DN_DIM, DN_HEADS, DN_HEADS, 2 * D_MODEL)
N_IN = sum(IN_SPLITS)


def rms_norm_2(x, w):
    xf = x.astype(jnp.float32)
    y = xf * lax.rsqrt(jnp.mean(xf * xf, axis=-1, keepdims=True) + NORM_EPS)
    return (y * w.astype(jnp.float32)).astype(x.dtype)

def l2norm(x):
    return x * lax.rsqrt(jnp.sum(x * x, axis=-1, keepdims=True) + NORM_EPS)

def rope_tables(seq):
    inv = 1.0 / (ROPE_THETA ** (jnp.arange(0, HEAD_DIM, 2, dtype=jnp.float32) / HEAD_DIM))
    ang = jnp.arange(seq, dtype=jnp.float32)[:, None] * inv[None, :]
    return jnp.cos(ang), jnp.sin(ang)

def apply_rope(x, cos, sin):
    x1, x2 = jnp.split(x.astype(jnp.float32), 2, axis=-1)
    c = cos[None, :, None, :]
    s = sin[None, :, None, :]
    return jnp.concatenate([x1 * c - x2 * s, x2 * c + x1 * s], axis=-1).astype(x.dtype)

def masked_softmax(s, mask):
    return jax.nn.softmax(jnp.where(mask, s.astype(jnp.float32), NEG_INF), axis=-1)

def split_points():
    return [int(v) for v in np.cumsum(IN_SPLITS)[:-1]]

def cmp_to_sel_overlap(n_cmp, n_sel):
    cs = np.arange(n_cmp)[:, None] * CMP_STRIDE
    ss = np.arange(n_sel)[None, :] * SEL_BLOCK
    ov = np.clip(np.minimum(cs + CMP_BLOCK, ss + SEL_BLOCK) - np.maximum(cs, ss), 0, None)
    return jnp.asarray(ov / CMP_BLOCK, dtype=jnp.float32)

def compress_blocks(t, pe, w1, w2):
    b, s, hk, d = t.shape
    n_cmp = (s - CMP_BLOCK) // CMP_STRIDE + 1
    idx = np.arange(n_cmp)[:, None] * CMP_STRIDE + np.arange(CMP_BLOCK)[None, :]
    blk = jnp.swapaxes(t[:, idx], 2, 3) + pe
    blk = blk.reshape(b, n_cmp, hk, CMP_BLOCK * d)
    return jax.nn.gelu(blk @ w1) @ w2

def nsa_mixer(q, kv, gate_logits, cmp_pe_k, cmp_w1_k, cmp_w2_k, cmp_pe_v, cmp_w1_v, cmp_w2_v, cos, sin):
    b, s, _, d = q.shape
    hk, g = NSA_KV_HEADS, NSA_GROUP
    scale = HEAD_DIM ** -0.5
    kv = kv.reshape(b, s, 6, hk, d)
    k_c = apply_rope(kv[:, :, 0], cos, sin)
    v_c = kv[:, :, 1]
    k_s = apply_rope(kv[:, :, 2], cos, sin)
    v_s = kv[:, :, 3]
    k_w = apply_rope(kv[:, :, 4], cos, sin)
    v_w = kv[:, :, 5]
    qg = q.reshape(b, s, hk, g, d)
    t_pos = jnp.arange(s)

    kc = compress_blocks(k_c, cmp_pe_k, cmp_w1_k, cmp_w2_k)
    vc = compress_blocks(v_c, cmp_pe_v, cmp_w1_v, cmp_w2_v)
    n_cmp = kc.shape[1]
    s_cmp = jnp.einsum('bshgd,bchd->bhgsc', qg, kc) * scale
    cmp_end = jnp.arange(n_cmp) * CMP_STRIDE + CMP_BLOCK - 1
    cmp_valid = cmp_end[None, :] <= t_pos[:, None]
    p_cmp = masked_softmax(s_cmp, cmp_valid) * jnp.any(cmp_valid, axis=-1)[:, None].astype(jnp.float32)
    o_cmp = jnp.einsum('bhgsc,bchd->bshgd', p_cmp, vc.astype(jnp.float32))

    n_sel = s // SEL_BLOCK
    imp = jnp.einsum('bhgsc,cj->bhsj', p_cmp, cmp_to_sel_overlap(n_cmp, n_sel))
    blk_t = (t_pos // SEL_BLOCK)[:, None]
    j = jnp.arange(n_sel)[None, :]
    forced = (j == 0) | (j == blk_t) | (j == blk_t - 1)
    imp = jnp.where(forced, FORCE_SCORE, jnp.where(j > blk_t, -FORCE_SCORE, imp))
    n_top = min(SEL_TOPK, n_sel)
    _, sel_idx = lax.top_k(imp, n_top)
    kb = k_s.reshape(b, n_sel, SEL_BLOCK, hk, d).transpose(0, 3, 1, 2, 4)
    vb = v_s.reshape(b, n_sel, SEL_BLOCK, hk, d).transpose(0, 3, 1, 2, 4)
    nqb = s // SEL_Q_BLOCK
    q_blocks = qg.reshape(b, nqb, SEL_Q_BLOCK, hk, g, d).transpose(1, 0, 2, 3, 4, 5)
    idx_blocks = sel_idx.reshape(b, hk, nqb, SEL_Q_BLOCK, n_top).transpose(2, 0, 1, 3, 4)
    pos_blocks = t_pos.reshape(nqb, SEL_Q_BLOCK)
    gather = jax.vmap(jax.vmap(lambda blocks, ix: blocks[ix]))

    def sel_block(args):
        qb, ib, tb = args
        kg = gather(kb, ib)
        vg = gather(vb, ib)
        sc = jnp.einsum('bqhgd,bhqnkd->bhgqnk', qb, kg) * scale
        kpos = ib[..., None] * SEL_BLOCK + jnp.arange(SEL_BLOCK)
        valid = (kpos <= tb[None, None, :, None, None]).reshape(b, hk, 1, SEL_Q_BLOCK, n_top * SEL_BLOCK)
        p = masked_softmax(sc.reshape(b, hk, g, SEL_Q_BLOCK, n_top * SEL_BLOCK), valid)
        p = p.reshape(b, hk, g, SEL_Q_BLOCK, n_top, SEL_BLOCK)
        return jnp.einsum('bhgqnk,bhqnkd->bqhgd', p, vg.astype(jnp.float32))

    o_sel = lax.map(sel_block, (q_blocks, idx_blocks, pos_blocks))
    o_sel = o_sel.transpose(1, 0, 2, 3, 4, 5).reshape(b, s, hk, g, d)

    nb = s // WIN_Q_BLOCK
    n_prev = WINDOW // WIN_Q_BLOCK
    pad = ((0, 0), (WINDOW, 0), (0, 0), (0, 0))
    kp = jnp.pad(k_w, pad).reshape(b, nb + n_prev, WIN_Q_BLOCK, hk, d)
    vp = jnp.pad(v_w, pad).reshape(b, nb + n_prev, WIN_Q_BLOCK, hk, d)
    k_band = jnp.concatenate([kp[:, i:i + nb] for i in range(n_prev + 1)], axis=2)
    v_band = jnp.concatenate([vp[:, i:i + nb] for i in range(n_prev + 1)], axis=2)
    qw = qg.reshape(b, nb, WIN_Q_BLOCK, hk, g, d)
    s_win = jnp.einsum('bnqhgd,bnkhd->bhgnqk', qw, k_band) * scale
    qpos = t_pos.reshape(nb, WIN_Q_BLOCK)
    kpos = (jnp.arange(nb) * WIN_Q_BLOCK - WINDOW)[:, None] + jnp.arange((n_prev + 1) * WIN_Q_BLOCK)[None, :]
    diff = qpos[:, :, None] - kpos[:, None, :]
    win_valid = (diff >= 0) & (diff < WINDOW) & (kpos[:, None, :] >= 0)
    p_win = masked_softmax(s_win, win_valid)
    o_win = jnp.einsum('bhgnqk,bnkhd->bnqhgd', p_win, v_band.astype(jnp.float32)).reshape(b, s, hk, g, d)

    gates = jax.nn.sigmoid(gate_logits.astype(jnp.float32)).reshape(b, s, hk, g, 3)
    o = gates[..., 0:1] * o_cmp + gates[..., 1:2] * o_sel + gates[..., 2:3] * o_win
    return o.reshape(b, s, NSA_DIM)

def gated_deltanet(qkv, z, a, beta_logit, conv_w, a_log, dt_bias, norm_w):
    b, s, c3 = qkv.shape
    h, dk, c = DN_HEADS, DN_HEAD_DIM, DN_CHUNK
    n = s // c
    qkv = lax.conv_general_dilated(qkv, conv_w.astype(qkv.dtype), window_strides=(1,), padding=[(CONV_K - 1, 0)],
                                   dimension_numbers=('NWC', 'WIO', 'NWC'), feature_group_count=c3)
    qkv = jax.nn.silu(qkv.astype(jnp.float32))
    q, k, v = [t.reshape(b, s, h, dk) for t in jnp.split(qkv, 3, axis=-1)]
    q = l2norm(q) * dk ** -0.5
    k = l2norm(k)
    beta = jax.nn.sigmoid(beta_logit.astype(jnp.float32))
    gdec = -jnp.exp(a_log.astype(jnp.float32)) * jax.nn.softplus(a.astype(jnp.float32) + dt_bias.astype(jnp.float32))

    def chunks(t):
        return t.reshape(b, n, c, h, -1).transpose(0, 3, 1, 2, 4)

    q, k, v = chunks(q), chunks(k), chunks(v)
    beta = chunks(beta[..., None])[..., 0]
    gc = jnp.cumsum(chunks(gdec[..., None])[..., 0], axis=-1)
    lower_incl = np.tril(np.ones((c, c), dtype=bool))
    strict = np.tril(np.ones((c, c), dtype=bool), -1)
    decay = jnp.exp(jnp.where(lower_incl, gc[..., :, None] - gc[..., None, :], -jnp.inf))
    kb = k * beta[..., None]
    lmat = jnp.where(strict, jnp.einsum('bhnid,bhnjd->bhnij', kb, k) * decay, 0.0)
    eye = jnp.eye(c, dtype=jnp.float32)
    tinv = lax.linalg.triangular_solve(eye + lmat, jnp.broadcast_to(eye, lmat.shape), left_side=True, lower=True)
    u = tinv @ (v * beta[..., None])
    w = tinv @ (kb * jnp.exp(gc)[..., None])
    attn = jnp.einsum('bhnid,bhnjd->bhnij', q, k) * decay
    g_last = gc[..., -1]
    k_dec = k * jnp.exp(g_last[..., None] - gc)[..., None]
    q_dec = q * jnp.exp(gc)[..., None]

    def step(state, xs):
        q_i, k_i, u_i, w_i, attn_i, gl_i = xs
        v_new = u_i - jnp.einsum('bhck,bhkv->bhcv', w_i, state)
        o_i = jnp.einsum('bhck,bhkv->bhcv', q_i, state) + jnp.einsum('bhij,bhjv->bhiv', attn_i, v_new)
        state = state * jnp.exp(gl_i)[..., None, None] + jnp.einsum('bhck,bhcv->bhkv', k_i, v_new)
        return state, o_i

    xs = tuple(jnp.moveaxis(t, 2, 0) for t in (q_dec, k_dec, u, w, attn, g_last))
    state0 = jnp.zeros((b, h, dk, dk), jnp.float32)
    _, o = lax.scan(step, state0, xs)
    o = o.transpose(1, 0, 3, 2, 4).reshape(b, s, h, dk)
    o = rms_norm_2(o, norm_w) * jax.nn.silu(z.astype(jnp.float32).reshape(b, s, h, dk))
    return o.reshape(b, s, DN_DIM)

def second_inputs(seed: int = 0) -> dict:
    key = jax.random.key(seed)
    ks = jax.random.split(key, 24)

    def nrm(k, shape, fan_in):
        return jax.random.normal(k, shape, jnp.float32) * fan_in ** -0.5

    def gain(k, shape):
        return 1.0 + 0.02 * jax.random.normal(k, shape, jnp.float32)

    dt = jnp.exp(jax.random.uniform(ks[5], (DEPTH_2, DN_HEADS), jnp.float32, math.log(1e-3), math.log(1e-1)))
    return {
        'x': jax.random.normal(ks[0], (BATCH, SEQ, D_MODEL), jnp.float32),
        'norm1_w': gain(ks[1], (DEPTH_2, D_MODEL)),
        'w_in': nrm(ks[2], (DEPTH_2, D_MODEL, N_IN), D_MODEL),
        'conv_w': nrm(ks[3], (DEPTH_2, CONV_K, 1, 3 * DN_DIM), CONV_K),
        'a_log': jnp.log(jax.random.uniform(ks[4], (DEPTH_2, DN_HEADS), jnp.float32, 1.0, 16.0)),
        'dt_bias': dt + jnp.log(-jnp.expm1(-dt)),
        'dn_norm_w': gain(ks[6], (DEPTH_2, DN_HEAD_DIM)),
        'cmp_pe_k': 0.02 * jax.random.normal(ks[7], (DEPTH_2, CMP_BLOCK, HEAD_DIM), jnp.float32),
        'cmp_w1_k': nrm(ks[8], (DEPTH_2, CMP_BLOCK * HEAD_DIM, HEAD_DIM), CMP_BLOCK * HEAD_DIM),
        'cmp_w2_k': nrm(ks[9], (DEPTH_2, HEAD_DIM, HEAD_DIM), HEAD_DIM),
        'cmp_pe_v': 0.02 * jax.random.normal(ks[10], (DEPTH_2, CMP_BLOCK, HEAD_DIM), jnp.float32),
        'cmp_w1_v': nrm(ks[11], (DEPTH_2, CMP_BLOCK * HEAD_DIM, HEAD_DIM), CMP_BLOCK * HEAD_DIM),
        'cmp_w2_v': nrm(ks[12], (DEPTH_2, HEAD_DIM, HEAD_DIM), HEAD_DIM),
        'w_up_nsa': nrm(ks[13], (DEPTH_2, NSA_DIM, D_MODEL), NSA_DIM),
        'w_up_dn': nrm(ks[14], (DEPTH_2, DN_DIM, D_MODEL), DN_DIM),
        'w_o': nrm(ks[15], (DEPTH_2, D_MODEL, D_MODEL), D_MODEL),
        'norm2_w': gain(ks[16], (DEPTH_2, D_MODEL)),
        'w_ffn_gate': nrm(ks[17], (DEPTH_2, D_MODEL, D_FF), D_MODEL),
        'w_ffn_up': nrm(ks[18], (DEPTH_2, D_MODEL, D_FF), D_MODEL),
        'w_ffn_down': nrm(ks[19], (DEPTH_2, D_FF, D_MODEL), D_FF),
        'norm_f_w': gain(ks[20], (D_MODEL,)),
    }

def second_block(x, norm1_w, w_in, conv_w, a_log, dt_bias, dn_norm_w, cmp_pe_k, cmp_w1_k, cmp_w2_k,
              cmp_pe_v, cmp_w1_v, cmp_w2_v, w_up_nsa, w_up_dn, w_o, norm2_w, w_ffn_gate, w_ffn_up,
              w_ffn_down, norm_f_w):
    b, s, _ = x.shape
    cos, sin = rope_tables(s)
    for l in range(DEPTH_2):
        h = rms_norm_2(x, norm1_w[l])
        proj = h @ w_in[l]
        nsa_q, nsa_kv, nsa_g, dn_qkv, dn_z, dn_a, dn_b, merge_g = jnp.split(proj, split_points(), axis=-1)
        q = apply_rope(nsa_q.reshape(b, s, NSA_HEADS, HEAD_DIM), cos, sin)
        o_nsa = nsa_mixer(q, nsa_kv, nsa_g, cmp_pe_k[l], cmp_w1_k[l], cmp_w2_k[l],
                          cmp_pe_v[l], cmp_w1_v[l], cmp_w2_v[l], cos, sin).astype(x.dtype)
        o_dn = gated_deltanet(dn_qkv, dn_z, dn_a, dn_b, conv_w[l], a_log[l], dt_bias[l], dn_norm_w[l]).astype(x.dtype)
        g_nsa, g_dn = jnp.split(jax.nn.sigmoid(merge_g), 2, axis=-1)
        mixed = g_nsa * (o_nsa @ w_up_nsa[l]) + g_dn * (o_dn @ w_up_dn[l])
        x = x + mixed @ w_o[l]
        h2 = rms_norm_2(x, norm2_w[l])
        x = x + (jax.nn.silu(h2 @ w_ffn_gate[l]) * (h2 @ w_ffn_up[l])) @ w_ffn_down[l]
    return rms_norm_2(x, norm_f_w)


def setup_inputs(seed=0):
    out = dict(first_inputs(seed))
    for name, value in second_inputs(seed + 1).items():
        if name != "x":
            out[name + "_2"] = value
    return out


def reference(
    x, a_norm, a_w_in, a_q_norm, a_k_norm, a_w_out, b_norm, b_w_in, b_q_norm, b_k_norm, b_w_out,
    c_norm, c_w_in, c_gn, c_w_out, d_norm, d_w_in, d_f_bias, d_q_norm, d_k_norm, d_w_out,
    norm1_w_2, w_in_2, conv_w_2, a_log_2, dt_bias_2, dn_norm_w_2, cmp_pe_k_2, cmp_w1_k_2,
    cmp_w2_k_2, cmp_pe_v_2, cmp_w1_v_2, cmp_w2_v_2, w_up_nsa_2, w_up_dn_2, w_o_2, norm2_w_2,
    w_ffn_gate_2, w_ffn_up_2, w_ffn_down_2, norm_f_w_2,
):
    x = first_block(
        x, a_norm, a_w_in, a_q_norm, a_k_norm, a_w_out, b_norm, b_w_in, b_q_norm, b_k_norm,
        b_w_out, c_norm, c_w_in, c_gn, c_w_out, d_norm, d_w_in, d_f_bias, d_q_norm, d_k_norm,
        d_w_out,
    )
    return second_block(
        x, norm1_w_2, w_in_2, conv_w_2, a_log_2, dt_bias_2, dn_norm_w_2, cmp_pe_k_2, cmp_w1_k_2,
        cmp_w2_k_2, cmp_pe_v_2, cmp_w1_v_2, cmp_w2_v_2, w_up_nsa_2, w_up_dn_2, w_o_2, norm2_w_2,
        w_ffn_gate_2, w_ffn_up_2, w_ffn_down_2, norm_f_w_2,
    )


_drawn_inputs = setup_inputs


def setup_inputs(seed=0):
    import zlib

    import numpy as np

    out = dict(_drawn_inputs(seed))
    spreads = {}
    factors = {'a_norm': 2.769,
     'a_q_norm': 8.0,
     'a_k_norm': 8.0,
     'b_norm': 8.0,
     'b_q_norm': 8.0,
     'b_k_norm': 8.0,
     'norm1_w_2': 17.15,
     'dn_norm_w_2': 60.224,
     'cmp_pe_k_2': 200.0,
     'cmp_pe_v_2': 200.0,
     'norm2_w_2': 31.648,
     'norm_f_w_2': 21.952,
     'cmp_w1_k_2': 14.158,
     'cmp_w2_k_2': 14.779,
     'cmp_w1_v_2': 4.279,
     'cmp_w2_v_2': 3.425}
    for name, (base, spread) in spreads.items():
        noise = np.random.default_rng([zlib.crc32(name.encode()), seed]).standard_normal(out[name].shape)
        drawn = base * np.exp(spread * noise) if base else spread * noise
        out[name] = __import__('jax').numpy.asarray(drawn.astype(out[name].dtype))
    for name, factor in factors.items():
        out[name] = (out[name] * factor).astype(out[name].dtype)
    return out
```

```python
from contextlib import contextmanager, ExitStack

import numpy as np
import concourse.bass as bass
from concourse import mybir

F32 = mybir.dt.float32
F32R = mybir.dt.float32r
ALU = mybir.AluOpType
ACT = mybir.ActivationFunctionType
AX = mybir.AxisListType

P = 128
T = 256
TB = T // P
D = 2048
KT_D = D // P
CH = 512
QK = 4
NH, NKV, HD = 16, 4, 128
GRP = NH // NKV
IH, ID = 16, 64
KEEP = min(256, T // 4)
EPS = 1e-6
NEG = -1e30
REMOVED = -3e38
CREDIT = 4096

N2, NG2 = 8, 4
NC2 = (T - 32) // 16 + 1
DH, DC = 8, 64
F_FF = 5632


ARENA = 15400

CONSTS = {"identity": P, "causal": 3 * P, "cos": TB * HD, "sin": TB * HD, "cos_index": TB * ID, "sin_index": TB * ID}
CONST_AT, CONST_COLS = {}, 0
for _name, _n in CONSTS.items():
    CONST_AT[_name] = (CONST_COLS, CONST_COLS + _n)
    CONST_COLS += _n


def shape_constants():
    out = {"identity": np.eye(P)}
    q, s = np.arange(P)[:, None], np.arange(T)[None, :]
    out["causal"] = np.concatenate([np.where(s[:, :P] <= q, 0, NEG), np.where(s <= q + P, 0, NEG)], 1)
    for name, w in (("", HD), ("_index", ID)):
        inv = np.float32(10000.0) ** (-np.arange(0, w, 2, dtype=np.float32) / np.float32(w))
        ang = np.arange(T, dtype=np.float32)[:, None] * inv[None, :]
        blocks = lambda a: a.reshape(TB, P, w).transpose(1, 0, 2).reshape(P, TB * w)
        out["cos" + name] = blocks(np.concatenate([np.cos(ang), np.cos(ang)], 1))
        out["sin" + name] = blocks(np.concatenate([-np.sin(ang), np.sin(ang)], 1))
    return np.concatenate([out[n].astype(np.float32) for n in CONSTS], 1)


def more_constants():
    j, i = np.arange(P)[:, None], np.arange(P)[None, :]
    same = (j // DC == i // DC)
    levels = []
    for level in range(LEVELS):
        b = 1 << level
        levels.append((j // (2 * b) == i // (2 * b)) & (j % (2 * b) >= b) & (i % (2 * b) < b))
    dn = [np.ones((P, P)), same & (j <= i), same, np.where(same & (i <= j), 0, NEG)] + levels
    q, c = np.arange(T), np.arange(PADC)
    seen = (c[None, :] < NC2) & (16 * c[None, :] + 31 <= q[:, None])
    bias = np.tile(np.where(seen, 0, NEG), (1, HQ)).reshape(TB, P, HQ * PADC).transpose(1, 0, 2).reshape(P, -1)
    head_of = np.arange(P)[:, None] // PADC == np.arange(HQ)[None, :]
    some = seen.any(1).reshape(TB, P).T
    return (np.concatenate(dn, 1).astype(np.float32), np.concatenate([bias, head_of, some], 1).astype(np.float32))


class Names:
    pass


class Line:

    def __init__(self, prog, name, by=1):
        self.prog, self.name, self.by = prog, name, by
        self.sem = prog.ctx.enter_context(prog.nc.semaphore(name))
        self.total = self.local = 0
        prog.lines.append(self)
        prog.nc.sync.sem_inc(self.sem, CREDIT)

    def tick(self, ins):
        ins.then_inc(self.sem, self.by)
        self.local += 1
        return self.now()

    def now(self, back=0):
        return Point(self, self.local - back, self.total, self.prog.loop)


class Point:
    def __init__(self, line, local, start, loop):
        self.line, self.local, self.start, self.loop = line, local, start, loop

    def value(self):
        line, prog = self.line, self.line.prog
        if self.loop is None:
            return (self.start + self.local) * line.by + CREDIT
        per = self.loop.counts.get(line.name, 0)
        if prog.loop is self.loop:
            v = (self.start + self.local) * line.by + CREDIT
            return v if per == 0 else self.loop.reg * (per * line.by) + v
        return (self.start + (self.loop.turns - 1) * per + self.local) * line.by + CREDIT


class Loop:
    def __init__(self, reg, turns, counts):
        self.reg, self.turns, self.counts = reg, turns, counts


class Prog:

    def __init__(self, nc, counts, ctx):
        self.nc, self.counts, self.ctx = nc, counts, ctx
        self.lines, self.loop, self.seen = [], None, {}
        self.pe, self.act, self.dve = Eng(self, nc.tensor, "pe"), Eng(self, nc.scalar, "act"), Eng(self, nc.vector, "dve")
        self.pool = Eng(self, nc.gpsimd, "pool")

    @contextmanager
    def turns(self, name, n):
        for line in self.lines:
            line.total, line.local = line.total + line.local, 0
        counts = self.counts.get(name, {})
        with self.nc.Fori(0, n) as i:
            self.loop = Loop(i, n, counts)
            yield i
            self.loop = None
        self.seen[name] = {line.name: line.local for line in self.lines}
        for line in self.lines:
            line.total, line.local = line.total + n * line.local, 0


class Eng:

    def __init__(self, prog, raw, name):
        self.prog, self.raw, self.name = prog, raw, name
        self.line = Line(prog, name + "_done")
        self.held = 0

    def wait(self, *points):
        for p in points:
            if p is not None:
                self.raw.wait_ge(p.line.sem, p.value())

    def after(self, *engines):
        self.wait(*(e.line.now() for e in engines))

    def sync(self):
        self.wait(self.line.now())

    def constant_wait(self):
        if self.prog.loop:
            self.held += 1
            assert self.held < CREDIT
            self.raw.wait_ge(self.line.sem, self.held)

    def did(self, ins):
        return self.line.tick(ins)


def memory(nc, prog):
    core = Names()
    core.nc, core.prog = nc, prog
    sb = lambda name, shape, dt=F32: prog.ctx.enter_context(nc.sbuf_tensor(name, shape, dt))
    core.sb = sb
    core.X = sb("X", [P, TB, D])
    core.XH = sb("XH", [P, KT_D, T], F32R)
    core.XL = sb("XL", [P, KT_D, T], F32R)
    core.W = [sb(f"W{i}", [P, QK, CH]) for i in range(4)]
    core.WH = [sb(f"WH{i}", [P, QK, CH], F32R) for i in range(2)]
    core.WL = [sb(f"WL{i}", [P, QK, CH], F32R) for i in range(2)]
    bank = lambda name: prog.ctx.enter_context(nc.psum_tensor(name, [P, CH], F32))
    core.ACC = [bank(f"ACC{t}") for t in range(TB)]
    core.TP = [bank(f"TP{i}") for i in range(2)]
    core.SC = [bank(f"SC{i}") for i in range(2)]
    core.PV = [bank(f"PV{i}") for i in range(2)]
    line = lambda name, by=1: Line(prog, name, by)
    core.landed = [line(f"weights_landed{i}", 16) for i in range(4)]
    core.hi_done, core.lo_done = line("weights_rounded"), line("weights_rest")
    core.quad_done, core.acc0_done = line("quad_multiplied"), line("block0_accumulated")
    core.acc_taken, core.tp_taken = line("accumulators_taken"), line("transposes_taken")
    core.small = line("constants_landed", 16)
    core.n_quad = 0
    core.consts = sb("consts", [P, CONST_COLS])
    c = lambda n: core.consts[:, CONST_AT[n][0]:CONST_AT[n][1]]
    core.ident, core.causal = c("identity"), c("causal")
    by_block = lambda n: c(n).rearrange("p (t w) -> p t w", t=TB)
    core.cos, core.sin, core.cos_i, core.sin_i = by_block("cos"), by_block("sin"), by_block("cos_index"), by_block("sin_index")
    core.gains = sb("gains", [P, 4, KT_D])
    core.ss, core.rs = sb("sums_of_squares", [P, 64]), sb("reciprocal_roots", [P, 64])
    core.TMP = sb("TMP", [P, 2048])
    core.small_tables = sb("small_tables", [P, 8 * TB * DH])
    core.GT, core.AB = sb("GT", [P, TB, 3 * N2]), sb("AB", [P, TB, 2 * DH])
    core.QKG = sb("qk_gains", [P, (NH // GRP + 1) * HD])
    core.mixers = ExitStack()
    own = lambda name, shape: core.mixers.enter_context(nc.sbuf_tensor(name, shape, F32))
    core.arena, core.fixed = own("arena", [P, ARENA]), own("attention_memory", [P, 4760])
    core.at = core.fixed_at = 0
    core.att = attention_memory(core)
    return core


def cut(core, mem, at, shape):
    n = 1
    for d in shape:
        n *= d
    assert at + n <= mem.shape[1], (at + n, mem.shape)
    flat = mem[:, at:at + n]
    if len(shape) == 1:
        return flat, at + n
    names = "abc"[:len(shape)]
    return flat.rearrange(f"p ({' '.join(names)}) -> p {' '.join(names)}", **dict(zip(names, shape))), at + n


def arena(core, name, shape):
    view, core.at = cut(core, core.arena, core.at, shape)
    return view


def places(core, regions):
    left = [list(r) for r in regions]

    def own(cols):
        for r in left:
            if r[1] + cols <= r[2]:
                r[1] += cols
                return r[0][:, r[1] - cols:r[1]]
        raise ValueError("no place left")
    return own


def fixed(core, name, shape):
    view, core.fixed_at = cut(core, core.fixed, core.fixed_at, shape)
    return view




def quad(core, rows, width, k0, first, last, x_ready=None, xs=None):
    nc, pe, act, dve, slot, half = core.nc, core.prog.pe, core.prog.act, core.prog.dve, core.n_quad % 4, core.n_quad % 2
    W, WH, WL = core.W[slot], core.WH[half], core.WL[half]
    core.n_quad += 1
    nc.sync.wait_ge(core.lo_done.sem, core.lo_done.now(back=3).value())
    here = core.landed[slot].tick(nc.sync.dma_start(W[:, :, 0:width], rows.rearrange("(k p) n -> p k n", p=P)))
    act.wait(here, core.quad_done.now(back=1))
    hi = core.hi_done.tick(nc.scalar.activation(WH[:, :, 0:width], W[:, :, 0:width], ACT.Copy))
    dve.wait(hi)
    lo = core.lo_done.tick(nc.vector.tensor_tensor(WL[:, :, 0:width], W[:, :, 0:width],
                                                   WH[:, :, 0:width].bitcast(F32), ALU.subtract))
    pe.wait(lo, x_ready)
    for t in range(TB):
        if first:
            pe.wait(core.acc_taken.now(back=1) if t == 0 else core.acc_taken.now())
        out = core.ACC[t][:, 0:width]
        for k in range(QK):
            hi_x, lo_x = (x[:, k0 + k, t * P:(t + 1) * P] for x in (xs or (core.XH, core.XL)))
            nc.tensor.matmul(out, hi_x, WH[:, k, 0:width], start=first and k == 0, stop=False)
            nc.tensor.matmul(out, hi_x, WL[:, k, 0:width], start=False, stop=False)
            mm = nc.tensor.matmul(out, lo_x, WH[:, k, 0:width], start=False, stop=last and k == QK - 1)
        if last and t == 0:
            core.acc0_done.tick(mm)
    core.quad_done.tick(mm)


def project(core, w, col, width=CH, n_quads=4, take=None, between=None, x_ready=None, row0=0, k0=0, xs=None):
    for q in range(n_quads):
        r = row0 + q * QK * P
        quad(core, w[r:r + QK * P, bass.ds(col, width)], width, k0 + q * QK, q == 0, q == n_quads - 1,
                  x_ready[q] if x_ready else None, xs)
        if between:
            between(q)
    out = None
    for t in range(TB):
        eng, make = take() if callable(take) else take
        eng.wait(core.acc0_done.now() if t == 0 else core.quad_done.now())
        eng.constant_wait()
        out = core.acc_taken.tick(make(t, core.ACC[t][:, 0:width]))
    return out


def copy_to(core, dst):
    return core.prog.act, lambda t, acc: core.nc.scalar.activation(dst(t), acc, ACT.Copy)




def rstd(core, ss, out, width, ready, eps=EPS):
    act, dve, nc = core.prog.act, core.prog.dve, core.nc
    dve.wait(ready)
    dve.did(nc.vector.tensor_scalar(out, ss, 1.0 / width, eps, ALU.mult, ALU.add))
    act.wait(dve.line.now())
    act.did(nc.scalar.activation(out, out, ACT.Sqrt))
    dve.wait(act.line.now())
    return dve.did(nc.vector.reciprocal(out, out))


def turn(core, src, gain=None, ready=None, k_tiles=KT_D, k0=0, xs=None):
    nc, pe, act, dve = core.nc, core.prog.pe, core.prog.act, core.prog.dve
    XH, XL = xs or (core.XH, core.XL)
    act.wait(core.quad_done.now())
    pe.wait(core.tp_taken.now(), ready)
    points = []
    for j in range(k_tiles // 2):
        tp = core.TP[j % 2]
        pe.wait(core.tp_taken.now(back=1))
        for k in range(2):
            for t in range(TB):
                c = (2 * j + k) * P
                ins = nc.tensor.transpose(tp[:, (2 * k + t) * P:(2 * k + t + 1) * P], src[:, t, c:c + P], core.ident)
        turned = pe.did(ins)
        act.wait(turned)
        parts = 1 if gain is None else 2
        piece = []
        for s in range(parts):
            n = 2 // parts
            k = k0 + 2 * j + s * n
            piece.append((tp[:, s * T:(s + n) * T], XH[:, k:k + n, :].rearrange("p k t -> p (k t)"),
                          XL[:, k:k + n, :].rearrange("p k t -> p (k t)"),
                          1.0 if gain is None else gain[:, 2 * j + s:2 * j + s + 1]))
        for ps, hi, lo, g in piece:
            rounded = act.did(nc.scalar.activation(hi, ps, ACT.Copy, scale=g))
        dve.wait(rounded)
        for s, (ps, hi, lo, g) in enumerate(piece):
            ins = nc.vector.scalar_tensor_tensor(lo, ps, g, hi.bitcast(F32), ALU.mult, ALU.subtract)
            done = core.tp_taken.tick(ins) if s == parts - 1 else dve.did(ins)
        points.append(done)
    return [points[min(len(points) - 1, 2 * q + 1)] for q in range((k_tiles + 3) // 4)]


def token_norm(core, gain, scratch, ready):
    nc, act, dve = core.nc, core.prog.act, core.prog.dve
    act.wait(ready)
    for t in range(TB):
        p = act.did(nc.scalar.activation(scratch[:, t, :], core.X[:, t, :], ACT.Square, accum_out=core.ss[:, t:t + 1]))
    rstd(core, core.ss[:, 0:TB], core.rs[:, 0:TB], D, p)
    for t in range(TB):
        dve.sync()
        p = dve.did(nc.vector.tensor_scalar(scratch[:, t, :], core.X[:, t, :], core.rs[:, t:t + 1], None, ALU.mult))
    return turn(core, scratch, gain, p)


def rope(core, x, out, cos, sin, heads, width, tmp, ready, eng=None):
    nc, dve = core.nc, core.prog.dve
    h = width // 2
    dve.wait(ready)
    for t in range(TB):
        tm = tmp[:, t * heads * width:(t + 1) * heads * width].rearrange("p (h w) -> p h w", h=heads)
        s1 = sin[:, t:t + 1, 0:h].to_broadcast([P, heads, h])
        s2 = sin[:, t:t + 1, h:width].to_broadcast([P, heads, h])
        c = cos[:, t:t + 1, :].to_broadcast([P, heads, width])
        dve.did(nc.vector.tensor_tensor(tm[:, :, 0:h], x[:, t, :, h:width], s1, ALU.mult))
        dve.did(nc.vector.tensor_tensor(tm[:, :, h:width], x[:, t, :, 0:h], s2, ALU.mult))
        dve.sync()
        dve.did(nc.vector.tensor_tensor(out[:, t], x[:, t], c, ALU.mult))
        dve.sync()
        p = dve.did(nc.vector.tensor_tensor(out[:, t], out[:, t], tm, ALU.add))
    return p


def attention_memory(core):
    F = lambda n, shape: fixed(core, n, shape)
    line = lambda n: Line(core.prog, n)
    att = Names()
    att.QR, att.QT = F("QR", [TB, GRP * HD]), F("QT", [GRP, T])
    att.LG = [F(f"LG{j}", [3 * P]) for j in range(2)]
    att.PR = [F(f"PR{j}", [3 * P]) for j in range(2)]
    att.PT = [F(f"PT{j}", [3 * P]) for j in range(2)]
    att.NM, att.SUM = F("NM", [GRP, TB]), F("SUM", [GRP, TB])
    att.qr_taken, att.qt_taken, att.sc_taken = line("qr_turned"), line("qt_multiplied"), line("scores_taken")
    att.pr_taken, att.pt_taken, att.pv_taken = line("probs_turned"), line("probs_multiplied"), line("outputs_taken")
    return att


def group_queries(core, q_src):
    nc, att, pe, act, pool = core.nc, core.att, core.prog.pe, core.prog.act, core.prog.pool
    pool.wait(att.qr_taken.now())
    here = pool.did(nc.gpsimd.tensor_copy(att.QR, q_src))
    pe.wait(here)
    for h2 in range(2):
        pe.wait(core.tp_taken.now(back=1))
        for h in range(2):
            for t in range(TB):
                c = (2 * h2 + h) * HD
                ins = nc.tensor.transpose(core.TP[h2][:, (2 * h + t) * P:(2 * h + t + 1) * P], att.QR[:, t, c:c + HD], core.ident)
        act.wait((att.qr_taken.tick(ins) if h2 else pe.did(ins)), att.qt_taken.now())
        done = core.tp_taken.tick(nc.scalar.activation(att.QT[:, 2 * h2:2 * h2 + 2, :].rearrange("p h t -> p (h t)"),
                                                       core.TP[h2][:, :], ACT.Copy))
    return done, here


def head_softmax(core, h, q_ready, kt, mask):
    nc, att, pe, act, dve = core.nc, core.att, core.prog.pe, core.prog.act, core.prog.dve
    LG, PR, sc = att.LG[h % 2], att.PR[h % 2], core.SC[h % 2]
    pe.wait(q_ready, att.sc_taken.now(back=1))
    nc.tensor.matmul(sc[:, 0:P], att.QT[:, h, 0:P], kt(0, P), start=True, stop=True)
    ins = nc.tensor.matmul(sc[:, P:3 * P], att.QT[:, h, P:T], kt(0, T), start=True, stop=True)
    scored = att.qt_taken.tick(ins) if h == GRP - 1 else pe.did(ins)
    dve.wait(scored, att.pr_taken.now(back=1))
    masked = att.sc_taken.tick(nc.vector.scalar_tensor_tensor(LG, sc[:, 0:3 * P], HD ** -0.5, mask, ALU.mult, ALU.add))
    dve.wait(masked, att.pv_taken.now(back=1))
    dve.did(nc.vector.tensor_reduce(att.NM[:, h, 0:1], LG[:, 0:P], AX.X, ALU.max, negate=True))
    top = dve.did(nc.vector.tensor_reduce(att.NM[:, h, 1:2], LG[:, P:3 * P], AX.X, ALU.max, negate=True))
    act.wait(top)
    act.did(nc.scalar.activation(PR[:, 0:P], LG[:, 0:P], ACT.Exp, bias=att.NM[:, h, 0:1], accum_out=att.SUM[:, h, 0:1]))
    return act.did(nc.scalar.activation(PR[:, P:3 * P], LG[:, P:3 * P], ACT.Exp, bias=att.NM[:, h, 1:2],
                                        accum_out=att.SUM[:, h, 1:2]))


def head_turn(core, h, exp_ready):
    nc, att, pe, act, dve = core.nc, core.att, core.prog.pe, core.prog.act, core.prog.dve
    tp = core.TP[h % 2]
    pe.wait(exp_ready, core.tp_taken.now(back=1))
    for b in range(3):
        ins = nc.tensor.transpose(tp[:, b * P:(b + 1) * P], att.PR[h % 2][:, b * P:(b + 1) * P], core.ident)
    act.wait(att.pr_taken.tick(ins), att.pt_taken.now(back=1))
    pt_ready = core.tp_taken.tick(nc.scalar.activation(att.PT[h % 2], tp[:, 0:3 * P], ACT.Copy))
    dve.wait(exp_ready)
    return pt_ready, dve.did(nc.vector.reciprocal(att.SUM[:, h, :], att.SUM[:, h, :]))


def head_outputs(core, h, pt_ready, sum_ready, src_read, vt, store):
    nc, att, pe = core.nc, core.att, core.prog.pe
    PT, pv = att.PT[h % 2], core.PV[h % 2]
    pe.wait(pt_ready, att.pv_taken.now(back=1))
    nc.tensor.matmul(pv[:, 0:HD], PT[:, 0:P], vt(0), start=True, stop=True)
    nc.tensor.matmul(pv[:, HD:2 * HD], PT[:, P:2 * P], vt(0), start=True, stop=False)
    ins = att.pt_taken.tick(nc.tensor.matmul(pv[:, HD:2 * HD], PT[:, 2 * P:3 * P], vt(1), start=False, stop=True))
    return store(h, pv, ins, sum_ready, src_read)


def attend(core, q_src, kt, vt, mask, store):
    q_ready, src_read = group_queries(core, q_src)
    exp_ready = head_softmax(core, 0, q_ready, kt, mask)
    held = {"exp": exp_ready}

    def between(q):
        turned = head_turn(core, q, held["exp"])
        if q + 1 < GRP:
            held["exp"] = head_softmax(core, q + 1, q_ready, kt, mask)
        if q >= 1:
            head_outputs(core, q - 1, *held["turned"], src_read, vt, store)
        if q == GRP - 1:
            head_outputs(core, q, *turned, src_read, vt, store)
        held["turned"] = turned
    return between


def attention_layer(core, name, w_in, w_out, gain, qk_gain, cols, index=None):
    nc, prog, att = core.nc, core.prog, core.att
    pe, act, dve, pool = prog.pe, prog.act, prog.dve, prog.pool
    core.at = 0
    Q = arena(core, "Q", [TB, (NH + NKV) * HD])
    V = arena(core, "V", [TB, NKV * HD])
    G = arena(core, "G", [TB, D])
    x_ready = token_norm(core, gain, G, core.x_ready)
    mask, mask_ready = core.causal, None
    if index:
        mask, mask_ready = index(core, w_in, x_ready, G)
    C, last = att.QR, [None]

    def to_chunk(t, acc):
        return nc.scalar.activation(C[:, t, :], acc, ACT.Copy)

    def finish(chunk):
        rs = core.rs[:, 0:TB * GRP].unsqueeze(2).to_broadcast([P, TB * GRP, HD])
        flat = C.rearrange("p t (h w) -> p (t h) w", w=HD)
        mine = Q[:, :, bass.ds(chunk * CH, CH)]
        gain = qk_gain[:, bass.ds(chunk * HD, HD)].unsqueeze(1).to_broadcast([P, TB * GRP, HD])
        heads = lambda ap: ap.rearrange("p t (h w) -> p t h w", w=HD)

        def between(q):
            if q == 0:
                act.after(dve)
                act.wait(core.acc_taken.now())
                sq = act.did(nc.scalar.activation(core.TMP[:, 0:TB * CH].rearrange("p (t w) -> p t w", t=TB), C, ACT.Square))
                dve.wait(sq)
                s = dve.did(nc.vector.tensor_reduce(core.ss[:, 0:TB * GRP], core.TMP[:, 0:TB * CH].rearrange("p (h w) -> p h w", w=HD), AX.X, ALU.add))
                rstd(core, core.ss[:, 0:TB * GRP], core.rs[:, 0:TB * GRP], HD, s)
            if q == 1:
                dve.sync()
                dve.did(nc.vector.tensor_tensor(flat, flat, rs, ALU.mult))
                dve.sync()
                dve.did(nc.vector.tensor_tensor(flat, flat, gain, ALU.mult))
            if q == 2:
                last[0] = rope(core, heads(C), heads(mine), core.cos, core.sin, GRP, HD, core.TMP, dve.line.now())
        return between

    def take_chunk():
        act.after(dve)
        return act, to_chunk
    project(core, w_in, cols[0], take=(act, to_chunk), x_ready=x_ready)
    with prog.turns(name + "_qk", NH // GRP) as i:
        project(core, w_in, cols[0] + CH + i * CH, take=take_chunk, between=finish(i))
    v_ready = project(core, w_in, cols[1], take=copy_to(core, lambda t: V[:, t, :]), between=finish(NH // GRP))
    roped = last[0]
    KT = arena(core, "KT", [NKV, T])
    for j in range(2):
        pe.wait(roped, core.tp_taken.now(back=1))
        for h in range(2):
            for t in range(TB):
                c = NH * HD + (2 * j + h) * HD
                ins = nc.tensor.transpose(core.TP[j][:, (2 * h + t) * P:(2 * h + t + 1) * P], Q[:, t, c:c + HD], core.ident)
        act.wait(pe.did(ins))
        kt_ready = core.tp_taken.tick(nc.scalar.activation(KT[:, 2 * j:2 * j + 2, :].rearrange("p h t -> p (h t)"), core.TP[j][:, :], ACT.Copy))
    pe.wait(kt_ready, v_ready)
    pool.wait(roped)
    dve.wait(mask_ready)
    with prog.turns(name + "_attend", NKV) as i:
        kt = lambda t0, n: KT[:, bass.ds(i, 1), t0:t0 + n].rearrange("p a n -> p (a n)")
        vt = lambda t: V[:, t, bass.ds(i * HD, HD)]
        out = lambda h, t: Q[:, t, bass.ds(i * CH + h * HD, HD)]

        def store(h, pv, multiplied, sum_ready, src_read):
            act.wait(multiplied, sum_ready, src_read)
            act.constant_wait()
            act.did(nc.scalar.activation(out(h, 0), pv[:, 0:HD], ACT.Copy, scale=att.SUM[:, h, 0:1]))
            return att.pv_taken.tick(nc.scalar.activation(out(h, 1), pv[:, HD:2 * HD], ACT.Copy, scale=att.SUM[:, h, 1:2]))
        between = attend(core, Q[:, :, bass.ds(i * CH, CH)], kt, vt, mask, store)
        gated = project(core, w_in, cols[2] + i * CH, take=copy_to(core, lambda t: G[:, t, bass.ds(i * CH, CH)]), between=between)
    points = gate(core, G, Q, ACT.Silu, gated, att.pv_taken.now())
    x_ready = turn(core, Q, ready=points)
    return add_projection(core, name + "_out", w_out, x_ready)


def gate(core, G, O, func, gated, ready, width=D):
    nc, act, dve = core.nc, core.prog.act, core.prog.dve
    act.wait(gated, ready)
    for c in range(width // CH):
        cs = slice(c * CH, (c + 1) * CH)
        for t in range(TB):
            p = act.did(nc.scalar.activation(G[:, t, cs], G[:, t, cs], func))
            dve.wait(p)
            p = dve.did(nc.vector.tensor_tensor(O[:, t, cs], O[:, t, cs], G[:, t, cs], ALU.mult))
    return p


def add_projection(core, name, w, x_ready, n_quads=4, row0=0, xs=None):
    nc, dve = core.nc, core.prog.dve
    with core.prog.turns(name, D // CH) as i:
        def add(t, acc):
            mine = core.X[:, t, bass.ds(i * CH, CH)]
            return nc.vector.tensor_tensor(mine, acc, mine, ALU.add)
        done = project(core, w, i * CH, n_quads=n_quads, take=(dve, add), x_ready=x_ready, row0=row0, xs=xs)
    core.x_ready = done
    return done


def indexer(core, w_in, x_ready, spare):
    nc, prog = core.nc, core.prog
    pe, act, dve = prog.pe, prog.act, prog.dve
    c0 = INDEX_COL
    QI, KW = arena(core, "QI", [TB, IH * ID]), arena(core, "KW", [TB, ID + IH])
    KI, WI, KIT = arena(core, "KI", [TB, 2 * ID]), arena(core, "WI", [TB, IH]), arena(core, "KIT", [T])
    REL, SCORE = core.att.LG, core.att.PR[0]
    TOP, MASK = arena(core, "TOP", [TB, 8]), fixed(core, "MASK", [3 * P])
    QIT = spare[:, 0, :].rearrange("p (j t) -> p j t", t=T)
    with prog.turns("index_q", IH * ID // CH) as i:
        q_here = project(core, w_in, c0 + i * CH, take=copy_to(core, lambda t: QI[:, t, bass.ds(i * CH, CH)]), x_ready=x_ready)
    k_here = project(core, w_in, c0 + IH * ID, width=ID + IH, take=copy_to(core, lambda t: KW[:, t, :]))
    heads = lambda ap, n: ap.rearrange("p t (h w) -> p t h w", h=n)
    q_roped = rope(core, heads(QI, IH), heads(QI, IH), core.cos_i, core.sin_i, IH, ID, core.TMP, q_here)
    rope(core, heads(KW[:, :, 0:ID], 1), heads(KI[:, :, 0:ID], 1), core.cos_i, core.sin_i, 1, ID, core.TMP, k_here)
    dve.sync()
    dve.did(nc.vector.tensor_copy(KI[:, :, ID:2 * ID], KI[:, :, 0:ID]))
    k_roped = dve.did(nc.vector.tensor_scalar(WI[:, :, :], KW[:, :, ID:ID + IH], IH ** -0.5, None, ALU.mult))
    pe.wait(k_roped)
    pe.wait(core.tp_taken.now(back=1))
    for t in range(TB):
        ins = nc.tensor.transpose(core.TP[0][:, t * P:(t + 1) * P], KI[:, t, :], core.ident)
    act.wait(pe.did(ins))
    kit_ready = core.tp_taken.tick(nc.scalar.activation(KIT, core.TP[0][:, 0:T], ACT.Copy))
    for j in range(IH // 4):
        tp = core.TP[(j + 1) % 2]
        pe.wait(core.tp_taken.now(back=1))
        for s in range(2):
            for t in range(TB):
                c = (2 * j + s) * P
                ins = nc.tensor.transpose(tp[:, (2 * s + t) * P:(2 * s + t + 1) * P], QI[:, t, c:c + P], core.ident)
        act.wait(pe.did(ins))
        qit_ready = core.tp_taken.tick(nc.scalar.activation(QIT[:, 2 * j:2 * j + 2, :].rearrange("p j t -> p (j t)"), tp[:, :], ACT.Copy))
    pe.wait(core.tp_taken.now())
    pe.wait(qit_ready)
    taken, summed = [None, None], [None, None]
    for h in range(IH):
        sc, half = core.SC[h % 2], slice(ID * (h % 2), ID * (h % 2 + 1))
        pe.wait(taken[h % 2])
        nc.tensor.matmul(sc[:, 0:P], QIT[half, h // 2, 0:P], KIT[half, 0:P], start=True, stop=True)
        scored = pe.did(nc.tensor.matmul(sc[:, P:3 * P], QIT[half, h // 2, P:T], KIT[half, :], start=True, stop=True))
        act.wait(scored, summed[h % 2])
        taken[h % 2] = act.did(nc.scalar.activation(REL[h % 2], sc[:, 0:3 * P], ACT.Relu, scale=ID ** -0.5))
        dve.wait(taken[h % 2])
        dve.sync()
        for t, cs in ((0, slice(0, P)), (1, slice(P, 3 * P))):
            w = WI[:, t, h:h + 1]
            if h == 0:
                ins = nc.vector.tensor_scalar(SCORE[:, cs], REL[0][:, cs], w, None, ALU.mult)
            else:
                ins = nc.vector.scalar_tensor_tensor(SCORE[:, cs], REL[h % 2][:, cs], w, SCORE[:, cs], ALU.mult, ALU.add)
            summed[h % 2] = dve.did(ins)
    dve.sync()
    dve.did(nc.vector.tensor_tensor(SCORE, SCORE, core.causal, ALU.add))
    blocks = ((0, slice(0, P)), (1, slice(P, 3 * P)))
    for _ in range(KEEP // 8):
        dve.sync()
        for t, cs in blocks:
            dve.did(nc.vector.max(TOP[:, t, :], SCORE[:, cs]))
        dve.sync()
        for t, cs in blocks:
            dve.did(nc.vector.match_replace(SCORE[:, cs], TOP[:, t, :], SCORE[:, cs], REMOVED))
    dve.sync()
    dve.did(nc.vector.tensor_scalar(MASK, SCORE, REMOVED / 2, NEG, ALU.is_gt, ALU.mult))
    dve.sync()
    return MASK, dve.did(nc.vector.tensor_tensor(MASK, MASK, core.causal, ALU.add))


Q_COL, KV_COL, GATE_COL = 0, N2 * HD, N2 * HD + 6 * 2 * HD
DN_COL = GATE_COL + 3 * N2
Z_COL = DN_COL + 3 * DH * HD
AB_COL = Z_COL + DH * HD
MERGE_COL = AB_COL + 2 * DH
HQ = 4
LEVELS = 6
PADC = 32


def deltanet(core, a, QKV, AB, O, ready, DN):
    nc, prog = core.nc, core.prog
    pe, act, dve, pool = prog.pe, prog.act, prog.dve, prog.pool
    V, TT, TS, MM = nc.vector, nc.vector.tensor_tensor, nc.vector.tensor_scalar, nc.tensor.matmul
    four = lambda ap: ap.rearrange("p (h w) -> p h w", h=HQ)
    flat = lambda ap: ap.rearrange("p h w -> p (h w)")
    over_heads = lambda m: m.unsqueeze(1).to_broadcast([P, HQ, P])
    per_head = lambda s: s.unsqueeze(2).to_broadcast([P, HQ, P])
    ones, tri, same, lower = DN["ones"], DN["tri"], DN["same"], DN["lower"]
    masks = DN["levels"].rearrange("p (l w) -> p l w", l=LEVELS)
    G, B, GC, GL, E1, EG, EKD, BEG = (core.small_tables[:, n * TB * DH:(n + 1) * TB * DH] for n in range(8))
    by = lambda ap: ap.rearrange("p (t h) -> p t h", t=TB)
    dt = DN["dt"].unsqueeze(1).to_broadcast([P, TB, DH])
    dve.wait(ready)
    act.wait(DN["ready"])
    dve.wait(DN["ready"])
    dve.did(TT(by(G), AB[:, :, 0:DH], dt, ALU.add))
    act.after(dve)
    act.did(nc.scalar.activation(E1, G, ACT.Abs))
    act.sync()
    act.did(nc.scalar.activation(E1, E1, ACT.Exp, scale=-1.0))
    dve.after(act)
    dve.did(TS(E1, E1, 1.0, None, ALU.add))
    act.after(dve)
    act.did(nc.scalar.activation(E1, E1, ACT.Ln))
    act.did(nc.scalar.activation(DN["alog"], DN["alog"], ACT.Exp))
    dve.after(act)
    dve.did(V.scalar_tensor_tensor(G, G, 0.0, E1, ALU.max, ALU.add))
    dve.sync()
    dve.did(TT(by(G), by(G), DN["alog"].unsqueeze(1).to_broadcast([P, TB, DH]), ALU.mult))
    dve.sync()
    dve.did(TS(G, G, -1.0, None, ALU.mult))
    act.did(nc.scalar.activation(by(B), AB[:, :, DH:2 * DH], ACT.Sigmoid))
    pe.after(dve)
    pe.wait(core.tp_taken.now())
    pe.did(MM(core.TP[0][:, 0:TB * DH], tri, G, start=True, stop=True))
    pe.did(MM(core.TP[0][:, TB * DH:2 * TB * DH], same, G, start=True, stop=True))
    act.after(pe)
    act.did(nc.scalar.activation(GC, core.TP[0][:, 0:TB * DH], ACT.Copy))
    act.did(nc.scalar.activation(GL, core.TP[0][:, TB * DH:2 * TB * DH], ACT.Copy))
    dve.after(act)
    dve.did(TT(EKD, GL, GC, ALU.subtract))
    act.after(dve)
    act.did(nc.scalar.activation(EKD, EKD, ACT.Exp))
    act.did(nc.scalar.activation(EG, GC, ACT.Exp))
    dve.after(act)
    dve.did(TT(BEG, B, EG, ALU.mult))
    own = places(core, DN["memory"])
    STG = core.TMP[:, 0:TB * CH].rearrange("p (t w) -> p t w", t=TB)
    SQ = core.TMP[:, TB * CH:2 * TB * CH]
    YT = [own(HQ * T).rearrange("p (h t) -> p h t", h=HQ) for c in range(3)]
    m = {n: four(own(HQ * P)) for n in "R D L S TI Y QD EGR KBG KD VB STATE".split()}
    m.update(M=m["R"], DT=m["D"], VN=m["L"], WT=m["TI"], U=m["Y"])
    cw = own(3 * HQ * 4).rearrange("p (c n) -> p c n", c=3)
    h4 = {n: own(TB * HQ).rearrange("p (t h) -> p t h", t=TB) for n in ("G", "B", "GC", "EKD", "BEG")}
    src = dict(G=G, B=B, GC=GC, EKD=EKD, BEG=BEG)
    with prog.turns("deltanet", DH // HQ) as i:
        dve.after(pe, act)
        dve.sync()
        for n, v in h4.items():
            dve.did(V.tensor_copy(v, by(src[n])[:, :, bass.ds(i * HQ, HQ)]))
        dve.did(V.tensor_copy(cw, DN["conv"].rearrange("p (c n) -> p c n", c=3)[:, :, bass.ds(i * HQ * 4, HQ * 4)]))
        for c in range(3):
            pool.after(pe)
            pool.did(nc.gpsimd.tensor_copy(STG, QKV[:, :, bass.ds(i * CH + c * DH * HD, CH)]))
            pe.after(pool)
            for h in range(HQ):
                tp = core.TP[h // 2][:, (h % 2) * T:(h % 2 + 1) * T]
                if h % 2 == 0:
                    pe.after(dve)
                for t in range(TB):
                    pe.did(nc.tensor.transpose(tp[:, t * P:(t + 1) * P], STG[:, t, h * HD:(h + 1) * HD], core.ident))
            for h in range(HQ):
                x, y = core.TP[h // 2][:, (h % 2) * T:(h % 2 + 1) * T], YT[c][:, h, :]
                tap = lambda s: cw[:, c, h * 4 + 3 - s:h * 4 + 4 - s]
                dve.after(pe)
                dve.sync()
                dve.did(TS(y, x, tap(0), None, ALU.mult))
                for s in (1, 2, 3):
                    dve.sync()
                    dve.did(V.scalar_tensor_tensor(y[:, s:T], x[:, 0:T - s], tap(s), y[:, s:T], ALU.mult, ALU.add))
            act.after(dve)
            act.did(nc.scalar.activation(flat(YT[c]), flat(YT[c]), ACT.Silu))
        for c in range(2):
            act.after(act, pe, dve)
            act.did(nc.scalar.activation(SQ, flat(YT[c]), ACT.Square))
            pe.after(act)
            for j in range(2):
                pe.after(dve, act)
                pe.did(MM(core.SC[j][:, :], ones, SQ[:, j * CH:(j + 1) * CH], start=True, stop=True))
            for j in range(2):
                dve.after(pe)
                dve.did(TS(SQ[:, j * CH:(j + 1) * CH], core.SC[j][:, :], EPS, None, ALU.add))
            act.after(dve)
            act.did(nc.scalar.activation(SQ, SQ, ACT.Sqrt))
            dve.after(act)
            dve.did(V.reciprocal(SQ, SQ))
            dve.sync()
            y = flat(YT[c])
            if c == 0:
                dve.did(V.scalar_tensor_tensor(y, y, HD ** -0.5, SQ, ALU.mult, ALU.mult))
            else:
                dve.did(TT(y, y, SQ, ALU.mult))
        dve.did(V.memset(m["STATE"], 0.0))
        for t in range(TB):
            block = lambda c, h: YT[c][:, h, t * P:(t + 1) * P]
            for h in range(HQ):
                pe.after(dve, act)
                nc.tensor.transpose(core.TP[0][:, h * P:(h + 1) * P], block(1, h), core.ident)
                pe.did(nc.tensor.transpose(core.TP[1][:, h * P:(h + 1) * P], block(2, h), core.ident))
            dve.after(pe)
            dve.did(TT(m["KBG"], four(core.TP[0][:, :]), per_head(h4["BEG"][:, t, :]), ALU.mult))
            dve.did(TT(m["KD"], four(core.TP[0][:, :]), per_head(h4["EKD"][:, t, :]), ALU.mult))
            dve.did(TT(m["VB"], four(core.TP[1][:, :]), per_head(h4["B"][:, t, :]), ALU.mult))
            dve.did(TT(m["R"], over_heads(tri), per_head(h4["G"][:, t, :]), ALU.mult))
            pe.after(dve)
            pe.did(MM(core.SC[0][:, :], ones, flat(m["R"]), start=True, stop=True))
            act.after(pe)
            act.did(nc.scalar.activation(flat(m["EGR"]), core.SC[0][:, :], ACT.Exp))
            dve.after(act)
            dve.did(TT(m["D"], over_heads(lower), four(core.SC[0][:, :]), ALU.subtract))
            dve.sync()
            dve.did(TT(m["D"], m["D"], per_head(h4["GC"][:, t, :]), ALU.add))
            act.after(dve)
            act.did(nc.scalar.activation(flat(m["D"]), flat(m["D"]), ACT.Exp))
            for h in range(HQ):
                pe.did(MM(core.SC[1][:, h * P:(h + 1) * P], block(1, h), block(1, h), start=True, stop=True))
            dve.after(pe, act)
            dve.did(TT(m["L"], four(core.SC[1][:, :]), m["D"], ALU.mult))
            dve.did(TT(m["QD"], YT[0][:, :, t * P:(t + 1) * P], m["EGR"], ALU.mult))
            dve.sync()
            dve.did(TT(m["L"], m["L"], per_head(h4["B"][:, t, :]), ALU.mult))
            pe.after(act)
            for h in range(HQ):
                nc.tensor.transpose(core.TP[0][:, h * P:(h + 1) * P], m["D"][:, h, :], core.ident)
                pe.did(MM(core.TP[1][:, h * P:(h + 1) * P], block(1, h), block(0, h), start=True, stop=True))
            act.after(pe, dve)
            act.did(nc.scalar.activation(flat(m["DT"]), core.TP[0][:, :], ACT.Copy))
            dve.after(act)
            dve.did(TT(m["DT"], four(core.TP[1][:, :]), m["DT"], ALU.mult))
            dve.did(V.tensor_copy(m["TI"], over_heads(core.ident)))
            dve.did(V.tensor_copy(m["S"], over_heads(core.ident)))
            for level in range(LEVELS):
                dve.sync()
                dve.did(TT(m["M"], m["L"], over_heads(masks[:, level, :]), ALU.mult))
                pe.after(dve)
                for h in range(HQ):
                    pe.did(MM(core.SC[0][:, h * P:(h + 1) * P], m["M"][:, h, :], m["S"][:, h, :], start=True, stop=True))
                act.after(pe)
                act.did(nc.scalar.activation(flat(m["Y"]), core.SC[0][:, :], ACT.Copy))
                pe.after(act)
                for h in range(HQ):
                    pe.did(MM(core.SC[1][:, h * P:(h + 1) * P], m["TI"][:, h, :], m["Y"][:, h, :], start=True, stop=True))
                if level < LEVELS - 1:
                    for h in range(HQ):
                        pe.did(MM(core.SC[0][:, h * P:(h + 1) * P], m["Y"][:, h, :], m["TI"][:, h, :], start=True, stop=True))
                dve.after(pe)
                dve.did(TT(m["S"], m["S"], four(core.SC[1][:, :]), ALU.subtract))
                if level < LEVELS - 1:
                    dve.did(TT(m["TI"], m["TI"], four(core.SC[0][:, :]), ALU.subtract))
            pe.after(dve)
            for h in range(HQ):
                pe.did(MM(core.PV[0][:, h * P:(h + 1) * P], m["S"][:, h, :], m["VB"][:, h, :], start=True, stop=True))
                pe.did(MM(core.PV[1][:, h * P:(h + 1) * P], m["KBG"][:, h, :], m["S"][:, h, :], start=True, stop=True))
            act.after(pe)
            act.did(nc.scalar.activation(flat(m["U"]), core.PV[0][:, :], ACT.Copy))
            act.did(nc.scalar.activation(flat(m["WT"]), core.PV[1][:, :], ACT.Copy))
            for c in range(P // DC):
                r = slice(c * DC, (c + 1) * DC)
                pe.after(dve, act)
                pe.constant_wait()
                for h in range(HQ):
                    hs = slice(h * P, (h + 1) * P)
                    pe.did(MM(core.SC[0][r, hs], m["WT"][:, h, r], m["STATE"][:, h, :], start=True, stop=True))
                dve.after(pe)
                dve.did(TT(m["VN"][r], m["U"][r], four(core.SC[0][:, :])[r], ALU.subtract))
                pe.after(dve)
                pe.constant_wait()
                for h in range(HQ):
                    hs = slice(h * P, (h + 1) * P)
                    MM(core.PV[0][r, hs], m["QD"][:, h, r], m["STATE"][:, h, :], start=True, stop=False)
                    MM(core.PV[0][r, hs], m["DT"][r, h, r], m["VN"][r, h, :], start=False, stop=True)
                    pe.did(MM(core.SC[1][:, hs], m["KD"][r, h, :], m["VN"][r, h, :], start=True, stop=True))
                last = c * DC + DC - 1
                dve.after(pe)
                dve.did(TT(m["STATE"], m["STATE"], m["EGR"][:, :, last:last + 1].to_broadcast([P, HQ, P]), ALU.mult))
                dve.sync()
                dve.did(TT(m["STATE"], m["STATE"], four(core.SC[1][:, :]), ALU.add))
            act.after(pe)
            act.constant_wait()
            act.did(nc.scalar.activation(O[:, t, bass.ds(i * CH, CH)], core.PV[0][:, :], ACT.Copy))
    return act.line.now()


def third_layer(core, a, stop):
    nc, prog = core.nc, core.prog
    pe, act, dve, pool = prog.pe, prog.act, prog.dve, prog.pool
    w = a["w_in_2"][0]
    core.at = 0
    MG0, Q2, KV, Z = arena(core, "MG0", [TB, D]), arena(core, "Q2", [TB, N2 * HD]), arena(core, "KV", [TB, 6 * 2 * HD]), arena(core, "Z", [TB, DH * HD])
    MG1 = cut(core, core.arena, 4096, [TB, D])[0]
    rest = core.at
    own = places(core, [(core.arena, rest, ARENA)])
    QKV = cut(core, core.arena, 0, [TB, 3 * DH * HD])[0]
    GT, AB = core.GT, core.AB
    DN, at = {}, 6144
    sizes = dict(ones=P, tri=P, same=P, lower=P, levels=LEVELS * P, conv=24 * 4, dt=DH, alog=DH)
    dn_at = at
    for n, size in sizes.items():
        DN[n], at = cut(core, core.arena, at, [size])
    DN["memory"] = [(core.fixed, 0, core.fixed.shape[1]), (core.arena, at, 9216), (core.arena, rest, ARENA)]
    nc.sync.wait_ge(act.line.sem, act.line.now().value())
    nc.sync.wait_ge(dve.line.sem, dve.line.now().value())
    nc.sync.wait_ge(pe.line.sem, pe.line.now().value())
    nc.sync.wait_ge(core.quad_done.sem, core.quad_done.now().value())
    core.small.tick(nc.sync.dma_start(core.arena[:, dn_at:dn_at + 10 * P], a["dn_consts"]))
    core.small.tick(nc.sync.dma_start(DN["conv"], a["dn_conv"]))
    core.small.tick(nc.sync.dma_start(DN["dt"], a["dt_bias_2"][0].partition_broadcast(P)))
    DN["ready"] = core.small.tick(nc.sync.dma_start(DN["alog"], a["a_log_2"][0].partition_broadcast(P)))
    x_ready = token_norm(core, core.gains[:, 2, :], cut(core, core.arena, rest, [TB, D])[0], core.x_ready)
    project(core, w, GATE_COL, width=3 * N2, take=copy_to(core, lambda t: GT[:, t, :]), x_ready=x_ready)
    ab_ready = project(core, w, AB_COL, width=2 * DH, take=copy_to(core, lambda t: AB[:, t, :]))
    with prog.turns("dn_in", 3 * DH * HD // CH) as i:
        qkv_ready = project(core, w, DN_COL + i * CH, take=copy_to(core, lambda t: QKV[:, t, bass.ds(i * CH, CH)]))
    for e in (pool, dve, pe, act):
        e.wait(qkv_ready, ab_ready)
        e.wait(core.tp_taken.now())
    o_ready = deltanet(core, a, QKV, AB, Z, ab_ready, DN)
    O, SQ = Z, cut(core, core.arena, 0, [TB, DH * HD])[0]
    ZG = core.TMP[:, :].rearrange("p (t w) -> p t w", t=TB)
    act.after(pe, dve, pool)
    act.wait(o_ready)
    with prog.turns("z_in", DH * HD // CH) as i:
        z_ready = project(core, w, Z_COL + i * CH, take=copy_to(core, lambda t: ZG[:, t, bass.ds(i * CH, CH)]))
    act.wait(z_ready)
    act.did(nc.scalar.activation(SQ, O, ACT.Square))
    dve.after(act)
    dve.did(nc.vector.tensor_reduce(core.ss[:, 0:16], SQ.rearrange("p t (h w) -> p (t h) w", w=HD), AX.X, ALU.add))
    rstd(core, core.ss[:, 0:16], core.rs[:, 0:16], HD, dve.line.now())
    o16 = O.rearrange("p t (h w) -> p (t h) w", w=HD)
    dve.sync()
    dve.did(nc.vector.tensor_tensor(o16, o16, core.rs[:, 0:16].unsqueeze(2).to_broadcast([P, 16, HD]), ALU.mult))
    nc.sync.wait_ge(dve.line.sem, dve.line.now().value())
    g = core.small.tick(nc.sync.dma_start(SQ[:, 0, 0:HD], a["dn_norm_w_2"][0].partition_broadcast(P)))
    dve.wait(g)
    dve.sync()
    dve.did(nc.vector.tensor_tensor(o16, o16, SQ[:, 0, 0:HD].unsqueeze(1).to_broadcast([P, 16, HD]), ALU.mult))
    act.did(nc.scalar.activation(ZG, ZG, ACT.Silu))
    dve.after(act)
    dve.sync()
    dn_out = dve.did(nc.vector.tensor_tensor(Z, O, ZG, ALU.mult))
    act.after(dve)
    with prog.turns("q_in", N2 * HD // CH) as i:
        q_ready = project(core, w, Q_COL + i * CH, take=copy_to(core, lambda t: Q2[:, t, bass.ds(i * CH, CH)]))
    act.after(dve, pe)
    with prog.turns("kv_in", 6 * 2 * HD // CH) as i:
        q_ready = project(core, w, KV_COL + i * CH, take=copy_to(core, lambda t: KV[:, t, bass.ds(i * CH, CH)]))
    W1 = cut(core, core.arena, 0, [32, HD])[0]
    CW = own(2 * (HD + 32)).rearrange("p (j w) -> p j w", j=2)
    MC = own(TB * HQ * PADC + HQ + TB)
    KS, BD = own(4 * T).rearrange("p (j t) -> p j t", j=4), own(2 * HQ * HD).rearrange("p (g h d) -> p g h d", g=2, h=HQ)
    KC = own(4 * T).rearrange("p (j t) -> p j t", j=4)
    nc.sync.wait_ge(dve.line.sem, dve.line.now().value())
    nc.sync.wait_ge(pe.line.sem, pe.line.now().value())
    nc.sync.wait_ge(act.line.sem, act.line.now().value())
    w1_ready = core.small.tick(nc.sync.dma_start(W1, a["cmp_w1_k_2"][0].rearrange("(i d) e -> d i e", d=HD)))
    for j, n in enumerate("kv"):
        core.small.tick(nc.sync.dma_start(CW[:, j, 0:HD], a[f"cmp_w2_{n}_2"][0]))
        core.small.tick(nc.sync.dma_start(CW[:, j, HD:], a[f"cmp_pe_{n}_2"]))
    cmp_ready = core.small.tick(nc.sync.dma_start(MC, a["cmp_masks"]))
    cmp_mask = MC[:, 0:TB * HQ * PADC].rearrange("p (t n) -> p t n", t=TB)
    head_of, any_valid = MC[:, TB * HQ * PADC:TB * HQ * PADC + HQ], MC[:, TB * HQ * PADC + HQ:]
    heads = lambda ap: ap.rearrange("p t (h w) -> p t h w", w=HD)
    rope(core, heads(Q2), heads(Q2), core.cos, core.sin, N2, HD, core.TMP, q_ready)
    for kind in (0, 2, 4):
        mine = KV[:, :, kind * 2 * HD:(kind + 1) * 2 * HD]
        dve.sync()
        rope(core, heads(mine), heads(mine), core.cos, core.sin, 2, HD, core.TMP, None)
    att = core.att
    for n, (dst, kinds) in enumerate(((KC, (0, 1)), (KS, (2, 4)))):
        for j, kind in enumerate(kinds):
            pe.after(dve)
            pe.wait(core.tp_taken.now())
            for h in range(2):
                for t in range(TB):
                    c = (kind * 2 + h) * HD
                    ins = nc.tensor.transpose(core.TP[j][:, (2 * h + t) * P:(2 * h + t + 1) * P], KV[:, t, c:c + HD], core.ident)
            act.wait(pe.did(ins))
            core.tp_taken.tick(nc.scalar.activation(dst[:, 2 * j:2 * j + 2, :].rearrange("p h t -> p (h t)"), core.TP[j][:, :], ACT.Copy))
    BL = core.TMP[:, 0:32 * 2 * NC2].rearrange("p (i c) -> p i c", i=32)
    H1 = [att.LG[j][:, 0:2 * NC2] for j in range(2)]
    KCT, GV4 = att.PR[0][:, 0:2 * PADC], att.PR[1][:, 0:2 * P]
    dve.wait(cmp_ready, core.tp_taken.now())
    act.wait(cmp_ready)
    pe.wait(cmp_ready)
    for j in range(2):
        dve.after(pe)
        for h in range(2):
            x = KC[:, 2 * j + h, :]
            for half in range(2):
                rows = x[:, 16 * half:16 * half + 16 * NC2].rearrange("p (c i) -> p i c", i=16)
                pe_rows = CW[:, j, HD + 16 * half:HD + 16 * half + 16].unsqueeze(2).to_broadcast([P, 16, NC2])
                dve.did(nc.vector.tensor_tensor(BL[:, 16 * half:16 * half + 16, h * NC2:(h + 1) * NC2], rows, pe_rows, ALU.add))
        pe.after(dve)
        for i in range(32):
            ins = nc.tensor.matmul(core.SC[j][:, 0:2 * NC2], W1[:, i, :], BL[:, i, :], start=i == 0, stop=i == 31)
        act.wait(pe.did(ins))
        if j == 0:
            nc.sync.wait_ge(pe.line.sem, pe.line.now().value())
            w1_ready = core.small.tick(nc.sync.dma_start(W1, a["cmp_w1_v_2"][0].rearrange("(i d) e -> d i e", d=HD)))
            pe.wait(w1_ready)
        act.did(nc.scalar.activation(H1[j], core.SC[j][:, 0:2 * NC2], ACT.Gelu_apprx_tanh))
    dve.did(nc.vector.memset(KCT, 0.0))
    dve.did(nc.vector.memset(GV4, 0.0))
    dve.sync()
    dve.after(act)
    for g in range(2):
        for h in range(HQ):
            c = g * P + h * PADC
            dve.did(nc.vector.tensor_copy(GV4[:, c:c + NC2], H1[1][:, g * NC2:(g + 1) * NC2]))
    pe.after(act, dve)
    pe.did(nc.tensor.matmul(core.SC[0][:, 0:2 * NC2], CW[:, 0, 0:HD], H1[0], start=True, stop=True))
    for g in range(2):
        pe.did(nc.tensor.matmul(core.SC[1][:, g * HD:(g + 1) * HD], GV4[:, g * P:(g + 1) * P], CW[:, 1, 0:HD], start=True, stop=True))
    dve.after(pe)
    for g in range(2):
        dve.did(nc.vector.tensor_copy(KCT[:, g * PADC:g * PADC + NC2], core.SC[0][:, g * NC2:(g + 1) * NC2]))
        for h in range(HQ):
            dve.did(nc.vector.tensor_scalar(BD[:, g, h, :], core.SC[1][:, g * HD:(g + 1) * HD], head_of[:, h:h + 1], None, ALU.mult))
    act.did(nc.scalar.activation(GT[:, :, :], GT[:, :, :], ACT.Sigmoid))
    gates = GT[:, :, :].rearrange("p t (h b) -> p t h b", b=3)
    GB = own(3 * TB * N2).rearrange("p (b t h) -> p b t h", b=3, t=TB)
    dve.after(act)
    for b in range(3):
        dve.did(nc.vector.tensor_copy(GB[:, b], gates[:, :, :, b]))
    O = core.TMP[:, :].rearrange("p (t w) -> p t w", t=TB)
    GBS = own(TB * HQ).rearrange("p (t h) -> p t h", t=TB)
    CP, CS = att.LG[0][:, 0:TB * P].rearrange("p (t n) -> p t n", t=TB), own(TB * HQ)
    CPT = att.LG[1][:, 0:TB * P].rearrange("p (t n) -> p t n", t=TB)
    pool.after(dve, act)
    act.after(dve)
    pe.after(dve)
    with prog.turns("compressed", 2) as g:
        q_ready, _ = group_queries(core, Q2[:, :, bass.ds(g * CH, CH)])
        pe.wait(q_ready)
        pe.after(dve)
        for t in range(TB):
            for h in range(HQ):
                c = (t * HQ + h) * PADC
                ins = nc.tensor.matmul(core.SC[0][:, c:c + PADC], att.QT[:, h, t * P:(t + 1) * P], KCT[:, bass.ds(g * PADC, PADC)], start=True, stop=True)
        att.qt_taken.tick(ins)
        dve.wait(att.qt_taken.now())
        dve.after(act, pe)
        dve.did(nc.vector.scalar_tensor_tensor(CP[:, :, :], core.SC[0][:, 0:TB * HQ * PADC].rearrange("p (t n) -> p t n", t=TB), HD ** -0.5, cmp_mask, ALU.mult, ALU.add))
        dve.sync()
        cp = CP[:, :, :].rearrange("p t (h c) -> p (t h) c", c=PADC)
        wide = lambda s: s.unsqueeze(2).to_broadcast([P, TB * HQ, PADC])
        dve.did(nc.vector.tensor_reduce(CS, cp, AX.X, ALU.max))
        dve.sync()
        dve.did(nc.vector.tensor_tensor(cp, cp, wide(CS), ALU.subtract))
        act.after(dve)
        act.did(nc.scalar.activation(CP[:, :, :], CP[:, :, :], ACT.Exp))
        dve.after(act)
        dve.did(nc.vector.tensor_reduce(CS, cp, AX.X, ALU.add))
        dve.sync()
        dve.did(nc.vector.reciprocal(CS, CS))
        dve.did(nc.vector.tensor_copy(GBS[:, :, :], GB[:, 0, :, bass.ds(g * HQ, HQ)]))
        dve.sync()
        for t in range(TB):
            dve.did(nc.vector.scalar_tensor_tensor(CS[:, t * HQ:(t + 1) * HQ], CS[:, t * HQ:(t + 1) * HQ], any_valid[:, t:t + 1], GBS[:, t, :], ALU.mult, ALU.mult))
        dve.sync()
        dve.did(nc.vector.tensor_tensor(cp, cp, wide(CS), ALU.mult))
        pe.after(dve)
        pe.wait(core.tp_taken.now())
        for t in range(TB):
            ins = nc.tensor.transpose(core.TP[0][:, t * P:(t + 1) * P], CP[:, t, :], core.ident)
        act.wait(pe.did(ins))
        core.tp_taken.tick(nc.scalar.activation(CPT[:, :, :].rearrange("p t n -> p (t n)"), core.TP[0][:, 0:T], ACT.Copy))
        pe.wait(core.tp_taken.now())
        pe.after(act)
        for t in range(TB):
            pe.did(nc.tensor.matmul(core.PV[t][:, :], CPT[:, t, :], BD[:, bass.ds(g, 1), :, :].rearrange("p a h d -> p (a h d)"), start=True, stop=True))
            act.after(pe)
            act.constant_wait()
            act.did(nc.scalar.activation(O[:, t, bass.ds(g * CH, CH)], core.PV[t][:, :], ACT.Copy))
    dve.after(act, pe)
    dve.wait(core.tp_taken.now())
    for b, kind in ((1, 3), (2, 5)):
        with prog.turns(f"branch{b}", 2) as g:
            kt = lambda t0, n: KS[:, bass.ds(2 * (b - 1) + g, 1), t0:t0 + n].rearrange("p a n -> p (a n)")
            vt = lambda t: KV[:, t, bass.ds(kind * 2 * HD + g * HD, HD)]
            dve.wait(att.pv_taken.now())
            dve.did(nc.vector.tensor_copy(GBS[:, :, :], GB[:, b, :, bass.ds(g * HQ, HQ)]))

            def add_to(h, pv, multiplied, sum_ready, src_read):
                dve.wait(multiplied, sum_ready)
                for t in range(TB):
                    dve.did(nc.vector.tensor_tensor(att.SUM[:, h, t:t + 1], att.SUM[:, h, t:t + 1], GBS[:, t, h:h + 1], ALU.mult))
                dve.sync()
                for t in range(TB):
                    o = O[:, t, bass.ds(g * CH + h * HD, HD)]
                    ins = nc.vector.scalar_tensor_tensor(o, pv[:, t * HD:(t + 1) * HD], att.SUM[:, h, t:t + 1], o, ALU.mult, ALU.add)
                    p = att.pv_taken.tick(ins) if t else dve.did(ins)
                return p
            between = attend(core, Q2[:, :, bass.ds(g * CH, CH)], kt, vt, core.causal, add_to)
            m = 2 * (b - 1) + g
            mg = project(core, w, MERGE_COL + m * CH, take=copy_to(core, lambda t: MG0[:, t, bass.ds(m * CH, CH)]),
                           between=between)
    act.wait(att.pv_taken.now(), att.qt_taken.now(), att.qr_taken.now(), att.pt_taken.now())
    with prog.turns("merge_in", 4) as i:
        mg = project(core, w, MERGE_COL + (4 + i) * CH, take=copy_to(core, lambda t: MG1[:, t, bass.ds(i * CH, CH)]))
    act.wait(mg)
    for m in (MG0, MG1):
        for t in range(TB):
            act.did(nc.scalar.activation(m[:, t, :], m[:, t, :], ACT.Sigmoid))
    turn(core, O, ready=att.pv_taken.now(), k_tiles=8)
    x_ready = turn(core, Z, ready=dn_out, k_tiles=8, k0=8)
    pe.wait(x_ready[-1])
    dve.after(act)
    with prog.turns("up", D // CH) as i:
        g0 = lambda t: MG0[:, t, bass.ds(i * CH, CH)]
        g1 = lambda t: MG1[:, t, bass.ds(i * CH, CH)]
        gated0 = lambda t, acc: nc.vector.tensor_tensor(g0(t), acc, g0(t), ALU.mult)
        gated1 = lambda t, acc: nc.vector.tensor_tensor(g1(t), acc, g1(t), ALU.mult)
        project(core, a["w_up_nsa_2"][0], i * CH, n_quads=2, take=(dve, gated0))
        project(core, a["w_up_dn_2"][0], i * CH, n_quads=2, k0=8, take=(dve, gated1))
        dve.wait(core.acc_taken.now())
        for t in range(TB):
            dve.did(nc.vector.tensor_tensor(g0(t), g0(t), g1(t), ALU.add))
    x_ready = turn(core, MG0, ready=dve.line.now())
    return add_projection(core, "w_o", a["w_o_2"][0], x_ready)


def feed_forward(core, a, stop):
    nc, prog = core.nc, core.prog
    pe, act, dve = prog.pe, prog.act, prog.dve
    for e in (act, dve):
        e.after(pe, act, dve, prog.pool)
        e.wait(core.x_ready)
    SG, H = core.sb("SG", [P, TB, CH]), core.sb("H", [P, TB, D])
    hid = [core.sb(n, [P, KT_D, T], F32R) for n in ("HH", "HL")]
    x_ready = token_norm(core, core.gains[:, 3, :], H, core.x_ready)
    chunks, done = F_FF // CH, 0
    pe.wait(x_ready[-1])
    for part, n in enumerate((4, 4, 3)):
        act.after(pe)
        with prog.turns(f"ff{part}", n) as i:
            col = i * CH + done * CH
            act.wait(core.acc_taken.now())
            project(core, a["w_ffn_gate_2"][0], col, take=(act, lambda t, acc: nc.scalar.activation(SG[:, t, :], acc, ACT.Silu)))
            silu = core.acc_taken.now()
            dve.wait(silu)
            h_ready = project(core, a["w_ffn_up_2"][0], col, take=(dve, lambda t, acc: nc.vector.tensor_tensor(
                H[:, t, bass.ds(i * CH, CH)], acc, SG[:, t, :], ALU.mult)))
        ready = turn(core, H, ready=h_ready, k_tiles=n * QK, xs=hid)
        if n < 4:
            pe.wait(ready[-1])
            for c in range(D // CH):
                cs = slice(c * CH, (c + 1) * CH)
                core.x_ready = project(core, a["w_ffn_down_2"][0], c * CH, n_quads=n, row0=done * CH, xs=hid, take=(dve,
                    lambda t, acc: nc.vector.tensor_tensor(core.X[:, t, cs], acc, core.X[:, t, cs], ALU.add)))
        else:
            add_projection(core, f"down{part}", a["w_ffn_down_2"][0], ready, row0=done * CH, xs=hid)
        done += n
    if stop == "d":
        return
    nc.sync.wait_ge(dve.line.sem, dve.line.now().value())
    nc.sync.wait_ge(core.acc_taken.sem, core.acc_taken.now().value())
    nc.sync.wait_ge(core.tp_taken.sem, core.tp_taken.now().value())
    gain = H[:, 0, :]
    here = core.small.tick(nc.sync.dma_start(gain, a["norm_f_w_2"].partition_broadcast(P)))
    act.wait(core.x_ready)
    act.after(dve)
    for t in range(TB):
        act.did(nc.scalar.activation(hid[0][:, :, :].rearrange("p k t -> p (k t)")[:, t * D:(t + 1) * D], core.X[:, t, :], ACT.Square, accum_out=core.ss[:, t:t + 1]))
    rstd(core, core.ss[:, 0:TB], core.rs[:, 0:TB], D, act.line.now())
    dve.wait(here, core.x_ready)
    dve.sync()
    for t in range(TB):
        core.x_ready = dve.did(nc.vector.scalar_tensor_tensor(core.X[:, t, :], core.X[:, t, :], core.rs[:, t:t + 1], gain, ALU.mult, ALU.mult))


A_COLS = (0, 2560, 3072)
INDEX_COL = 5120


def program(nc, counts, a, out, stop=None):
    with ExitStack() as ctx:
        prog = Prog(nc, counts, ctx)
        core = memory(nc, prog)
        core.x_landed = Line(prog, "x_landed", 16)
        x_src, x_dst = a["x"], out
        for t in range(TB):
            core.x_ready = core.x_landed.tick(nc.sync.dma_start(core.X[:, t, :], x_src[0, t * P:(t + 1) * P, :]))
        core.small.tick(nc.scalar.dma_start(core.consts[:, :], a["consts"]))
        core.small.tick(nc.scalar.dma_start(core.gains[:, :, :], a["norm_gains"]))
        QKG = core.QKG
        p = core.small.tick(nc.scalar.dma_start(QKG[:, :], a["a_qk_gains"].partition_broadcast(P)))
        for e in (prog.pe, prog.act, prog.dve):
            e.wait(p)
        attention_layer(core, "a", a["a_w_in"][0], a["a_w_out"][0], core.gains[:, 0, :], QKG, A_COLS, indexer)
        if stop != "a":
            nc.sync.wait_ge(prog.dve.line.sem, prog.dve.line.now().value())
            p = core.small.tick(nc.sync.dma_start(QKG[:, :], a["b_qk_gains"].partition_broadcast(P)))
            prog.dve.wait(p)
            attention_layer(core, "b", a["b_w_in"][0], a["b_w_out"][0], core.gains[:, 1, :], QKG, A_COLS)
        if stop not in ("a", "b"):
            third_layer(core, a, stop)
        core.mixers.close()
        if stop not in ("a", "b", "c"):
            feed_forward(core, a, stop)
        nc.sync.wait_ge(core.x_ready.line.sem, core.x_ready.value())
        stored = Line(prog, "x_stored", 16)
        for t in range(TB):
            stored.tick(nc.sync.dma_start(x_dst[0, t * P:(t + 1) * P, :], core.X[:, t, :]))
        nc.sync.wait_ge(stored.sem, stored.now().value())
    return prog.seen


def laid_out(inputs):
    a = {n: np.ascontiguousarray(v) for n, v in inputs.items()}
    cols = lambda v: v.reshape(KT_D, P).T
    out = {n: a[n] for n in ("x", "a_w_in", "a_w_out", "b_w_in", "b_w_out")}
    out["consts"] = shape_constants()
    out["norm_gains"] = np.ascontiguousarray(np.stack([cols(a[n]) for n in ("a_norm", "b_norm", "norm1_w_2", "norm2_w_2")], 1))
    for n in ("w_in_2", "w_up_nsa_2", "w_up_dn_2", "w_o_2", "w_ffn_gate_2", "w_ffn_up_2", "w_ffn_down_2", "dt_bias_2", "a_log_2",
              "dn_norm_w_2", "cmp_w1_k_2", "cmp_w1_v_2", "cmp_w2_k_2", "cmp_w2_v_2", "norm_f_w_2"):
        out[n] = a[n]
    for n in ("cmp_pe_k_2", "cmp_pe_v_2"):
        out[n] = np.ascontiguousarray(a[n][0].T)
    out["dn_conv"] = np.ascontiguousarray(a["conv_w_2"][0, :, 0, :].reshape(4, 24, P).transpose(2, 1, 0).reshape(P, 96))
    out["dn_consts"], out["cmp_masks"] = more_constants()
    for l in ("a", "b"):
        out[l + "_qk_gains"] = np.concatenate([a[l + "_q_norm"][0]] * (NH // GRP) + [a[l + "_k_norm"][0]])
    return out


def kernel(**inputs):
    import concourse.bacc as bacc
    from concourse.bass_utils import run_bass_kernel_spmd
    arrays = laid_out(inputs)
    counts = {}
    for _ in range(2):
        nc = bacc.Bacc("TRN2", target_bir_lowering=False, num_devices=1)
        a = {n: nc.dram_tensor("in_" + n, v.shape, F32, kind="ExternalInput").ap() for n, v in arrays.items()}
        out = nc.dram_tensor("out_0", (1, T, D), F32, kind="ExternalOutput").ap()
        counts = program(nc, counts, a, out)
    r = run_bass_kernel_spmd(nc, [{"in_" + n: v for n, v in arrays.items()}], core_ids=[0])
    return r.results[0]["out_0"]
```

```python
from contextlib import contextmanager, ExitStack

import numpy as np
import concourse.bass as bass
from concourse import mybir

F32 = mybir.dt.float32
F32R = mybir.dt.float32r
ALU = mybir.AluOpType
ACT = mybir.ActivationFunctionType
AX = mybir.AxisListType

P = 128
T = 256
TB = T // P
D = 2048
KT_D = D // P
CH = 512
QK = 4
NH, NKV, HD = 16, 4, 128
GRP = NH // NKV
IH, ID = 16, 64
KEEP = min(256, T // 4)
EPS = 1e-6
NEG = -1e30
REMOVED = -3e38
CREDIT = 4096

N2, NG2 = 8, 4
NC2 = (T - 32) // 16 + 1
DH, DC = 8, 64
F_FF = 5632


ARENA = 15400

CONSTS = {"identity": P, "causal": 3 * P, "cos": TB * HD, "sin": TB * HD, "cos_index": TB * ID, "sin_index": TB * ID}
CONST_AT, CONST_COLS = {}, 0
for _name, _n in CONSTS.items():
    CONST_AT[_name] = (CONST_COLS, CONST_COLS + _n)
    CONST_COLS += _n


def shape_constants():
    out = {"identity": np.eye(P)}
    q, s = np.arange(P)[:, None], np.arange(T)[None, :]
    out["causal"] = np.concatenate([np.where(s[:, :P] <= q, 0, NEG), np.where(s <= q + P, 0, NEG)], 1)
    for name, w in (("", HD), ("_index", ID)):
        inv = np.float32(10000.0) ** (-np.arange(0, w, 2, dtype=np.float32) / np.float32(w))
        ang = np.arange(T, dtype=np.float32)[:, None] * inv[None, :]
        blocks = lambda a: a.reshape(TB, P, w).transpose(1, 0, 2).reshape(P, TB * w)
        out["cos" + name] = blocks(np.concatenate([np.cos(ang), np.cos(ang)], 1))
        out["sin" + name] = blocks(np.concatenate([-np.sin(ang), np.sin(ang)], 1))
    return np.concatenate([out[n].astype(np.float32) for n in CONSTS], 1)


def more_constants():
    j, i = np.arange(P)[:, None], np.arange(P)[None, :]
    same = (j // DC == i // DC)
    levels = []
    for level in range(LEVELS):
        b = 1 << level
        levels.append((j // (2 * b) == i // (2 * b)) & (j % (2 * b) >= b) & (i % (2 * b) < b))
    dn = [np.ones((P, P)), same & (j <= i), same, np.where(same & (i <= j), 0, NEG)] + levels
    q, c = np.arange(T), np.arange(PADC)
    seen = (c[None, :] < NC2) & (16 * c[None, :] + 31 <= q[:, None])
    bias = np.tile(np.where(seen, 0, NEG), (1, HQ)).reshape(TB, P, HQ * PADC).transpose(1, 0, 2).reshape(P, -1)
    head_of = np.arange(P)[:, None] // PADC == np.arange(HQ)[None, :]
    some = seen.any(1).reshape(TB, P).T
    return (np.concatenate(dn, 1).astype(np.float32), np.concatenate([bias, head_of, some], 1).astype(np.float32))


class Names:
    pass


class Line:

    def __init__(self, prog, name, by=1, credit=CREDIT):
        self.prog, self.name, self.by, self.credit = prog, name, by, credit
        self.sem = prog.ctx.enter_context(prog.nc.semaphore(name))
        self.total = self.local = 0
        prog.lines.append(self)
        if credit:
            prog.nc.sync.sem_inc(self.sem, credit)

    def tick(self, ins):
        ins.then_inc(self.sem, self.by)
        self.local += 1
        return self.now()

    def now(self, back=0):
        return Point(self, self.local - back, self.total, self.prog.loop)


class Point:
    def __init__(self, line, local, start, loop):
        self.line, self.local, self.start, self.loop = line, local, start, loop

    def value(self):
        line, prog = self.line, self.line.prog
        if self.loop is None:
            return (self.start + self.local) * line.by + line.credit
        per = self.loop.counts.get(line.name, 0)
        if prog.loop is self.loop:
            v = (self.start + self.local) * line.by + line.credit
            return v if per == 0 else self.loop.reg * (per * line.by) + v
        return (self.start + (self.loop.turns - 1) * per + self.local) * line.by + line.credit


class Loop:
    def __init__(self, reg, turns, counts):
        self.reg, self.turns, self.counts = reg, turns, counts


class Prog:

    def __init__(self, nc, counts, ctx):
        self.nc, self.counts, self.ctx = nc, counts, ctx
        self.lines, self.loop, self.seen = [], None, {}
        self.pe, self.act, self.dve = Eng(self, nc.tensor, "pe"), Eng(self, nc.scalar, "act"), Eng(self, nc.vector, "dve")
        self.pool = Eng(self, nc.gpsimd, "pool")

    @contextmanager
    def turns(self, name, n):
        for line in self.lines:
            line.total, line.local = line.total + line.local, 0
        counts = self.counts.get(name, {})
        with self.nc.Fori(0, n) as i:
            self.loop = Loop(i, n, counts)
            yield i
            self.loop = None
        self.seen[name] = {line.name: line.local for line in self.lines}
        for line in self.lines:
            line.total, line.local = line.total + n * line.local, 0


class Eng:

    def __init__(self, prog, raw, name):
        self.prog, self.raw, self.name = prog, raw, name
        self.line = Line(prog, name + "_done")
        self.held = 0

    def wait(self, *points):
        for p in points:
            if p is not None:
                self.raw.wait_ge(p.line.sem, p.value())

    def after(self, *engines):
        self.wait(*(e.line.now() for e in engines))

    def sync(self):
        self.wait(self.line.now())

    def constant_wait(self):
        if self.prog.loop:
            self.held += 1
            assert self.held < CREDIT
            self.raw.wait_ge(self.line.sem, self.held)

    def did(self, ins):
        return self.line.tick(ins)


def memory(nc, prog):
    core = Names()
    core.nc, core.prog = nc, prog
    sb = lambda name, shape, dt=F32: prog.ctx.enter_context(nc.sbuf_tensor(name, shape, dt))
    core.sb = sb
    core.X = sb("X", [P, TB, D])
    core.XH = sb("XH", [P, KT_D, T], F32R)
    core.XL = sb("XL", [P, KT_D, T], F32R)
    core.W = [sb(f"W{i}", [P, QK, CH]) for i in range(4)]
    core.WH = [sb(f"WH{i}", [P, QK, CH], F32R) for i in range(2)]
    core.WL = [sb(f"WL{i}", [P, QK, CH], F32R) for i in range(2)]
    bank = lambda name: prog.ctx.enter_context(nc.psum_tensor(name, [P, CH], F32))
    core.ACC = [bank(f"ACC{t}") for t in range(TB)]
    core.TP = [bank(f"TP{i}") for i in range(2)]
    core.SC = [bank(f"SC{i}") for i in range(2)]
    core.PV = [bank(f"PV{i}") for i in range(2)]
    line = lambda name, by=1: Line(prog, name, by)
    core.landed = [line(f"weights_landed{i}", 16) for i in range(4)]
    core.hi_done, core.lo_done = line("weights_rounded"), line("weights_rest")
    core.quad_done, core.acc0_done = line("quad_multiplied"), line("block0_accumulated")
    core.acc_taken, core.tp_taken = line("accumulators_taken"), line("transposes_taken")
    core.free_slots = line("free_weight_slots")
    core.small = line("constants_landed", 16)
    core.late = Line(prog, "late_constants_landed", 16, 0)
    core.n_quad, core.pending = 0, []
    core.consts = sb("consts", [P, CONST_COLS])
    c = lambda n: core.consts[:, CONST_AT[n][0]:CONST_AT[n][1]]
    core.ident, core.causal = c("identity"), c("causal")
    by_block = lambda n: c(n).rearrange("p (t w) -> p t w", t=TB)
    core.cos, core.sin, core.cos_i, core.sin_i = by_block("cos"), by_block("sin"), by_block("cos_index"), by_block("sin_index")
    core.gains = sb("gains", [P, 4, KT_D])
    core.ss, core.rs = sb("sums_of_squares", [P, 64]), sb("reciprocal_roots", [P, 64])
    core.TMP = sb("TMP", [P, 2048])
    core.small_tables = sb("small_tables", [P, 8 * TB * DH])
    core.GT, core.AB = sb("GT", [P, TB, 3 * N2]), sb("AB", [P, TB, 2 * DH])
    core.QKG = sb("qk_gains", [P, (NH // GRP + 1) * HD])
    core.mixers = ExitStack()
    own = lambda name, shape: core.mixers.enter_context(nc.sbuf_tensor(name, shape, F32))
    core.arena, core.fixed = own("arena", [P, ARENA]), own("attention_memory", [P, 4760])
    core.at = core.fixed_at = 0
    core.att = attention_memory(core)
    return core


def cut(core, mem, at, shape):
    n = 1
    for d in shape:
        n *= d
    assert at + n <= mem.shape[1], (at + n, mem.shape)
    flat = mem[:, at:at + n]
    if len(shape) == 1:
        return flat, at + n
    names = "abc"[:len(shape)]
    return flat.rearrange(f"p ({' '.join(names)}) -> p {' '.join(names)}", **dict(zip(names, shape))), at + n


def arena(core, name, shape):
    view, core.at = cut(core, core.arena, core.at, shape)
    return view


def places(core, regions):
    left = [list(r) for r in regions]

    def own(cols):
        for r in left:
            if r[1] + cols <= r[2]:
                r[1] += cols
                return r[0][:, r[1] - cols:r[1]]
        raise ValueError("no place left")
    return own


def fixed(core, name, shape):
    view, core.fixed_at = cut(core, core.fixed, core.fixed_at, shape)
    return view




def quads_of(w, col, n=4, width=CH, row0=0):
    return [(w[row0 + q * QK * P:row0 + (q + 1) * QK * P, bass.ds(col, width)], width) for q in range(n)]


def load_and_round(core, rows, width):
    nc, act = core.nc, core.prog.act
    slot, half, ahead = core.n_quad % 4, core.n_quad % 2, len(core.pending)
    core.n_quad += 1
    nc.sync.wait_ge(core.lo_done.sem, core.lo_done.now(back=3).value())
    if core.prog.loop:
        nc.sync.sem_inc(core.free_slots.sem, 1)
    here = core.landed[slot].tick(nc.sync.dma_start(core.W[slot][:, :, 0:width], rows.rearrange("(k p) n -> p k n", p=P)))
    act.wait(here, core.quad_done.now(back=1 - ahead))
    core.hi_done.tick(nc.scalar.activation(core.WH[half][:, :, 0:width], core.W[slot][:, :, 0:width], ACT.Copy))
    core.pending.append((slot, half, width))


def subtract_rounded(core):
    nc, dve = core.nc, core.prog.dve
    slot, half, width = core.pending[-1]
    dve.wait(core.hi_done.now())
    core.lo_done.tick(nc.vector.tensor_tensor(core.WL[half][:, :, 0:width], core.W[slot][:, :, 0:width],
                                              core.WH[half][:, :, 0:width].bitcast(F32), ALU.subtract))


def prime(core, quads):
    for rows, width in quads[len(core.pending):2]:
        load_and_round(core, rows, width)
        subtract_rounded(core)


def multiply(core, k0, first, last, xs=None):
    nc, pe = core.nc, core.prog.pe
    pe.wait(core.lo_done.now(back=len(core.pending) - 1))
    slot, half, width = core.pending.pop(0)
    WH, WL = core.WH[half], core.WL[half]
    for t in range(TB):
        if first:
            pe.wait(core.acc_taken.now(back=1) if t == 0 else core.acc_taken.now())
        out = core.ACC[t][:, 0:width]
        for k in range(QK):
            hi_x, lo_x = (x[:, k0 + k, t * P:(t + 1) * P] for x in (xs or (core.XH, core.XL)))
            nc.tensor.matmul(out, hi_x, WH[:, k, 0:width], start=first and k == 0, stop=False)
            nc.tensor.matmul(out, hi_x, WL[:, k, 0:width], start=False, stop=False)
            mm = nc.tensor.matmul(out, lo_x, WH[:, k, 0:width], start=False, stop=last and k == QK - 1)
        if last and t == 0:
            core.acc0_done.tick(mm)
    core.quad_done.tick(mm)


def project(core, quads, take, then=(), between=None, x_ready=None, k0=0, xs=None):
    pe, n = core.prog.pe, len(quads)
    prime(core, quads)
    coming = list(quads[len(core.pending):]) + list(then[:2])
    for q in range(n):
        if x_ready:
            pe.wait(x_ready[q])
        multiply(core, k0 + q * QK, q == 0, q == n - 1, xs)
        if q == n - 1:
            for t in range(TB):
                eng, make = take() if callable(take) else take
                eng.wait(core.acc0_done.now() if t == 0 else core.quad_done.now())
                eng.constant_wait()
                core.acc_taken.tick(make(t, core.ACC[t][:, 0:quads[-1][1]]))
        if coming:
            load_and_round(core, *coming[0])
        if between:
            between(q)
        if coming:
            subtract_rounded(core)
            coming.pop(0)
    return core.acc_taken.now()


def stream(core, name, n, quads, body, then):
    prime(core, quads(0))
    if n > 2:
        with core.prog.turns(name, n - 1) as i:
            body(i, quads(i + 1))
    else:
        body(0, quads(1))
    return body(n - 1, then)


def copy_to(core, dst):
    return core.prog.act, lambda t, acc: core.nc.scalar.activation(dst(t), acc, ACT.Copy)




def rstd(core, ss, out, width, ready, eps=EPS):
    act, dve, nc = core.prog.act, core.prog.dve, core.nc
    dve.wait(ready)
    dve.did(nc.vector.tensor_scalar(out, ss, 1.0 / width, eps, ALU.mult, ALU.add))
    act.wait(dve.line.now())
    act.did(nc.scalar.activation(out, out, ACT.Sqrt))
    dve.wait(act.line.now())
    return dve.did(nc.vector.reciprocal(out, out))


def turn(core, src, gain=None, ready=None, k_tiles=KT_D, k0=0, xs=None):
    nc, pe, act, dve = core.nc, core.prog.pe, core.prog.act, core.prog.dve
    XH, XL = xs or (core.XH, core.XL)
    act.wait(core.quad_done.now())
    pe.wait(core.tp_taken.now(), ready)
    points = []
    for j in range(k_tiles // 2):
        tp = core.TP[j % 2]
        pe.wait(core.tp_taken.now(back=1))
        for k in range(2):
            for t in range(TB):
                c = (2 * j + k) * P
                ins = nc.tensor.transpose(tp[:, (2 * k + t) * P:(2 * k + t + 1) * P], src[:, t, c:c + P], core.ident)
        turned = pe.did(ins)
        act.wait(turned)
        parts = 1 if gain is None else 2
        piece = []
        for s in range(parts):
            n = 2 // parts
            k = k0 + 2 * j + s * n
            piece.append((tp[:, s * T:(s + n) * T], XH[:, k:k + n, :].rearrange("p k t -> p (k t)"),
                          XL[:, k:k + n, :].rearrange("p k t -> p (k t)"),
                          1.0 if gain is None else gain[:, 2 * j + s:2 * j + s + 1]))
        for ps, hi, lo, g in piece:
            rounded = act.did(nc.scalar.activation(hi, ps, ACT.Copy, scale=g))
        dve.wait(rounded)
        for s, (ps, hi, lo, g) in enumerate(piece):
            ins = nc.vector.scalar_tensor_tensor(lo, ps, g, hi.bitcast(F32), ALU.mult, ALU.subtract)
            done = core.tp_taken.tick(ins) if s == parts - 1 else dve.did(ins)
        points.append(done)
    return [points[min(len(points) - 1, 2 * q + 1)] for q in range((k_tiles + 3) // 4)]


def token_norm(core, gain, scratch, ready):
    nc, act, dve = core.nc, core.prog.act, core.prog.dve
    act.wait(ready)
    for t in range(TB):
        p = act.did(nc.scalar.activation(scratch[:, t, :], core.X[:, t, :], ACT.Square, accum_out=core.ss[:, t:t + 1]))
    rstd(core, core.ss[:, 0:TB], core.rs[:, 0:TB], D, p)
    for t in range(TB):
        dve.sync()
        p = dve.did(nc.vector.tensor_scalar(scratch[:, t, :], core.X[:, t, :], core.rs[:, t:t + 1], None, ALU.mult))
    return turn(core, scratch, gain, p)


def rope(core, x, out, cos, sin, heads, width, tmp, ready, eng=None):
    nc, dve = core.nc, core.prog.dve
    h = width // 2
    dve.wait(ready)
    for t in range(TB):
        tm = tmp[:, t * heads * width:(t + 1) * heads * width].rearrange("p (h w) -> p h w", h=heads)
        s1 = sin[:, t:t + 1, 0:h].to_broadcast([P, heads, h])
        s2 = sin[:, t:t + 1, h:width].to_broadcast([P, heads, h])
        c = cos[:, t:t + 1, :].to_broadcast([P, heads, width])
        dve.did(nc.vector.tensor_tensor(tm[:, :, 0:h], x[:, t, :, h:width], s1, ALU.mult))
        dve.did(nc.vector.tensor_tensor(tm[:, :, h:width], x[:, t, :, 0:h], s2, ALU.mult))
        dve.sync()
        dve.did(nc.vector.tensor_tensor(out[:, t], x[:, t], c, ALU.mult))
        dve.sync()
        p = dve.did(nc.vector.tensor_tensor(out[:, t], out[:, t], tm, ALU.add))
    return p


def attention_memory(core):
    F = lambda n, shape: fixed(core, n, shape)
    line = lambda n: Line(core.prog, n)
    att = Names()
    att.QR, att.QT = F("QR", [TB, GRP * HD]), F("QT", [GRP, T])
    att.LG = [F(f"LG{j}", [3 * P]) for j in range(2)]
    att.PR = [F(f"PR{j}", [3 * P]) for j in range(2)]
    att.PT = [F(f"PT{j}", [3 * P]) for j in range(2)]
    att.NM, att.SUM = F("NM", [GRP, TB]), F("SUM", [GRP, TB])
    att.qr_taken, att.qt_taken, att.sc_taken = line("qr_turned"), line("qt_multiplied"), line("scores_taken")
    att.pr_taken, att.pt_taken, att.pv_taken = line("probs_turned"), line("probs_multiplied"), line("outputs_taken")
    return att


def group_queries(core, q_src):
    nc, att, pe, act, pool = core.nc, core.att, core.prog.pe, core.prog.act, core.prog.pool
    pool.wait(att.qr_taken.now())
    here = pool.did(nc.gpsimd.tensor_copy(att.QR, q_src))
    pe.wait(here)
    for h2 in range(2):
        pe.wait(core.tp_taken.now(back=1))
        for h in range(2):
            for t in range(TB):
                c = (2 * h2 + h) * HD
                ins = nc.tensor.transpose(core.TP[h2][:, (2 * h + t) * P:(2 * h + t + 1) * P], att.QR[:, t, c:c + HD], core.ident)
        act.wait((att.qr_taken.tick(ins) if h2 else pe.did(ins)), att.qt_taken.now())
        done = core.tp_taken.tick(nc.scalar.activation(att.QT[:, 2 * h2:2 * h2 + 2, :].rearrange("p h t -> p (h t)"),
                                                       core.TP[h2][:, :], ACT.Copy))
    return done, here


def head_softmax(core, h, q_ready, kt, mask):
    nc, att, pe, act, dve = core.nc, core.att, core.prog.pe, core.prog.act, core.prog.dve
    LG, PR, sc = att.LG[h % 2], att.PR[h % 2], core.SC[h % 2]
    pe.wait(q_ready, att.sc_taken.now(back=1))
    nc.tensor.matmul(sc[:, 0:P], att.QT[:, h, 0:P], kt(0, P), start=True, stop=True)
    ins = nc.tensor.matmul(sc[:, P:3 * P], att.QT[:, h, P:T], kt(0, T), start=True, stop=True)
    scored = att.qt_taken.tick(ins) if h == GRP - 1 else pe.did(ins)
    dve.wait(scored, att.pr_taken.now(back=1))
    masked = att.sc_taken.tick(nc.vector.scalar_tensor_tensor(LG, sc[:, 0:3 * P], HD ** -0.5, mask, ALU.mult, ALU.add))
    dve.wait(masked, att.pv_taken.now(back=1))
    dve.did(nc.vector.tensor_reduce(att.NM[:, h, 0:1], LG[:, 0:P], AX.X, ALU.max, negate=True))
    top = dve.did(nc.vector.tensor_reduce(att.NM[:, h, 1:2], LG[:, P:3 * P], AX.X, ALU.max, negate=True))
    act.wait(top)
    act.did(nc.scalar.activation(PR[:, 0:P], LG[:, 0:P], ACT.Exp, bias=att.NM[:, h, 0:1], accum_out=att.SUM[:, h, 0:1]))
    return act.did(nc.scalar.activation(PR[:, P:3 * P], LG[:, P:3 * P], ACT.Exp, bias=att.NM[:, h, 1:2],
                                        accum_out=att.SUM[:, h, 1:2]))


def head_turn(core, h, exp_ready):
    nc, att, pe, act, dve = core.nc, core.att, core.prog.pe, core.prog.act, core.prog.dve
    tp = core.TP[h % 2]
    pe.wait(exp_ready, core.tp_taken.now(back=1))
    for b in range(3):
        ins = nc.tensor.transpose(tp[:, b * P:(b + 1) * P], att.PR[h % 2][:, b * P:(b + 1) * P], core.ident)
    act.wait(att.pr_taken.tick(ins), att.pt_taken.now(back=1))
    pt_ready = core.tp_taken.tick(nc.scalar.activation(att.PT[h % 2], tp[:, 0:3 * P], ACT.Copy))
    dve.wait(exp_ready)
    return pt_ready, dve.did(nc.vector.reciprocal(att.SUM[:, h, :], att.SUM[:, h, :]))


def head_outputs(core, h, pt_ready, sum_ready, src_read, vt, store):
    nc, att, pe = core.nc, core.att, core.prog.pe
    PT, pv = att.PT[h % 2], core.PV[h % 2]
    pe.wait(pt_ready, att.pv_taken.now(back=1))
    nc.tensor.matmul(pv[:, 0:HD], PT[:, 0:P], vt(0), start=True, stop=True)
    nc.tensor.matmul(pv[:, HD:2 * HD], PT[:, P:2 * P], vt(0), start=True, stop=False)
    ins = att.pt_taken.tick(nc.tensor.matmul(pv[:, HD:2 * HD], PT[:, 2 * P:3 * P], vt(1), start=False, stop=True))
    return store(h, pv, ins, sum_ready, src_read)


def attend(core, q_src, kt, vt, mask, store):
    q_ready, src_read = group_queries(core, q_src)
    exp_ready = head_softmax(core, 0, q_ready, kt, mask)
    held = {"exp": exp_ready}

    def between(q):
        turned = head_turn(core, q, held["exp"])
        if q + 1 < GRP:
            held["exp"] = head_softmax(core, q + 1, q_ready, kt, mask)
        if q >= 1:
            head_outputs(core, q - 1, *held["turned"], src_read, vt, store)
        if q == GRP - 1:
            head_outputs(core, q, *turned, src_read, vt, store)
        held["turned"] = turned
    return between


def attention_layer(core, name, w_in, w_out, gain, qk_gain, cols, then, index=None):
    nc, prog, att = core.nc, core.prog, core.att
    pe, act, dve, pool = prog.pe, prog.act, prog.dve, prog.pool
    core.at = 0
    Q = arena(core, "Q", [TB, (NH + NKV) * HD])
    V = arena(core, "V", [TB, NKV * HD])
    G = arena(core, "G", [TB, D])
    prime(core, quads_of(w_in, INDEX_COL if index else cols[0]))
    x_ready = token_norm(core, gain, G, core.x_ready)
    core.prog.pe.wait(x_ready[-1])
    mask, mask_ready = core.causal, None
    if index:
        mask, mask_ready = index(core, w_in, x_ready, G, quads_of(w_in, cols[0]))
    C, last = att.QR, [None]

    def to_chunk(t, acc):
        return nc.scalar.activation(C[:, t, :], acc, ACT.Copy)

    def finish(chunk):
        rs = core.rs[:, 0:TB * GRP].unsqueeze(2).to_broadcast([P, TB * GRP, HD])
        flat = C.rearrange("p t (h w) -> p (t h) w", w=HD)
        mine = Q[:, :, bass.ds(chunk * CH, CH)]
        gain = qk_gain[:, bass.ds(chunk * HD, HD)].unsqueeze(1).to_broadcast([P, TB * GRP, HD])
        heads = lambda ap: ap.rearrange("p t (h w) -> p t h w", w=HD)

        def between(q):
            if q == 0:
                act.after(dve)
                act.wait(core.acc_taken.now())
                sq = act.did(nc.scalar.activation(core.TMP[:, 0:TB * CH].rearrange("p (t w) -> p t w", t=TB), C, ACT.Square))
                dve.wait(sq)
                s = dve.did(nc.vector.tensor_reduce(core.ss[:, 0:TB * GRP], core.TMP[:, 0:TB * CH].rearrange("p (h w) -> p h w", w=HD), AX.X, ALU.add))
                rstd(core, core.ss[:, 0:TB * GRP], core.rs[:, 0:TB * GRP], HD, s)
            if q == 1:
                dve.sync()
                dve.did(nc.vector.tensor_tensor(flat, flat, rs, ALU.mult))
                dve.sync()
                dve.did(nc.vector.tensor_tensor(flat, flat, gain, ALU.mult))
            if q == 2:
                last[0] = rope(core, heads(C), heads(mine), core.cos, core.sin, GRP, HD, core.TMP, dve.line.now())
        return between

    def take_chunk():
        act.after(dve)
        return act, to_chunk
    quads = lambda c: quads_of(w_in, cols[0] + c * CH)
    v_quads, g_quads = quads_of(w_in, cols[1]), lambda c: quads_of(w_in, cols[2] + c * CH)
    project(core, quads(0), (act, to_chunk), then=quads(1))
    stream(core, name + "_qk", NH // GRP, lambda c: quads(c + 1),
           lambda i, then: project(core, quads(i + 1), take_chunk, then=then, between=finish(i)), v_quads)
    v_ready = project(core, v_quads, copy_to(core, lambda t: V[:, t, :]), then=g_quads(0), between=finish(NH // GRP))
    roped = last[0]
    KT = arena(core, "KT", [NKV, T])
    for j in range(2):
        pe.wait(roped, core.tp_taken.now(back=1))
        for h in range(2):
            for t in range(TB):
                c = NH * HD + (2 * j + h) * HD
                ins = nc.tensor.transpose(core.TP[j][:, (2 * h + t) * P:(2 * h + t + 1) * P], Q[:, t, c:c + HD], core.ident)
        act.wait(pe.did(ins))
        kt_ready = core.tp_taken.tick(nc.scalar.activation(KT[:, 2 * j:2 * j + 2, :].rearrange("p h t -> p (h t)"), core.TP[j][:, :], ACT.Copy))
    pe.wait(kt_ready, v_ready)
    pool.wait(roped)
    dve.wait(mask_ready)

    def attend_group(i, then):
        kt = lambda t0, n: KT[:, bass.ds(i, 1), t0:t0 + n].rearrange("p a n -> p (a n)")
        vt = lambda t: V[:, t, bass.ds(i * HD, HD)]
        out = lambda h, t: Q[:, t, bass.ds(i * CH + h * HD, HD)]

        def store(h, pv, multiplied, sum_ready, src_read):
            act.wait(multiplied, sum_ready, src_read)
            act.constant_wait()
            act.did(nc.scalar.activation(out(h, 0), pv[:, 0:HD], ACT.Copy, scale=att.SUM[:, h, 0:1]))
            return att.pv_taken.tick(nc.scalar.activation(out(h, 1), pv[:, HD:2 * HD], ACT.Copy, scale=att.SUM[:, h, 1:2]))
        between = attend(core, Q[:, :, bass.ds(i * CH, CH)], kt, vt, mask, store)
        return project(core, g_quads(i), copy_to(core, lambda t: G[:, t, bass.ds(i * CH, CH)]), then=then, between=between)
    gated = stream(core, name + "_attend", NKV, g_quads, attend_group, quads_of(w_out, 0))
    points = gate(core, G, Q, ACT.Silu, gated, att.pv_taken.now())
    x_ready = turn(core, Q, ready=points)
    return add_projection(core, name + "_out", w_out, x_ready, then)


def gate(core, G, O, func, gated, ready, width=D):
    nc, act, dve = core.nc, core.prog.act, core.prog.dve
    act.wait(gated, ready)
    for c in range(width // CH):
        cs = slice(c * CH, (c + 1) * CH)
        for t in range(TB):
            p = act.did(nc.scalar.activation(G[:, t, cs], G[:, t, cs], func))
            dve.wait(p)
            p = dve.did(nc.vector.tensor_tensor(O[:, t, cs], O[:, t, cs], G[:, t, cs], ALU.mult))
    return p


def add_projection(core, name, w, x_ready, then, n_quads=4, row0=0, xs=None):
    nc, dve, pe = core.nc, core.prog.dve, core.prog.pe
    quads = lambda c: quads_of(w, c * CH, n_quads, row0=row0)

    def add_chunk(i, then):
        def add(t, acc):
            mine = core.X[:, t, bass.ds(i * CH, CH)]
            return nc.vector.tensor_tensor(mine, acc, mine, ALU.add)
        return project(core, quads(i), (dve, add), then=then, xs=xs)
    prime(core, quads(0))
    pe.wait(x_ready[-1])
    if n_quads % 4 == 0:
        core.x_ready = stream(core, name, D // CH, quads, add_chunk, then)
    else:
        for c in range(D // CH):
            core.x_ready = add_chunk(c, quads(c + 1) if c + 1 < D // CH else then)
    return core.x_ready


def indexer(core, w_in, x_ready, spare, then):
    nc, prog = core.nc, core.prog
    pe, act, dve = prog.pe, prog.act, prog.dve
    c0 = INDEX_COL
    QI, KW = arena(core, "QI", [TB, IH * ID]), arena(core, "KW", [TB, ID + IH])
    KI, WI, KIT = arena(core, "KI", [TB, 2 * ID]), arena(core, "WI", [TB, IH]), arena(core, "KIT", [T])
    REL, SCORE = core.att.LG, core.att.PR[0]
    TOP, MASK = arena(core, "TOP", [TB, 8]), fixed(core, "MASK", [3 * P])
    QIT = spare[:, 0, :].rearrange("p (j t) -> p j t", t=T)
    quads, k_quads = lambda c: quads_of(w_in, c0 + c * CH), quads_of(w_in, c0 + IH * ID, width=ID + IH)
    q_here = stream(core, "index_q", IH * ID // CH, quads, lambda i, then: project(
        core, quads(i), copy_to(core, lambda t: QI[:, t, bass.ds(i * CH, CH)]), then=then), k_quads)
    k_here = project(core, k_quads, copy_to(core, lambda t: KW[:, t, :]), then=then)
    heads = lambda ap, n: ap.rearrange("p t (h w) -> p t h w", h=n)
    q_roped = rope(core, heads(QI, IH), heads(QI, IH), core.cos_i, core.sin_i, IH, ID, core.TMP, q_here)
    rope(core, heads(KW[:, :, 0:ID], 1), heads(KI[:, :, 0:ID], 1), core.cos_i, core.sin_i, 1, ID, core.TMP, k_here)
    dve.sync()
    dve.did(nc.vector.tensor_copy(KI[:, :, ID:2 * ID], KI[:, :, 0:ID]))
    k_roped = dve.did(nc.vector.tensor_scalar(WI[:, :, :], KW[:, :, ID:ID + IH], IH ** -0.5, None, ALU.mult))
    pe.wait(k_roped)
    pe.wait(core.tp_taken.now(back=1))
    for t in range(TB):
        ins = nc.tensor.transpose(core.TP[0][:, t * P:(t + 1) * P], KI[:, t, :], core.ident)
    act.wait(pe.did(ins))
    kit_ready = core.tp_taken.tick(nc.scalar.activation(KIT, core.TP[0][:, 0:T], ACT.Copy))
    for j in range(IH // 4):
        tp = core.TP[(j + 1) % 2]
        pe.wait(core.tp_taken.now(back=1))
        for s in range(2):
            for t in range(TB):
                c = (2 * j + s) * P
                ins = nc.tensor.transpose(tp[:, (2 * s + t) * P:(2 * s + t + 1) * P], QI[:, t, c:c + P], core.ident)
        act.wait(pe.did(ins))
        qit_ready = core.tp_taken.tick(nc.scalar.activation(QIT[:, 2 * j:2 * j + 2, :].rearrange("p j t -> p (j t)"), tp[:, :], ACT.Copy))
    pe.wait(core.tp_taken.now())
    pe.wait(qit_ready)
    taken, summed = [None, None], [None, None]
    for h in range(IH):
        sc, half = core.SC[h % 2], slice(ID * (h % 2), ID * (h % 2 + 1))
        pe.wait(taken[h % 2])
        nc.tensor.matmul(sc[:, 0:P], QIT[half, h // 2, 0:P], KIT[half, 0:P], start=True, stop=True)
        scored = pe.did(nc.tensor.matmul(sc[:, P:3 * P], QIT[half, h // 2, P:T], KIT[half, :], start=True, stop=True))
        act.wait(scored, summed[h % 2])
        taken[h % 2] = act.did(nc.scalar.activation(REL[h % 2], sc[:, 0:3 * P], ACT.Relu, scale=ID ** -0.5))
        dve.wait(taken[h % 2])
        dve.sync()
        for t, cs in ((0, slice(0, P)), (1, slice(P, 3 * P))):
            w = WI[:, t, h:h + 1]
            if h == 0:
                ins = nc.vector.tensor_scalar(SCORE[:, cs], REL[0][:, cs], w, None, ALU.mult)
            else:
                ins = nc.vector.scalar_tensor_tensor(SCORE[:, cs], REL[h % 2][:, cs], w, SCORE[:, cs], ALU.mult, ALU.add)
            summed[h % 2] = dve.did(ins)
    dve.sync()
    dve.did(nc.vector.tensor_tensor(SCORE, SCORE, core.causal, ALU.add))
    blocks = ((0, slice(0, P)), (1, slice(P, 3 * P)))
    for _ in range(KEEP // 8):
        dve.sync()
        for t, cs in blocks:
            dve.did(nc.vector.max(TOP[:, t, :], SCORE[:, cs]))
        dve.sync()
        for t, cs in blocks:
            dve.did(nc.vector.match_replace(SCORE[:, cs], TOP[:, t, :], SCORE[:, cs], REMOVED))
    dve.sync()
    dve.did(nc.vector.tensor_scalar(MASK, SCORE, REMOVED / 2, NEG, ALU.is_gt, ALU.mult))
    dve.sync()
    return MASK, dve.did(nc.vector.tensor_tensor(MASK, MASK, core.causal, ALU.add))


Q_COL, KV_COL, GATE_COL = 0, N2 * HD, N2 * HD + 6 * 2 * HD
DN_COL = GATE_COL + 3 * N2
Z_COL = DN_COL + 3 * DH * HD
AB_COL = Z_COL + DH * HD
MERGE_COL = AB_COL + 2 * DH
HQ = 4
LEVELS = 6
PADC = 32


def deltanet(core, a, QKV, AB, O, ready, DN):
    nc, prog = core.nc, core.prog
    pe, act, dve, pool = prog.pe, prog.act, prog.dve, prog.pool
    V, TT, TS, MM = nc.vector, nc.vector.tensor_tensor, nc.vector.tensor_scalar, nc.tensor.matmul
    four = lambda ap: ap.rearrange("p (h w) -> p h w", h=HQ)
    flat = lambda ap: ap.rearrange("p h w -> p (h w)")
    over_heads = lambda m: m.unsqueeze(1).to_broadcast([P, HQ, P])
    per_head = lambda s: s.unsqueeze(2).to_broadcast([P, HQ, P])
    ones, tri, same, lower = DN["ones"], DN["tri"], DN["same"], DN["lower"]
    masks = DN["levels"].rearrange("p (l w) -> p l w", l=LEVELS)
    G, B, GC, GL, E1, EG, EKD, BEG = (core.small_tables[:, n * TB * DH:(n + 1) * TB * DH] for n in range(8))
    by = lambda ap: ap.rearrange("p (t h) -> p t h", t=TB)
    dt = DN["dt"].unsqueeze(1).to_broadcast([P, TB, DH])
    dve.wait(ready)
    act.wait(DN["ready"])
    dve.wait(DN["ready"])
    dve.did(TT(by(G), AB[:, :, 0:DH], dt, ALU.add))
    act.after(dve)
    act.did(nc.scalar.activation(E1, G, ACT.Abs))
    act.sync()
    act.did(nc.scalar.activation(E1, E1, ACT.Exp, scale=-1.0))
    dve.after(act)
    dve.did(TS(E1, E1, 1.0, None, ALU.add))
    act.after(dve)
    act.did(nc.scalar.activation(E1, E1, ACT.Ln))
    act.did(nc.scalar.activation(DN["alog"], DN["alog"], ACT.Exp))
    dve.after(act)
    dve.did(V.scalar_tensor_tensor(G, G, 0.0, E1, ALU.max, ALU.add))
    dve.sync()
    dve.did(TT(by(G), by(G), DN["alog"].unsqueeze(1).to_broadcast([P, TB, DH]), ALU.mult))
    dve.sync()
    dve.did(TS(G, G, -1.0, None, ALU.mult))
    act.did(nc.scalar.activation(by(B), AB[:, :, DH:2 * DH], ACT.Sigmoid))
    pe.after(dve)
    pe.wait(core.tp_taken.now())
    pe.did(MM(core.TP[0][:, 0:TB * DH], tri, G, start=True, stop=True))
    pe.did(MM(core.TP[0][:, TB * DH:2 * TB * DH], same, G, start=True, stop=True))
    act.after(pe)
    act.did(nc.scalar.activation(GC, core.TP[0][:, 0:TB * DH], ACT.Copy))
    act.did(nc.scalar.activation(GL, core.TP[0][:, TB * DH:2 * TB * DH], ACT.Copy))
    dve.after(act)
    dve.did(TT(EKD, GL, GC, ALU.subtract))
    act.after(dve)
    act.did(nc.scalar.activation(EKD, EKD, ACT.Exp))
    act.did(nc.scalar.activation(EG, GC, ACT.Exp))
    dve.after(act)
    dve.did(TT(BEG, B, EG, ALU.mult))
    own = places(core, DN["memory"])
    STG = core.TMP[:, 0:TB * CH].rearrange("p (t w) -> p t w", t=TB)
    SQ = core.TMP[:, TB * CH:2 * TB * CH]
    YT = [own(HQ * T).rearrange("p (h t) -> p h t", h=HQ) for c in range(3)]
    m = {n: four(own(HQ * P)) for n in "R D L S TI Y QD EGR KBG KD VB STATE".split()}
    m.update(M=m["R"], DT=m["D"], VN=m["L"], WT=m["TI"], U=m["Y"])
    cw = own(3 * HQ * 4).rearrange("p (c n) -> p c n", c=3)
    h4 = {n: own(TB * HQ).rearrange("p (t h) -> p t h", t=TB) for n in ("G", "B", "GC", "EKD", "BEG")}
    src = dict(G=G, B=B, GC=GC, EKD=EKD, BEG=BEG)
    with prog.turns("deltanet", DH // HQ) as i:
        dve.after(pe, act)
        dve.sync()
        for n, v in h4.items():
            dve.did(V.tensor_copy(v, by(src[n])[:, :, bass.ds(i * HQ, HQ)]))
        dve.did(V.tensor_copy(cw, DN["conv"].rearrange("p (c n) -> p c n", c=3)[:, :, bass.ds(i * HQ * 4, HQ * 4)]))
        for c in range(3):
            pool.after(pe)
            pool.did(nc.gpsimd.tensor_copy(STG, QKV[:, :, bass.ds(i * CH + c * DH * HD, CH)]))
            pe.after(pool)
            for h in range(HQ):
                tp = core.TP[h // 2][:, (h % 2) * T:(h % 2 + 1) * T]
                if h % 2 == 0:
                    pe.after(dve)
                for t in range(TB):
                    pe.did(nc.tensor.transpose(tp[:, t * P:(t + 1) * P], STG[:, t, h * HD:(h + 1) * HD], core.ident))
            for h in range(HQ):
                x, y = core.TP[h // 2][:, (h % 2) * T:(h % 2 + 1) * T], YT[c][:, h, :]
                tap = lambda s: cw[:, c, h * 4 + 3 - s:h * 4 + 4 - s]
                dve.after(pe)
                dve.sync()
                dve.did(TS(y, x, tap(0), None, ALU.mult))
                for s in (1, 2, 3):
                    dve.sync()
                    dve.did(V.scalar_tensor_tensor(y[:, s:T], x[:, 0:T - s], tap(s), y[:, s:T], ALU.mult, ALU.add))
            act.after(dve)
            act.did(nc.scalar.activation(flat(YT[c]), flat(YT[c]), ACT.Silu))
        for c in range(2):
            act.after(act, pe, dve)
            act.did(nc.scalar.activation(SQ, flat(YT[c]), ACT.Square))
            pe.after(act)
            for j in range(2):
                pe.after(dve, act)
                pe.did(MM(core.SC[j][:, :], ones, SQ[:, j * CH:(j + 1) * CH], start=True, stop=True))
            for j in range(2):
                dve.after(pe)
                dve.did(TS(SQ[:, j * CH:(j + 1) * CH], core.SC[j][:, :], EPS, None, ALU.add))
            act.after(dve)
            act.did(nc.scalar.activation(SQ, SQ, ACT.Sqrt))
            dve.after(act)
            dve.did(V.reciprocal(SQ, SQ))
            dve.sync()
            y = flat(YT[c])
            if c == 0:
                dve.did(V.scalar_tensor_tensor(y, y, HD ** -0.5, SQ, ALU.mult, ALU.mult))
            else:
                dve.did(TT(y, y, SQ, ALU.mult))
        dve.did(V.memset(m["STATE"], 0.0))
        for t in range(TB):
            block = lambda c, h: YT[c][:, h, t * P:(t + 1) * P]
            for h in range(HQ):
                pe.after(dve, act)
                nc.tensor.transpose(core.TP[0][:, h * P:(h + 1) * P], block(1, h), core.ident)
                pe.did(nc.tensor.transpose(core.TP[1][:, h * P:(h + 1) * P], block(2, h), core.ident))
            dve.after(pe)
            dve.did(TT(m["KBG"], four(core.TP[0][:, :]), per_head(h4["BEG"][:, t, :]), ALU.mult))
            dve.did(TT(m["KD"], four(core.TP[0][:, :]), per_head(h4["EKD"][:, t, :]), ALU.mult))
            dve.did(TT(m["VB"], four(core.TP[1][:, :]), per_head(h4["B"][:, t, :]), ALU.mult))
            dve.did(TT(m["R"], over_heads(tri), per_head(h4["G"][:, t, :]), ALU.mult))
            pe.after(dve)
            pe.did(MM(core.SC[0][:, :], ones, flat(m["R"]), start=True, stop=True))
            act.after(pe)
            act.did(nc.scalar.activation(flat(m["EGR"]), core.SC[0][:, :], ACT.Exp))
            dve.after(act)
            dve.did(TT(m["D"], over_heads(lower), four(core.SC[0][:, :]), ALU.subtract))
            dve.sync()
            dve.did(TT(m["D"], m["D"], per_head(h4["GC"][:, t, :]), ALU.add))
            act.after(dve)
            act.did(nc.scalar.activation(flat(m["D"]), flat(m["D"]), ACT.Exp))
            for h in range(HQ):
                pe.did(MM(core.SC[1][:, h * P:(h + 1) * P], block(1, h), block(1, h), start=True, stop=True))
            dve.after(pe, act)
            dve.did(TT(m["L"], four(core.SC[1][:, :]), m["D"], ALU.mult))
            dve.did(TT(m["QD"], YT[0][:, :, t * P:(t + 1) * P], m["EGR"], ALU.mult))
            dve.sync()
            dve.did(TT(m["L"], m["L"], per_head(h4["B"][:, t, :]), ALU.mult))
            pe.after(act)
            for h in range(HQ):
                nc.tensor.transpose(core.TP[0][:, h * P:(h + 1) * P], m["D"][:, h, :], core.ident)
                pe.did(MM(core.TP[1][:, h * P:(h + 1) * P], block(1, h), block(0, h), start=True, stop=True))
            act.after(pe, dve)
            act.did(nc.scalar.activation(flat(m["DT"]), core.TP[0][:, :], ACT.Copy))
            dve.after(act)
            dve.did(TT(m["DT"], four(core.TP[1][:, :]), m["DT"], ALU.mult))
            dve.did(V.tensor_copy(m["TI"], over_heads(core.ident)))
            dve.did(V.tensor_copy(m["S"], over_heads(core.ident)))
            for level in range(LEVELS):
                dve.sync()
                dve.did(TT(m["M"], m["L"], over_heads(masks[:, level, :]), ALU.mult))
                pe.after(dve)
                for h in range(HQ):
                    pe.did(MM(core.SC[0][:, h * P:(h + 1) * P], m["M"][:, h, :], m["S"][:, h, :], start=True, stop=True))
                act.after(pe)
                act.did(nc.scalar.activation(flat(m["Y"]), core.SC[0][:, :], ACT.Copy))
                pe.after(act)
                for h in range(HQ):
                    pe.did(MM(core.SC[1][:, h * P:(h + 1) * P], m["TI"][:, h, :], m["Y"][:, h, :], start=True, stop=True))
                if level < LEVELS - 1:
                    for h in range(HQ):
                        pe.did(MM(core.SC[0][:, h * P:(h + 1) * P], m["Y"][:, h, :], m["TI"][:, h, :], start=True, stop=True))
                dve.after(pe)
                dve.did(TT(m["S"], m["S"], four(core.SC[1][:, :]), ALU.subtract))
                if level < LEVELS - 1:
                    dve.did(TT(m["TI"], m["TI"], four(core.SC[0][:, :]), ALU.subtract))
            pe.after(dve)
            for h in range(HQ):
                pe.did(MM(core.PV[0][:, h * P:(h + 1) * P], m["S"][:, h, :], m["VB"][:, h, :], start=True, stop=True))
                pe.did(MM(core.PV[1][:, h * P:(h + 1) * P], m["KBG"][:, h, :], m["S"][:, h, :], start=True, stop=True))
            act.after(pe)
            act.did(nc.scalar.activation(flat(m["U"]), core.PV[0][:, :], ACT.Copy))
            act.did(nc.scalar.activation(flat(m["WT"]), core.PV[1][:, :], ACT.Copy))
            for c in range(P // DC):
                r = slice(c * DC, (c + 1) * DC)
                pe.after(dve, act)
                pe.constant_wait()
                for h in range(HQ):
                    hs = slice(h * P, (h + 1) * P)
                    pe.did(MM(core.SC[0][r, hs], m["WT"][:, h, r], m["STATE"][:, h, :], start=True, stop=True))
                dve.after(pe)
                dve.did(TT(m["VN"][r], m["U"][r], four(core.SC[0][:, :])[r], ALU.subtract))
                pe.after(dve)
                pe.constant_wait()
                for h in range(HQ):
                    hs = slice(h * P, (h + 1) * P)
                    MM(core.PV[0][r, hs], m["QD"][:, h, r], m["STATE"][:, h, :], start=True, stop=False)
                    MM(core.PV[0][r, hs], m["DT"][r, h, r], m["VN"][r, h, :], start=False, stop=True)
                    pe.did(MM(core.SC[1][:, hs], m["KD"][r, h, :], m["VN"][r, h, :], start=True, stop=True))
                last = c * DC + DC - 1
                dve.after(pe)
                dve.did(TT(m["STATE"], m["STATE"], m["EGR"][:, :, last:last + 1].to_broadcast([P, HQ, P]), ALU.mult))
                dve.sync()
                dve.did(TT(m["STATE"], m["STATE"], four(core.SC[1][:, :]), ALU.add))
            act.after(pe)
            act.constant_wait()
            act.did(nc.scalar.activation(O[:, t, bass.ds(i * CH, CH)], core.PV[0][:, :], ACT.Copy))
    return act.line.now()


def third_layer(core, a, stop):
    nc, prog = core.nc, core.prog
    pe, act, dve, pool = prog.pe, prog.act, prog.dve, prog.pool
    w = a["w_in_2"][0]
    core.at = 0
    MG0, Q2, KV, Z = arena(core, "MG0", [TB, D]), arena(core, "Q2", [TB, N2 * HD]), arena(core, "KV", [TB, 6 * 2 * HD]), arena(core, "Z", [TB, DH * HD])
    MG1 = cut(core, core.arena, 4096, [TB, D])[0]
    rest = core.at
    own = places(core, [(core.arena, rest, ARENA)])
    QKV = cut(core, core.arena, 0, [TB, 3 * DH * HD])[0]
    GT, AB = core.GT, core.AB
    DN, at = {}, 6144
    sizes = dict(ones=P, tri=P, same=P, lower=P, levels=LEVELS * P, conv=24 * 4, dt=DH, alog=DH)
    dn_at = at
    for n, size in sizes.items():
        DN[n], at = cut(core, core.arena, at, [size])
    DN["memory"] = [(core.fixed, 0, core.fixed.shape[1]), (core.arena, at, 9216), (core.arena, rest, ARENA)]
    nc.gpsimd.wait_ge(act.line.sem, act.line.now().value())
    nc.gpsimd.wait_ge(dve.line.sem, dve.line.now().value())
    nc.gpsimd.wait_ge(pe.line.sem, pe.line.now().value())
    nc.gpsimd.wait_ge(core.quad_done.sem, core.quad_done.now().value())
    core.late.tick(nc.gpsimd.dma_start(core.arena[:, dn_at:dn_at + 10 * P], a["dn_consts"]))
    core.late.tick(nc.gpsimd.dma_start(DN["conv"], a["dn_conv"]))
    core.late.tick(nc.gpsimd.dma_start(DN["dt"], a["dt_bias_2"][0].partition_broadcast(P)))
    DN["ready"] = core.late.tick(nc.gpsimd.dma_start(DN["alog"], a["a_log_2"][0].partition_broadcast(P)))
    x_ready = token_norm(core, core.gains[:, 2, :], cut(core, core.arena, rest, [TB, D])[0], core.x_ready)
    take = lambda buf, i: copy_to(core, lambda t: buf[:, t, bass.ds(i * CH, CH)])
    gt_quads, ab_quads = quads_of(w, GATE_COL, width=3 * N2), quads_of(w, AB_COL, width=2 * DH)
    dn_quads = lambda c: quads_of(w, DN_COL + c * CH)
    z_quads, q_quads, kv_quads, mg_quads = (lambda c, col=col: quads_of(w, col + c * CH) for col in (Z_COL, Q_COL, KV_COL, MERGE_COL))
    pe.wait(x_ready[-1])
    project(core, gt_quads, copy_to(core, lambda t: GT[:, t, :]), then=ab_quads)
    ab_ready = project(core, ab_quads, copy_to(core, lambda t: AB[:, t, :]), then=dn_quads(0))
    qkv_ready = stream(core, "dn_in", 3 * DH * HD // CH, dn_quads, lambda i, then: project(
        core, dn_quads(i), take(QKV, i), then=then), z_quads(0))
    for e in (pool, dve, pe, act):
        e.wait(qkv_ready, ab_ready)
        e.wait(core.tp_taken.now())
    o_ready = deltanet(core, a, QKV, AB, Z, ab_ready, DN)
    O, SQ = Z, cut(core, core.arena, 0, [TB, DH * HD])[0]
    ZG = core.TMP[:, :].rearrange("p (t w) -> p t w", t=TB)
    act.after(pe, dve, pool)
    act.wait(o_ready)
    z_ready = stream(core, "z_in", 2, z_quads, lambda i, then: project(core, z_quads(i), take(ZG, i), then=then), q_quads(0))
    act.wait(z_ready)
    act.did(nc.scalar.activation(SQ, O, ACT.Square))
    dve.after(act)
    dve.did(nc.vector.tensor_reduce(core.ss[:, 0:16], SQ.rearrange("p t (h w) -> p (t h) w", w=HD), AX.X, ALU.add))
    rstd(core, core.ss[:, 0:16], core.rs[:, 0:16], HD, dve.line.now())
    o16 = O.rearrange("p t (h w) -> p (t h) w", w=HD)
    dve.sync()
    dve.did(nc.vector.tensor_tensor(o16, o16, core.rs[:, 0:16].unsqueeze(2).to_broadcast([P, 16, HD]), ALU.mult))
    nc.gpsimd.wait_ge(dve.line.sem, dve.line.now().value())
    g = core.late.tick(nc.gpsimd.dma_start(SQ[:, 0, 0:HD], a["dn_norm_w_2"][0].partition_broadcast(P)))
    dve.wait(g)
    dve.sync()
    dve.did(nc.vector.tensor_tensor(o16, o16, SQ[:, 0, 0:HD].unsqueeze(1).to_broadcast([P, 16, HD]), ALU.mult))
    act.did(nc.scalar.activation(ZG, ZG, ACT.Silu))
    dve.after(act)
    dve.sync()
    dn_out = dve.did(nc.vector.tensor_tensor(Z, O, ZG, ALU.mult))
    act.after(dve)
    stream(core, "q_in", 2, q_quads, lambda i, then: project(core, q_quads(i), take(Q2, i), then=then), kv_quads(0))
    act.after(dve, pe)
    q_ready = stream(core, "kv_in", 3, kv_quads, lambda i, then: project(core, kv_quads(i), take(KV, i), then=then), mg_quads(0))
    W1 = cut(core, core.arena, 0, [32, HD])[0]
    CW = own(2 * (HD + 32)).rearrange("p (j w) -> p j w", j=2)
    MC = own(TB * HQ * PADC + HQ + TB)
    KS, BD = own(4 * T).rearrange("p (j t) -> p j t", j=4), own(2 * HQ * HD).rearrange("p (g h d) -> p g h d", g=2, h=HQ)
    KC = own(4 * T).rearrange("p (j t) -> p j t", j=4)
    nc.gpsimd.wait_ge(dve.line.sem, dve.line.now().value())
    nc.gpsimd.wait_ge(pe.line.sem, pe.line.now().value())
    nc.gpsimd.wait_ge(act.line.sem, act.line.now().value())
    w1_ready = core.late.tick(nc.gpsimd.dma_start(W1, a["cmp_w1_k_2"][0].rearrange("(i d) e -> d i e", d=HD)))
    for j, n in enumerate("kv"):
        core.late.tick(nc.gpsimd.dma_start(CW[:, j, 0:HD], a[f"cmp_w2_{n}_2"][0]))
        core.late.tick(nc.gpsimd.dma_start(CW[:, j, HD:], a[f"cmp_pe_{n}_2"]))
    cmp_ready = core.late.tick(nc.gpsimd.dma_start(MC, a["cmp_masks"]))
    cmp_mask = MC[:, 0:TB * HQ * PADC].rearrange("p (t n) -> p t n", t=TB)
    head_of, any_valid = MC[:, TB * HQ * PADC:TB * HQ * PADC + HQ], MC[:, TB * HQ * PADC + HQ:]
    heads = lambda ap: ap.rearrange("p t (h w) -> p t h w", w=HD)
    rope(core, heads(Q2), heads(Q2), core.cos, core.sin, N2, HD, core.TMP, q_ready)
    for kind in (0, 2, 4):
        mine = KV[:, :, kind * 2 * HD:(kind + 1) * 2 * HD]
        dve.sync()
        rope(core, heads(mine), heads(mine), core.cos, core.sin, 2, HD, core.TMP, None)
    att = core.att
    for n, (dst, kinds) in enumerate(((KC, (0, 1)), (KS, (2, 4)))):
        for j, kind in enumerate(kinds):
            pe.after(dve)
            pe.wait(core.tp_taken.now())
            for h in range(2):
                for t in range(TB):
                    c = (kind * 2 + h) * HD
                    ins = nc.tensor.transpose(core.TP[j][:, (2 * h + t) * P:(2 * h + t + 1) * P], KV[:, t, c:c + HD], core.ident)
            act.wait(pe.did(ins))
            core.tp_taken.tick(nc.scalar.activation(dst[:, 2 * j:2 * j + 2, :].rearrange("p h t -> p (h t)"), core.TP[j][:, :], ACT.Copy))
    BL = core.TMP[:, 0:32 * 2 * NC2].rearrange("p (i c) -> p i c", i=32)
    H1 = [att.LG[j][:, 0:2 * NC2] for j in range(2)]
    KCT, GV4 = att.PR[0][:, 0:2 * PADC], att.PR[1][:, 0:2 * P]
    dve.wait(cmp_ready, core.tp_taken.now())
    act.wait(cmp_ready)
    pe.wait(cmp_ready)
    for j in range(2):
        dve.after(pe)
        for h in range(2):
            x = KC[:, 2 * j + h, :]
            for half in range(2):
                rows = x[:, 16 * half:16 * half + 16 * NC2].rearrange("p (c i) -> p i c", i=16)
                pe_rows = CW[:, j, HD + 16 * half:HD + 16 * half + 16].unsqueeze(2).to_broadcast([P, 16, NC2])
                dve.did(nc.vector.tensor_tensor(BL[:, 16 * half:16 * half + 16, h * NC2:(h + 1) * NC2], rows, pe_rows, ALU.add))
        pe.after(dve)
        for i in range(32):
            ins = nc.tensor.matmul(core.SC[j][:, 0:2 * NC2], W1[:, i, :], BL[:, i, :], start=i == 0, stop=i == 31)
        act.wait(pe.did(ins))
        if j == 0:
            nc.gpsimd.wait_ge(pe.line.sem, pe.line.now().value())
            w1_ready = core.late.tick(nc.gpsimd.dma_start(W1, a["cmp_w1_v_2"][0].rearrange("(i d) e -> d i e", d=HD)))
            pe.wait(w1_ready)
        act.did(nc.scalar.activation(H1[j], core.SC[j][:, 0:2 * NC2], ACT.Gelu_apprx_tanh))
    dve.did(nc.vector.memset(KCT, 0.0))
    dve.did(nc.vector.memset(GV4, 0.0))
    dve.sync()
    dve.after(act)
    for g in range(2):
        for h in range(HQ):
            c = g * P + h * PADC
            dve.did(nc.vector.tensor_copy(GV4[:, c:c + NC2], H1[1][:, g * NC2:(g + 1) * NC2]))
    pe.after(act, dve)
    pe.did(nc.tensor.matmul(core.SC[0][:, 0:2 * NC2], CW[:, 0, 0:HD], H1[0], start=True, stop=True))
    for g in range(2):
        pe.did(nc.tensor.matmul(core.SC[1][:, g * HD:(g + 1) * HD], GV4[:, g * P:(g + 1) * P], CW[:, 1, 0:HD], start=True, stop=True))
    dve.after(pe)
    for g in range(2):
        dve.did(nc.vector.tensor_copy(KCT[:, g * PADC:g * PADC + NC2], core.SC[0][:, g * NC2:(g + 1) * NC2]))
        for h in range(HQ):
            dve.did(nc.vector.tensor_scalar(BD[:, g, h, :], core.SC[1][:, g * HD:(g + 1) * HD], head_of[:, h:h + 1], None, ALU.mult))
    act.did(nc.scalar.activation(GT[:, :, :], GT[:, :, :], ACT.Sigmoid))
    gates = GT[:, :, :].rearrange("p t (h b) -> p t h b", b=3)
    GB = own(3 * TB * N2).rearrange("p (b t h) -> p b t h", b=3, t=TB)
    dve.after(act)
    for b in range(3):
        dve.did(nc.vector.tensor_copy(GB[:, b], gates[:, :, :, b]))
    O = core.TMP[:, :].rearrange("p (t w) -> p t w", t=TB)
    GBS = own(TB * HQ).rearrange("p (t h) -> p t h", t=TB)
    CP, CS = att.LG[0][:, 0:TB * P].rearrange("p (t n) -> p t n", t=TB), own(TB * HQ)
    CPT = att.LG[1][:, 0:TB * P].rearrange("p (t n) -> p t n", t=TB)
    pool.after(dve, act)
    act.after(dve)
    pe.after(dve)
    with prog.turns("compressed", 2) as g:
        q_ready, _ = group_queries(core, Q2[:, :, bass.ds(g * CH, CH)])
        pe.wait(q_ready)
        pe.after(dve)
        for t in range(TB):
            for h in range(HQ):
                c = (t * HQ + h) * PADC
                ins = nc.tensor.matmul(core.SC[0][:, c:c + PADC], att.QT[:, h, t * P:(t + 1) * P], KCT[:, bass.ds(g * PADC, PADC)], start=True, stop=True)
        att.qt_taken.tick(ins)
        dve.wait(att.qt_taken.now())
        dve.after(act, pe)
        dve.did(nc.vector.scalar_tensor_tensor(CP[:, :, :], core.SC[0][:, 0:TB * HQ * PADC].rearrange("p (t n) -> p t n", t=TB), HD ** -0.5, cmp_mask, ALU.mult, ALU.add))
        dve.sync()
        cp = CP[:, :, :].rearrange("p t (h c) -> p (t h) c", c=PADC)
        wide = lambda s: s.unsqueeze(2).to_broadcast([P, TB * HQ, PADC])
        dve.did(nc.vector.tensor_reduce(CS, cp, AX.X, ALU.max))
        dve.sync()
        dve.did(nc.vector.tensor_tensor(cp, cp, wide(CS), ALU.subtract))
        act.after(dve)
        act.did(nc.scalar.activation(CP[:, :, :], CP[:, :, :], ACT.Exp))
        dve.after(act)
        dve.did(nc.vector.tensor_reduce(CS, cp, AX.X, ALU.add))
        dve.sync()
        dve.did(nc.vector.reciprocal(CS, CS))
        dve.did(nc.vector.tensor_copy(GBS[:, :, :], GB[:, 0, :, bass.ds(g * HQ, HQ)]))
        dve.sync()
        for t in range(TB):
            dve.did(nc.vector.scalar_tensor_tensor(CS[:, t * HQ:(t + 1) * HQ], CS[:, t * HQ:(t + 1) * HQ], any_valid[:, t:t + 1], GBS[:, t, :], ALU.mult, ALU.mult))
        dve.sync()
        dve.did(nc.vector.tensor_tensor(cp, cp, wide(CS), ALU.mult))
        pe.after(dve)
        pe.wait(core.tp_taken.now())
        for t in range(TB):
            ins = nc.tensor.transpose(core.TP[0][:, t * P:(t + 1) * P], CP[:, t, :], core.ident)
        act.wait(pe.did(ins))
        core.tp_taken.tick(nc.scalar.activation(CPT[:, :, :].rearrange("p t n -> p (t n)"), core.TP[0][:, 0:T], ACT.Copy))
        pe.wait(core.tp_taken.now())
        pe.after(act)
        for t in range(TB):
            pe.did(nc.tensor.matmul(core.PV[t][:, :], CPT[:, t, :], BD[:, bass.ds(g, 1), :, :].rearrange("p a h d -> p (a h d)"), start=True, stop=True))
            act.after(pe)
            act.constant_wait()
            act.did(nc.scalar.activation(O[:, t, bass.ds(g * CH, CH)], core.PV[t][:, :], ACT.Copy))
    dve.after(act, pe)
    dve.wait(core.tp_taken.now())
    for b, kind in ((1, 3), (2, 5)):
        def branch(g, then):
            kt = lambda t0, n: KS[:, bass.ds(2 * (b - 1) + g, 1), t0:t0 + n].rearrange("p a n -> p (a n)")
            vt = lambda t: KV[:, t, bass.ds(kind * 2 * HD + g * HD, HD)]
            dve.wait(att.pv_taken.now())
            dve.did(nc.vector.tensor_copy(GBS[:, :, :], GB[:, b, :, bass.ds(g * HQ, HQ)]))

            def add_to(h, pv, multiplied, sum_ready, src_read):
                dve.wait(multiplied, sum_ready)
                for t in range(TB):
                    dve.did(nc.vector.tensor_tensor(att.SUM[:, h, t:t + 1], att.SUM[:, h, t:t + 1], GBS[:, t, h:h + 1], ALU.mult))
                dve.sync()
                for t in range(TB):
                    o = O[:, t, bass.ds(g * CH + h * HD, HD)]
                    ins = nc.vector.scalar_tensor_tensor(o, pv[:, t * HD:(t + 1) * HD], att.SUM[:, h, t:t + 1], o, ALU.mult, ALU.add)
                    p = att.pv_taken.tick(ins) if t else dve.did(ins)
                return p
            between = attend(core, Q2[:, :, bass.ds(g * CH, CH)], kt, vt, core.causal, add_to)
            m = 2 * (b - 1) + g
            return project(core, mg_quads(m), take(MG0, m), then=then, between=between)
        for g in range(2):
            branch(g, mg_quads(2 * (b - 1) + g + 1))
    act.wait(att.pv_taken.now(), att.qt_taken.now(), att.qr_taken.now(), att.pt_taken.now())
    up0, up1 = (lambda c, w=w: quads_of(w, c * CH, 2) for w in (a["w_up_nsa_2"][0], a["w_up_dn_2"][0]))
    mg = stream(core, "merge_in", 4, lambda c: mg_quads(c + 4), lambda i, then: project(
        core, mg_quads(i + 4), take(MG1, i), then=then), up0(0))
    act.wait(mg)
    for m in (MG0, MG1):
        for t in range(TB):
            act.did(nc.scalar.activation(m[:, t, :], m[:, t, :], ACT.Sigmoid))
    turn(core, O, ready=att.pv_taken.now(), k_tiles=8)
    x_ready = turn(core, Z, ready=dn_out, k_tiles=8, k0=8)
    pe.wait(x_ready[-1])
    dve.after(act)

    def up(i, then):
        g0 = lambda t: MG0[:, t, bass.ds(i * CH, CH)]
        g1 = lambda t: MG1[:, t, bass.ds(i * CH, CH)]
        gated0 = lambda t, acc: nc.vector.tensor_tensor(g0(t), acc, g0(t), ALU.mult)
        gated1 = lambda t, acc: nc.vector.tensor_tensor(g1(t), acc, g1(t), ALU.mult)
        project(core, up0(i), (dve, gated0), then=up1(i))
        project(core, up1(i), (dve, gated1), then=then, k0=8)
        dve.wait(core.acc_taken.now())
        for t in range(TB):
            dve.did(nc.vector.tensor_tensor(g0(t), g0(t), g1(t), ALU.add))
    stream(core, "up", D // CH, up0, up, quads_of(a["w_o_2"][0], 0))
    x_ready = turn(core, MG0, ready=dve.line.now())
    return add_projection(core, "w_o", a["w_o_2"][0], x_ready, quads_of(a["w_ffn_gate_2"][0], 0))


def feed_forward(core, a, stop):
    nc, prog = core.nc, core.prog
    pe, act, dve = prog.pe, prog.act, prog.dve
    for e in (act, dve):
        e.after(pe, act, dve, prog.pool)
        e.wait(core.x_ready)
    SG, H = core.sb("SG", [P, TB, CH]), core.sb("H", [P, TB, D])
    hid = [core.sb(n, [P, KT_D, T], F32R) for n in ("HH", "HL")]
    x_ready = token_norm(core, core.gains[:, 3, :], H, core.x_ready)
    done = 0
    gate_quads, up_quads = (lambda c, w=a[n][0]: quads_of(w, c * CH) for n in ("w_ffn_gate_2", "w_ffn_up_2"))
    down = a["w_ffn_down_2"][0]
    pe.wait(x_ready[-1])
    for part, n in enumerate((4, 4, 3)):
        def hidden(i, then):
            silu = lambda t, acc: nc.scalar.activation(SG[:, t, :], acc, ACT.Silu)
            product = lambda t, acc: nc.vector.tensor_tensor(H[:, t, bass.ds(i * CH, CH)], acc, SG[:, t, :], ALU.mult)
            act.wait(core.acc_taken.now())
            project(core, gate_quads(done + i), (act, silu), then=up_quads(done + i))
            dve.wait(core.acc_taken.now())
            return project(core, up_quads(done + i), (dve, product), then=then)
        act.after(pe)
        h_ready = stream(core, f"ff{part}", n, lambda c: gate_quads(done + c), hidden, quads_of(down, 0, n, row0=done * CH))
        ready = turn(core, H, ready=h_ready, k_tiles=n * QK, xs=hid)
        add_projection(core, f"down{part}", down, ready, gate_quads(done + n) if part < 2 else (), n, done * CH, hid)
        done += n
    if stop == "d":
        return
    nc.gpsimd.wait_ge(dve.line.sem, dve.line.now().value())
    nc.gpsimd.wait_ge(core.acc_taken.sem, core.acc_taken.now().value())
    nc.gpsimd.wait_ge(core.tp_taken.sem, core.tp_taken.now().value())
    gain = H[:, 0, :]
    here = core.late.tick(nc.gpsimd.dma_start(gain, a["norm_f_w_2"].partition_broadcast(P)))
    act.wait(core.x_ready)
    act.after(dve)
    for t in range(TB):
        act.did(nc.scalar.activation(hid[0][:, :, :].rearrange("p k t -> p (k t)")[:, t * D:(t + 1) * D], core.X[:, t, :], ACT.Square, accum_out=core.ss[:, t:t + 1]))
    rstd(core, core.ss[:, 0:TB], core.rs[:, 0:TB], D, act.line.now())
    dve.wait(here, core.x_ready)
    dve.sync()
    for t in range(TB):
        core.x_ready = dve.did(nc.vector.scalar_tensor_tensor(core.X[:, t, :], core.X[:, t, :], core.rs[:, t:t + 1], gain, ALU.mult, ALU.mult))


A_COLS = (0, 2560, 3072)
INDEX_COL = 5120


def program(nc, counts, a, out, stop=None):
    with ExitStack() as ctx:
        prog = Prog(nc, counts, ctx)
        core = memory(nc, prog)
        core.x_landed = Line(prog, "x_landed", 16)
        x_src, x_dst = a["x"], out
        for t in range(TB):
            core.x_ready = core.x_landed.tick(nc.sync.dma_start(core.X[:, t, :], x_src[0, t * P:(t + 1) * P, :]))
        core.small.tick(nc.scalar.dma_start(core.consts[:, :], a["consts"]))
        core.small.tick(nc.scalar.dma_start(core.gains[:, :, :], a["norm_gains"]))
        QKG = core.QKG
        p = core.small.tick(nc.scalar.dma_start(QKG[:, :], a["a_qk_gains"].partition_broadcast(P)))
        for e in (prog.pe, prog.act, prog.dve):
            e.wait(p)
        attention_layer(core, "a", a["a_w_in"][0], a["a_w_out"][0], core.gains[:, 0, :], QKG, A_COLS,
                        quads_of(a["b_w_in"][0], A_COLS[0]) if stop != "a" else (), indexer)
        if stop != "a":
            nc.gpsimd.wait_ge(prog.dve.line.sem, prog.dve.line.now().value())
            p = core.late.tick(nc.gpsimd.dma_start(QKG[:, :], a["b_qk_gains"].partition_broadcast(P)))
            prog.dve.wait(p)
            attention_layer(core, "b", a["b_w_in"][0], a["b_w_out"][0], core.gains[:, 1, :], QKG, A_COLS,
                            quads_of(a["w_in_2"][0], GATE_COL, width=3 * N2) if stop != "b" else ())
        if stop not in ("a", "b"):
            third_layer(core, a, stop)
        core.mixers.close()
        if stop not in ("a", "b", "c"):
            feed_forward(core, a, stop)
        nc.sync.wait_ge(core.x_ready.line.sem, core.x_ready.value())
        stored = Line(prog, "x_stored", 16)
        for t in range(TB):
            stored.tick(nc.sync.dma_start(x_dst[0, t * P:(t + 1) * P, :], core.X[:, t, :]))
        nc.sync.wait_ge(stored.sem, stored.now().value())
    return prog.seen


def laid_out(inputs):
    a = {n: np.ascontiguousarray(v) for n, v in inputs.items()}
    cols = lambda v: v.reshape(KT_D, P).T
    out = {n: a[n] for n in ("x", "a_w_in", "a_w_out", "b_w_in", "b_w_out")}
    out["consts"] = shape_constants()
    out["norm_gains"] = np.ascontiguousarray(np.stack([cols(a[n]) for n in ("a_norm", "b_norm", "norm1_w_2", "norm2_w_2")], 1))
    for n in ("w_in_2", "w_up_nsa_2", "w_up_dn_2", "w_o_2", "w_ffn_gate_2", "w_ffn_up_2", "w_ffn_down_2", "dt_bias_2", "a_log_2",
              "dn_norm_w_2", "cmp_w1_k_2", "cmp_w1_v_2", "cmp_w2_k_2", "cmp_w2_v_2", "norm_f_w_2"):
        out[n] = a[n]
    for n in ("cmp_pe_k_2", "cmp_pe_v_2"):
        out[n] = np.ascontiguousarray(a[n][0].T)
    out["dn_conv"] = np.ascontiguousarray(a["conv_w_2"][0, :, 0, :].reshape(4, 24, P).transpose(2, 1, 0).reshape(P, 96))
    out["dn_consts"], out["cmp_masks"] = more_constants()
    for l in ("a", "b"):
        out[l + "_qk_gains"] = np.concatenate([a[l + "_q_norm"][0]] * (NH // GRP) + [a[l + "_k_norm"][0]])
    return out


def kernel(**inputs):
    import concourse.bacc as bacc
    from concourse.bass_utils import run_bass_kernel_spmd
    arrays = laid_out(inputs)
    counts = {}
    for _ in range(2):
        nc = bacc.Bacc("TRN2", target_bir_lowering=False, num_devices=1)
        a = {n: nc.dram_tensor("in_" + n, v.shape, F32, kind="ExternalInput").ap() for n, v in arrays.items()}
        out = nc.dram_tensor("out_0", (1, T, D), F32, kind="ExternalOutput").ap()
        counts = program(nc, counts, a, out)
    r = run_bass_kernel_spmd(nc, [{"in_" + n: v for n, v in arrays.items()}], core_ids=[0])
    return r.results[0]["out_0"]
```

```python
from contextlib import contextmanager, ExitStack

import numpy as np
import concourse.bass as bass
from concourse import mybir

F32 = mybir.dt.float32
F32R = mybir.dt.float32r
ALU = mybir.AluOpType
ACT = mybir.ActivationFunctionType
AX = mybir.AxisListType

P = 128
T = 256
TB = T // P
D = 2048
KT_D = D // P
CH = 512
QK = 4
NH, NKV, HD = 16, 4, 128
GRP = NH // NKV
IH, ID = 16, 64
KEEP = min(256, T // 4)
EPS = 1e-6
NEG = -1e30
REMOVED = -3e38
CREDIT = 4096

N2, NG2 = 8, 4
NC2 = (T - 32) // 16 + 1
DH, DC = 8, 64
PH = 2
F_FF = 5632


ARENA = 15400

CONSTS = {"identity": P, "causal": 3 * P, "cos": TB * HD, "sin": TB * HD, "cos_index": TB * ID, "sin_index": TB * ID}
CONST_AT, CONST_COLS = {}, 0
for _name, _n in CONSTS.items():
    CONST_AT[_name] = (CONST_COLS, CONST_COLS + _n)
    CONST_COLS += _n


def shape_constants():
    out = {"identity": np.eye(P)}
    q, s = np.arange(P)[:, None], np.arange(T)[None, :]
    out["causal"] = np.concatenate([np.where(s[:, :P] <= q, 0, NEG), np.where(s <= q + P, 0, NEG)], 1)
    for name, w in (("", HD), ("_index", ID)):
        inv = np.float32(10000.0) ** (-np.arange(0, w, 2, dtype=np.float32) / np.float32(w))
        ang = np.arange(T, dtype=np.float32)[:, None] * inv[None, :]
        blocks = lambda a: a.reshape(TB, P, w).transpose(1, 0, 2).reshape(P, TB * w)
        out["cos" + name] = blocks(np.concatenate([np.cos(ang), np.cos(ang)], 1))
        out["sin" + name] = blocks(np.concatenate([-np.sin(ang), np.sin(ang)], 1))
    return np.concatenate([out[n].astype(np.float32) for n in CONSTS], 1)


def more_constants():
    j, i = np.arange(P)[:, None], np.arange(P)[None, :]
    same = (j // DC == i // DC)
    levels = []
    for level in range(LEVELS):
        b = 1 << level
        levels.append((j // (2 * b) == i // (2 * b)) & (j % (2 * b) >= b) & (i % (2 * b) < b))
    dn = [np.ones((P, P)), same & (j <= i), same, np.where(same & (i <= j), 0, NEG)] + levels
    q, c = np.arange(T), np.arange(PADC)
    seen = (c[None, :] < NC2) & (16 * c[None, :] + 31 <= q[:, None])
    bias = np.tile(np.where(seen, 0, NEG), (1, HQ)).reshape(TB, P, HQ * PADC).transpose(1, 0, 2).reshape(P, -1)
    head_of = np.arange(P)[:, None] // PADC == np.arange(HQ)[None, :]
    some = seen.any(1).reshape(TB, P).T
    return (np.concatenate(dn, 1).astype(np.float32), np.concatenate([bias, head_of, some], 1).astype(np.float32))


class Names:
    pass


class Line:

    def __init__(self, prog, name, by=1, credit=CREDIT):
        self.prog, self.name, self.by, self.credit = prog, name, by, credit
        self.sem = prog.ctx.enter_context(prog.nc.semaphore(name))
        self.total = self.local = 0
        prog.lines.append(self)
        if credit:
            prog.nc.sync.sem_inc(self.sem, credit)

    def tick(self, ins):
        ins.then_inc(self.sem, self.by)
        self.local += 1
        return self.now()

    def now(self, back=0):
        return Point(self, self.local - back, self.total, self.prog.loop)


class Point:
    def __init__(self, line, local, start, loop):
        self.line, self.local, self.start, self.loop = line, local, start, loop

    def value(self):
        line, prog = self.line, self.line.prog
        if self.loop is None:
            return (self.start + self.local) * line.by + line.credit
        per = self.loop.counts.get(line.name, 0)
        if prog.loop is self.loop:
            v = (self.start + self.local) * line.by + line.credit
            return v if per == 0 else self.loop.reg * (per * line.by) + v
        return (self.start + (self.loop.turns - 1) * per + self.local) * line.by + line.credit


class Loop:
    def __init__(self, reg, turns, counts):
        self.reg, self.turns, self.counts = reg, turns, counts


class Prog:

    def __init__(self, nc, counts, ctx):
        self.nc, self.counts, self.ctx = nc, counts, ctx
        self.lines, self.loop, self.seen = [], None, {}
        self.pe, self.act, self.dve = Eng(self, nc.tensor, "pe"), Eng(self, nc.scalar, "act"), Eng(self, nc.vector, "dve")
        self.pool = Eng(self, nc.gpsimd, "pool")

    @contextmanager
    def turns(self, name, n):
        for line in self.lines:
            line.total, line.local = line.total + line.local, 0
        counts = self.counts.get(name, {})
        with self.nc.Fori(0, n) as i:
            self.loop = Loop(i, n, counts)
            yield i
            self.loop = None
        self.seen[name] = {line.name: line.local for line in self.lines}
        for line in self.lines:
            line.total, line.local = line.total + n * line.local, 0


class Eng:

    def __init__(self, prog, raw, name):
        self.prog, self.raw, self.name = prog, raw, name
        self.line = Line(prog, name + "_done")
        self.held = 0

    def wait(self, *points):
        for p in points:
            if p is not None:
                self.raw.wait_ge(p.line.sem, p.value())

    def after(self, *engines):
        self.wait(*(e.line.now() for e in engines))

    def sync(self):
        self.wait(self.line.now())

    def constant_wait(self):
        if self.prog.loop:
            self.held += 1
            assert self.held < CREDIT
            self.raw.wait_ge(self.line.sem, self.held)

    def did(self, ins):
        return self.line.tick(ins)


def memory(nc, prog):
    core = Names()
    core.nc, core.prog = nc, prog
    sb = lambda name, shape, dt=F32: prog.ctx.enter_context(nc.sbuf_tensor(name, shape, dt))
    core.sb = sb
    core.X = sb("X", [P, TB, D])
    core.XH = sb("XH", [P, KT_D, T], F32R)
    core.XL = sb("XL", [P, KT_D, T], F32R)
    core.W = [sb(f"W{i}", [P, QK, CH]) for i in range(4)]
    core.WH = [sb(f"WH{i}", [P, QK, CH], F32R) for i in range(2)]
    core.WL = [sb(f"WL{i}", [P, QK, CH], F32R) for i in range(2)]
    bank = lambda name: prog.ctx.enter_context(nc.psum_tensor(name, [P, CH], F32))
    core.ACC = [bank(f"ACC{t}") for t in range(TB)]
    core.TP = [bank(f"TP{i}") for i in range(2)]
    core.SC = [bank(f"SC{i}") for i in range(2)]
    core.PV = [bank(f"PV{i}") for i in range(2)]
    line = lambda name, by=1: Line(prog, name, by)
    core.landed = [line(f"weights_landed{i}", 16) for i in range(4)]
    core.hi_done, core.lo_done = line("weights_rounded"), line("weights_rest")
    core.quad_done, core.acc0_done = line("quad_multiplied"), line("block0_accumulated")
    core.acc_taken, core.tp_taken = line("accumulators_taken"), line("transposes_taken")
    core.free_slots = line("free_weight_slots")
    core.small = line("constants_landed", 16)
    core.late = Line(prog, "late_constants_landed", 16, 0)
    core.n_quad, core.pending = 0, []
    core.consts = sb("consts", [P, CONST_COLS])
    c = lambda n: core.consts[:, CONST_AT[n][0]:CONST_AT[n][1]]
    core.ident, core.causal = c("identity"), c("causal")
    by_block = lambda n: c(n).rearrange("p (t w) -> p t w", t=TB)
    core.cos, core.sin, core.cos_i, core.sin_i = by_block("cos"), by_block("sin"), by_block("cos_index"), by_block("sin_index")
    core.gains = sb("gains", [P, 4, KT_D])
    core.ss, core.rs = sb("sums_of_squares", [P, 64]), sb("reciprocal_roots", [P, 64])
    core.TMP = sb("TMP", [P, 2048])
    core.small_tables = sb("small_tables", [P, 8 * TB * DH])
    core.GT, core.AB = sb("GT", [P, TB, 3 * N2]), sb("AB", [P, TB, 2 * DH])
    core.QKG = sb("qk_gains", [P, (NH // GRP + 1) * HD])
    core.mixers = ExitStack()
    own = lambda name, shape: core.mixers.enter_context(nc.sbuf_tensor(name, shape, F32))
    core.arena, core.fixed = own("arena", [P, ARENA]), own("attention_memory", [P, 4760])
    core.at = core.fixed_at = 0
    core.att = attention_memory(core)
    return core


def cut(core, mem, at, shape):
    n = 1
    for d in shape:
        n *= d
    assert at + n <= mem.shape[1], (at + n, mem.shape)
    flat = mem[:, at:at + n]
    if len(shape) == 1:
        return flat, at + n
    names = "abc"[:len(shape)]
    return flat.rearrange(f"p ({' '.join(names)}) -> p {' '.join(names)}", **dict(zip(names, shape))), at + n


def arena(core, name, shape):
    view, core.at = cut(core, core.arena, core.at, shape)
    return view


def places(core, regions):
    left = [list(r) for r in regions]

    def own(cols):
        for r in left:
            if r[1] + cols <= r[2]:
                r[1] += cols
                return r[0][:, r[1] - cols:r[1]]
        raise ValueError("no place left")
    return own


def fixed(core, name, shape):
    view, core.fixed_at = cut(core, core.fixed, core.fixed_at, shape)
    return view




def quads_of(w, col, n=4, width=CH, row0=0):
    return [(w[row0 + q * QK * P:row0 + (q + 1) * QK * P, bass.ds(col, width)], width) for q in range(n)]


def load_and_round(core, rows, width):
    nc, act = core.nc, core.prog.act
    slot, half, ahead = core.n_quad % 4, core.n_quad % 2, len(core.pending)
    core.n_quad += 1
    nc.sync.wait_ge(core.lo_done.sem, core.lo_done.now(back=3).value())
    if core.prog.loop:
        nc.sync.sem_inc(core.free_slots.sem, 1)
    here = core.landed[slot].tick(nc.sync.dma_start(core.W[slot][:, :, 0:width], rows.rearrange("(k p) n -> p k n", p=P)))
    act.wait(here, core.quad_done.now(back=1 - ahead))
    core.hi_done.tick(nc.scalar.activation(core.WH[half][:, :, 0:width], core.W[slot][:, :, 0:width], ACT.Copy))
    core.pending.append((slot, half, width))


def subtract_rounded(core):
    nc, dve = core.nc, core.prog.dve
    slot, half, width = core.pending[-1]
    dve.wait(core.hi_done.now())
    core.lo_done.tick(nc.vector.tensor_tensor(core.WL[half][:, :, 0:width], core.W[slot][:, :, 0:width],
                                              core.WH[half][:, :, 0:width].bitcast(F32), ALU.subtract))


def prime(core, quads):
    for rows, width in quads[len(core.pending):2]:
        load_and_round(core, rows, width)
        subtract_rounded(core)


def multiply(core, k0, first, last, xs=None):
    nc, pe = core.nc, core.prog.pe
    pe.wait(core.lo_done.now(back=len(core.pending) - 1))
    slot, half, width = core.pending.pop(0)
    WH, WL = core.WH[half], core.WL[half]
    for t in range(TB):
        if first:
            pe.wait(core.acc_taken.now(back=1) if t == 0 else core.acc_taken.now())
        out = core.ACC[t][:, 0:width]
        for k in range(QK):
            hi_x, lo_x = (x[:, k0 + k, t * P:(t + 1) * P] for x in (xs or (core.XH, core.XL)))
            nc.tensor.matmul(out, hi_x, WH[:, k, 0:width], start=first and k == 0, stop=False)
            nc.tensor.matmul(out, hi_x, WL[:, k, 0:width], start=False, stop=False)
            mm = nc.tensor.matmul(out, lo_x, WH[:, k, 0:width], start=False, stop=last and k == QK - 1)
        if last and t == 0:
            core.acc0_done.tick(mm)
    core.quad_done.tick(mm)


def project(core, quads, take, then=(), between=None, x_ready=None, k0=0, xs=None):
    pe, n = core.prog.pe, len(quads)
    prime(core, quads)
    coming = list(quads[len(core.pending):]) + list(then[:2])
    for q in range(n):
        if x_ready:
            pe.wait(x_ready[q])
        multiply(core, k0 + q * QK, q == 0, q == n - 1, xs)
        if q == n - 1:
            for t in range(TB):
                eng, make = take() if callable(take) else take
                eng.wait(core.acc0_done.now() if t == 0 else core.quad_done.now())
                eng.constant_wait()
                core.acc_taken.tick(make(t, core.ACC[t][:, 0:quads[-1][1]]))
        if coming:
            load_and_round(core, *coming[0])
        if between:
            between(q)
        if coming:
            subtract_rounded(core)
            coming.pop(0)
    return core.acc_taken.now()


def stream(core, name, n, quads, body, then):
    prime(core, quads(0))
    if n > 2:
        with core.prog.turns(name, n - 1) as i:
            body(i, quads(i + 1))
    else:
        body(0, quads(1))
    return body(n - 1, then)


def copy_to(core, dst):
    return core.prog.act, lambda t, acc: core.nc.scalar.activation(dst(t), acc, ACT.Copy)




def rstd(core, ss, out, width, ready, eps=EPS):
    act, dve, nc = core.prog.act, core.prog.dve, core.nc
    dve.wait(ready)
    dve.did(nc.vector.tensor_scalar(out, ss, 1.0 / width, eps, ALU.mult, ALU.add))
    act.wait(dve.line.now())
    act.did(nc.scalar.activation(out, out, ACT.Sqrt))
    dve.wait(act.line.now())
    return dve.did(nc.vector.reciprocal(out, out))


def turn(core, src, gain=None, ready=None, k_tiles=KT_D, k0=0, xs=None, prepare=None):
    nc, pe, act, dve = core.nc, core.prog.pe, core.prog.act, core.prog.dve
    XH, XL = xs or (core.XH, core.XL)
    act.wait(core.quad_done.now())
    pe.wait(core.tp_taken.now(), ready)
    points, n_pieces = [], k_tiles * P // CH
    prepared = [prepare(0)] if prepare else []
    for j in range(k_tiles // 2):
        tp = core.TP[j % 2]
        if prepare and j % 2 == 0:
            pe.wait(prepared[j // 2])
            if j // 2 + 1 < n_pieces:
                prepared.append(prepare(j // 2 + 1))
        pe.wait(core.tp_taken.now(back=1))
        for k in range(2):
            for t in range(TB):
                c = (2 * j + k) * P
                ins = nc.tensor.transpose(tp[:, (2 * k + t) * P:(2 * k + t + 1) * P], src[:, t, c:c + P], core.ident)
        turned = pe.did(ins)
        act.wait(turned)
        parts = 1 if gain is None else 2
        piece = []
        for s in range(parts):
            n = 2 // parts
            k = k0 + 2 * j + s * n
            piece.append((tp[:, s * T:(s + n) * T], XH[:, k:k + n, :].rearrange("p k t -> p (k t)"),
                          XL[:, k:k + n, :].rearrange("p k t -> p (k t)"),
                          1.0 if gain is None else gain[:, 2 * j + s:2 * j + s + 1]))
        for ps, hi, lo, g in piece:
            rounded = act.did(nc.scalar.activation(hi, ps, ACT.Copy, scale=g))
        dve.wait(rounded)
        for s, (ps, hi, lo, g) in enumerate(piece):
            ins = nc.vector.scalar_tensor_tensor(lo, ps, g, hi.bitcast(F32), ALU.mult, ALU.subtract)
            done = core.tp_taken.tick(ins) if s == parts - 1 else dve.did(ins)
        points.append(done)
    return [points[min(len(points) - 1, 2 * q + 1)] for q in range((k_tiles + 3) // 4)]


def sums_of_squares(core, scratch, ready, first=0):
    nc, act, dve = core.nc, core.prog.act, core.prog.dve
    at = TB if first else 0
    for t in range(TB):
        act.wait(ready[t])
        p = act.did(nc.scalar.activation(scratch[:, t, first:D], core.X[:, t, first:D], ACT.Square, accum_out=core.ss[:, at + t:at + t + 1]))
    if first:
        dve.wait(p)
        p = dve.did(nc.vector.tensor_tensor(core.ss[:, 0:TB], core.ss[:, 0:TB], core.ss[:, TB:2 * TB], ALU.add))
    return p


def token_norm(core, gain, scratch):
    nc, act, dve = core.nc, core.prog.act, core.prog.dve
    p = sums_of_squares(core, scratch, core.x_ready, core.squared)
    act.wait(core.gains_ready)
    dve.wait(core.gains_ready)
    rstd(core, core.ss[:, 0:TB], core.rs[:, 0:TB], D, p)

    def scaled(c):
        cs = slice(c * CH, (c + 1) * CH)
        dve.sync()
        for t in range(TB):
            p = dve.did(nc.vector.tensor_scalar(scratch[:, t, cs], core.X[:, t, cs], core.rs[:, t:t + 1], None, ALU.mult))
        return p
    return turn(core, scratch, gain, prepare=scaled)


def rope(core, x, out, cos, sin, heads, width, tmp, ready):
    nc, dve = core.nc, core.prog.dve
    h = width // 2
    dve.wait(ready)
    for t in range(TB):
        tm = tmp[:, t * heads * width:(t + 1) * heads * width].rearrange("p (h w) -> p h w", h=heads)
        s1 = sin[:, t:t + 1, 0:h].to_broadcast([P, heads, h])
        s2 = sin[:, t:t + 1, h:width].to_broadcast([P, heads, h])
        c = cos[:, t:t + 1, :].to_broadcast([P, heads, width])
        dve.did(nc.vector.tensor_tensor(tm[:, :, 0:h], x[:, t, :, h:width], s1, ALU.mult))
        dve.did(nc.vector.tensor_tensor(tm[:, :, h:width], x[:, t, :, 0:h], s2, ALU.mult))
        dve.sync()
        dve.did(nc.vector.tensor_tensor(out[:, t], x[:, t], c, ALU.mult))
        dve.sync()
        p = dve.did(nc.vector.tensor_tensor(out[:, t], out[:, t], tm, ALU.add))
    return p


def attention_memory(core):
    F = lambda n, shape: fixed(core, n, shape)
    line = lambda n: Line(core.prog, n)
    att = Names()
    att.QR, att.QT = F("QR", [TB, GRP * HD]), F("QT", [GRP, T])
    att.LG = [F(f"LG{j}", [3 * P]) for j in range(2)]
    att.PR = [F(f"PR{j}", [3 * P]) for j in range(2)]
    att.PT = [F(f"PT{j}", [3 * P]) for j in range(2)]
    att.NM, att.SUM = F("NM", [GRP, TB]), F("SUM", [GRP, TB])
    att.qr_taken, att.qt_taken, att.sc_taken = line("qr_turned"), line("qt_multiplied"), line("scores_taken")
    att.pr_taken, att.pt_taken, att.pv_taken = line("probs_turned"), line("probs_multiplied"), line("outputs_taken")
    return att


def group_queries(core, q_src):
    nc, att, pe, act, pool = core.nc, core.att, core.prog.pe, core.prog.act, core.prog.pool
    pool.wait(att.qr_taken.now())
    here = pool.did(nc.gpsimd.tensor_copy(att.QR, q_src))
    pe.wait(here)
    for h2 in range(2):
        pe.wait(core.tp_taken.now(back=1))
        for h in range(2):
            for t in range(TB):
                c = (2 * h2 + h) * HD
                ins = nc.tensor.transpose(core.TP[h2][:, (2 * h + t) * P:(2 * h + t + 1) * P], att.QR[:, t, c:c + HD], core.ident)
        act.wait((att.qr_taken.tick(ins) if h2 else pe.did(ins)), att.qt_taken.now())
        done = core.tp_taken.tick(nc.scalar.activation(att.QT[:, 2 * h2:2 * h2 + 2, :].rearrange("p h t -> p (h t)"),
                                                       core.TP[h2][:, :], ACT.Copy))
    return done, here


def head_softmax(core, h, q_ready, kt, mask):
    nc, att, pe, act, dve = core.nc, core.att, core.prog.pe, core.prog.act, core.prog.dve
    LG, PR, sc = att.LG[h % 2], att.PR[h % 2], core.SC[h % 2]
    pe.wait(q_ready, att.sc_taken.now(back=1))
    nc.tensor.matmul(sc[:, 0:P], att.QT[:, h, 0:P], kt(0, P), start=True, stop=True)
    ins = nc.tensor.matmul(sc[:, P:3 * P], att.QT[:, h, P:T], kt(0, T), start=True, stop=True)
    scored = att.qt_taken.tick(ins) if h == GRP - 1 else pe.did(ins)
    dve.wait(scored, att.pr_taken.now(back=1))
    masked = att.sc_taken.tick(nc.vector.scalar_tensor_tensor(LG, sc[:, 0:3 * P], HD ** -0.5, mask, ALU.mult, ALU.add))
    dve.wait(masked, att.pv_taken.now(back=1))
    dve.did(nc.vector.tensor_reduce(att.NM[:, h, 0:1], LG[:, 0:P], AX.X, ALU.max, negate=True))
    top = dve.did(nc.vector.tensor_reduce(att.NM[:, h, 1:2], LG[:, P:3 * P], AX.X, ALU.max, negate=True))
    act.wait(top)
    act.did(nc.scalar.activation(PR[:, 0:P], LG[:, 0:P], ACT.Exp, bias=att.NM[:, h, 0:1], accum_out=att.SUM[:, h, 0:1]))
    return act.did(nc.scalar.activation(PR[:, P:3 * P], LG[:, P:3 * P], ACT.Exp, bias=att.NM[:, h, 1:2],
                                        accum_out=att.SUM[:, h, 1:2]))


def head_turn(core, h, exp_ready):
    nc, att, pe, act, dve = core.nc, core.att, core.prog.pe, core.prog.act, core.prog.dve
    tp = core.TP[h % 2]
    pe.wait(exp_ready, core.tp_taken.now(back=1))
    for b in range(3):
        ins = nc.tensor.transpose(tp[:, b * P:(b + 1) * P], att.PR[h % 2][:, b * P:(b + 1) * P], core.ident)
    act.wait(att.pr_taken.tick(ins), att.pt_taken.now(back=1))
    pt_ready = core.tp_taken.tick(nc.scalar.activation(att.PT[h % 2], tp[:, 0:3 * P], ACT.Copy))
    dve.wait(exp_ready)
    return pt_ready, dve.did(nc.vector.reciprocal(att.SUM[:, h, :], att.SUM[:, h, :]))


def head_outputs(core, h, pt_ready, sum_ready, src_read, vt, store):
    nc, att, pe = core.nc, core.att, core.prog.pe
    PT, pv = att.PT[h % 2], core.PV[h % 2]
    pe.wait(pt_ready, att.pv_taken.now(back=1))
    nc.tensor.matmul(pv[:, 0:HD], PT[:, 0:P], vt(0), start=True, stop=True)
    nc.tensor.matmul(pv[:, HD:2 * HD], PT[:, P:2 * P], vt(0), start=True, stop=False)
    ins = att.pt_taken.tick(nc.tensor.matmul(pv[:, HD:2 * HD], PT[:, 2 * P:3 * P], vt(1), start=False, stop=True))
    return store(h, pv, ins, sum_ready, src_read)


def attend(core, q_src, kt, vt, mask, store):
    q_ready, src_read = group_queries(core, q_src)
    exp_ready = head_softmax(core, 0, q_ready, kt, mask)
    held = {"exp": exp_ready}

    def between(q):
        turned = head_turn(core, q, held["exp"])
        if q + 1 < GRP:
            held["exp"] = head_softmax(core, q + 1, q_ready, kt, mask)
        if q >= 1:
            head_outputs(core, q - 1, *held["turned"], src_read, vt, store)
        if q == GRP - 1:
            head_outputs(core, q, *turned, src_read, vt, store)
        held["turned"] = turned
    return between


def attention_layer(core, name, w_in, w_out, gain, qk_gain, cols, then, index=None):
    nc, prog, att = core.nc, core.prog, core.att
    pe, act, dve, pool = prog.pe, prog.act, prog.dve, prog.pool
    core.at = 0
    Q = arena(core, "Q", [TB, (NH + NKV) * HD])
    V = arena(core, "V", [TB, NKV * HD])
    G = arena(core, "G", [TB, D])
    prime(core, quads_of(w_in, INDEX_COL if index else cols[0]))
    x_ready = token_norm(core, gain, G)
    core.prog.pe.wait(x_ready[-1])
    steps, begin_choice, end_choice = index(core, w_in, G, quads_of(w_in, cols[0])) if index else ([], None, None)
    C, last = att.QR, [None]

    def to_chunk(t, acc):
        return nc.scalar.activation(C[:, t, :], acc, ACT.Copy)

    def finish(chunk):
        rs = core.rs[:, 0:TB * GRP].unsqueeze(2).to_broadcast([P, TB * GRP, HD])
        flat = C.rearrange("p t (h w) -> p (t h) w", w=HD)
        mine = Q[:, :, bass.ds(chunk * CH, CH)]
        gain = qk_gain[:, bass.ds(chunk * HD, HD)].unsqueeze(1).to_broadcast([P, TB * GRP, HD])
        heads = lambda ap: ap.rearrange("p t (h w) -> p t h w", w=HD)

        def between(q):
            if q == 0:
                act.after(dve)
                act.wait(core.acc_taken.now())
                sq = act.did(nc.scalar.activation(core.TMP[:, 0:TB * CH].rearrange("p (t w) -> p t w", t=TB), C, ACT.Square))
                dve.wait(sq)
                s = dve.did(nc.vector.tensor_reduce(core.ss[:, 0:TB * GRP], core.TMP[:, 0:TB * CH].rearrange("p (h w) -> p h w", w=HD), AX.X, ALU.add))
                rstd(core, core.ss[:, 0:TB * GRP], core.rs[:, 0:TB * GRP], HD, s)
            if q == 1:
                dve.sync()
                dve.did(nc.vector.tensor_tensor(flat, flat, rs, ALU.mult))
                dve.sync()
                dve.did(nc.vector.tensor_tensor(flat, flat, gain, ALU.mult))
            if q == 2:
                last[0] = rope(core, heads(C), heads(mine), core.cos, core.sin, GRP, HD, core.TMP, dve.line.now())
        return between

    def take_chunk():
        act.after(dve)
        return act, to_chunk
    quads = lambda c: quads_of(w_in, cols[0] + c * CH)
    v_quads, g_quads = quads_of(w_in, cols[1]), lambda c: quads_of(w_in, cols[2] + c * CH)
    project(core, quads(0), (act, to_chunk), then=quads(1), between=lambda q: steps[q]() if steps else None)
    if index:
        begin_choice()
    stream(core, name + "_qk", NH // GRP, lambda c: quads(c + 1),
           lambda i, then: project(core, quads(i + 1), take_chunk, then=then, between=finish(i)), v_quads)
    v_ready = project(core, v_quads, copy_to(core, lambda t: V[:, t, :]), then=g_quads(0), between=finish(NH // GRP))
    roped = last[0]
    mask, mask_ready = end_choice() if index else (core.causal, None)
    KT = arena(core, "KT", [NKV, T])
    for j in range(2):
        pe.wait(roped, core.tp_taken.now(back=1))
        for h in range(2):
            for t in range(TB):
                c = NH * HD + (2 * j + h) * HD
                ins = nc.tensor.transpose(core.TP[j][:, (2 * h + t) * P:(2 * h + t + 1) * P], Q[:, t, c:c + HD], core.ident)
        act.wait(pe.did(ins))
        kt_ready = core.tp_taken.tick(nc.scalar.activation(KT[:, 2 * j:2 * j + 2, :].rearrange("p h t -> p (h t)"), core.TP[j][:, :], ACT.Copy))
    pe.wait(kt_ready, v_ready)
    pool.wait(roped)
    dve.wait(mask_ready)

    def attend_group(i, then):
        kt = lambda t0, n: KT[:, bass.ds(i, 1), t0:t0 + n].rearrange("p a n -> p (a n)")
        vt = lambda t: V[:, t, bass.ds(i * HD, HD)]
        out = lambda h, t: Q[:, t, bass.ds(i * CH + h * HD, HD)]

        def store(h, pv, multiplied, sum_ready, src_read):
            act.wait(multiplied, sum_ready, src_read)
            act.constant_wait()
            act.did(nc.scalar.activation(out(h, 0), pv[:, 0:HD], ACT.Copy, scale=att.SUM[:, h, 0:1]))
            return att.pv_taken.tick(nc.scalar.activation(out(h, 1), pv[:, HD:2 * HD], ACT.Copy, scale=att.SUM[:, h, 1:2]))
        between = attend(core, Q[:, :, bass.ds(i * CH, CH)], kt, vt, mask, store)
        return project(core, g_quads(i), copy_to(core, lambda t: G[:, t, bass.ds(i * CH, CH)]), then=then, between=between)
    gated = stream(core, name + "_attend", NKV, g_quads, attend_group, quads_of(w_out, 0))
    act.wait(gated, att.pv_taken.now())
    x_ready = turn_gated(core, G, Q, ACT.Silu)
    return add_projection(core, name + "_out", w_out, x_ready, then)


def turn_gated(core, G, O, func):
    nc, act, dve = core.nc, core.prog.act, core.prog.dve

    def gated(c):
        cs = slice(c * CH, (c + 1) * CH)
        p = act.did(nc.scalar.activation(G[:, :, cs], G[:, :, cs], func))
        dve.wait(p)
        return dve.did(nc.vector.tensor_tensor(O[:, :, cs], O[:, :, cs], G[:, :, cs], ALU.mult))
    return turn(core, O, prepare=gated)


def add_projection(core, name, w, x_ready, then, n_quads=4, row0=0, xs=None):
    nc, dve, pe, act = core.nc, core.prog.dve, core.prog.pe, core.prog.act
    quads = lambda c: quads_of(w, c * CH, n_quads, row0=row0)

    def squares(t):
        if t < TB:
            act.wait(core.acc_taken.now())
            act.after(dve, pe, act)
            act.did(nc.scalar.activation(core.TMP[:, 0:D - CH], core.X[:, t, 0:D - CH], ACT.Square, accum_out=core.ss[:, t:t + 1]))

    def add_chunk(i, then):
        def add(t, acc):
            mine = core.X[:, t, bass.ds(i * CH, CH)]
            return nc.vector.tensor_tensor(mine, acc, mine, ALU.add)
        return project(core, quads(i), (dve, add), then=then, xs=xs,
                       between=squares if type(i) is int and i == D // CH - 1 else None)
    prime(core, quads(0))
    pe.wait(x_ready[-1])
    if n_quads % 4 == 0:
        ready = stream(core, name, D // CH, quads, add_chunk, then)
    else:
        for c in range(D // CH):
            ready = add_chunk(c, quads(c + 1) if c + 1 < D // CH else then)
    core.x_ready, core.squared = [ready] * TB, D - CH
    return ready


def indexer(core, w_in, spare, then):
    nc, prog, att = core.nc, core.prog, core.att
    pe, act, dve = prog.pe, prog.act, prog.dve
    c0 = INDEX_COL
    QI, KW = arena(core, "QI", [TB, IH * ID]), arena(core, "KW", [TB, ID + IH])
    KI, WI, KIT = arena(core, "KI", [TB, 2 * ID]), arena(core, "WI", [TB, IH]), arena(core, "KIT", [T])
    REL, SCORE = att.LG + att.PT, att.PR[0]
    BANKS = core.SC + core.PV
    TOP, MASK = arena(core, "TOP", [TB, 8]), fixed(core, "MASK", [3 * P])
    QIT = spare[:, 0, :].rearrange("p (j t) -> p j t", t=T)
    quads, k_quads = lambda c: quads_of(w_in, c0 + c * CH), quads_of(w_in, c0 + IH * ID, width=ID + IH)
    heads = lambda ap, n: ap.rearrange("p t (h w) -> p t h w", h=n)
    in_chunk = CH // ID

    def project_queries(c, following, between=None):
        return project(core, quads(c), copy_to(core, lambda t: QI[:, t, c * CH:(c + 1) * CH]), then=following, between=between)

    def rope_chunk(c, ready):
        mine = heads(QI[:, :, c * CH:(c + 1) * CH], in_chunk)
        return rope(core, mine, mine, core.cos_i, core.sin_i, in_chunk, ID, core.TMP, ready)
    q0_here = project_queries(0, quads(1))
    q1_here = project_queries(1, k_quads, lambda q: rope_chunk(0, q0_here) if q == 0 else None)
    k_here = project(core, k_quads, copy_to(core, lambda t: KW[:, t, :]), then=then,
                     between=lambda q: rope_chunk(1, q1_here) if q == 0 else None)

    def turn_queries():
        roped = dve.line.now()
        rope(core, heads(KW[:, :, 0:ID], 1), heads(KI[:, :, 0:ID], 1), core.cos_i, core.sin_i, 1, ID, core.TMP, k_here)
        dve.sync()
        dve.did(nc.vector.tensor_copy(KI[:, :, ID:2 * ID], KI[:, :, 0:ID]))
        dve.did(nc.vector.tensor_scalar(WI[:, :, :], KW[:, :, ID:ID + IH], IH ** -0.5, None, ALU.mult))
        pe.wait(roped)
        for j in range(IH // 4):
            tp = core.TP[j % 2]
            pe.wait(core.tp_taken.now(back=1))
            for s in range(2):
                for t in range(TB):
                    c = (2 * j + s) * P
                    ins = nc.tensor.transpose(tp[:, (2 * s + t) * P:(2 * s + t + 1) * P], QI[:, t, c:c + P], core.ident)
            act.wait(pe.did(ins))
            core.tp_taken.tick(nc.scalar.activation(QIT[:, 2 * j:2 * j + 2, :].rearrange("p j t -> p (j t)"), tp[:, :], ACT.Copy))

    def turn_key():
        pe.after(dve)
        pe.wait(core.tp_taken.now(back=1))
        for t in range(TB):
            ins = nc.tensor.transpose(core.TP[0][:, t * P:(t + 1) * P], KI[:, t, :], core.ident)
        act.wait(pe.did(ins))
        core.tp_taken.tick(nc.scalar.activation(KIT, core.TP[0][:, 0:T], ACT.Copy))
        pe.wait(core.tp_taken.now())
    n_banks = len(BANKS)
    taken, summed = [None] * n_banks, [None] * n_banks

    def score(first, end):
        for h in range(first, end):
            b, half = h % n_banks, slice(ID * (h % 2), ID * (h % 2 + 1))
            sc = BANKS[b]
            pe.wait(taken[b])
            nc.tensor.matmul(sc[:, 0:P], QIT[half, h // 2, 0:P], KIT[half, 0:P], start=True, stop=True)
            scored = pe.did(nc.tensor.matmul(sc[:, P:3 * P], QIT[half, h // 2, P:T], KIT[half, :], start=True, stop=True))
            act.wait(scored, summed[b])
            taken[b] = act.did(nc.scalar.activation(REL[b], sc[:, 0:3 * P], ACT.Relu, scale=ID ** -0.5))
            dve.wait(taken[b])
            dve.sync()
            for t, cs in ((0, slice(0, P)), (1, slice(P, 3 * P))):
                w = WI[:, t, h:h + 1]
                if h == 0:
                    ins = nc.vector.tensor_scalar(SCORE[:, cs], REL[b][:, cs], w, None, ALU.mult)
                else:
                    ins = nc.vector.scalar_tensor_tensor(SCORE[:, cs], REL[b][:, cs], w, SCORE[:, cs], ALU.mult, ALU.add)
                summed[b] = dve.did(ins)

    def turn_key_and_score():
        turn_key()
        score(0, n_banks)

    def remove_largest(times):
        blocks = ((0, slice(0, P)), (1, slice(P, 3 * P)))
        for _ in range(times):
            dve.sync()
            for t, cs in blocks:
                dve.did(nc.vector.max(TOP[:, t, :], SCORE[:, cs]))
            dve.sync()
            for t, cs in blocks:
                dve.did(nc.vector.match_replace(SCORE[:, cs], TOP[:, t, :], SCORE[:, cs], REMOVED))
    times = KEEP // 8

    def begin_choice():
        pe.after(act)
        dve.sync()
        dve.did(nc.vector.tensor_tensor(SCORE, SCORE, core.causal, ALU.add))
        remove_largest(times // 2)

    def end_choice():
        remove_largest(times - times // 2)
        dve.sync()
        dve.did(nc.vector.tensor_scalar(MASK, SCORE, REMOVED / 2, NEG, ALU.is_gt, ALU.mult))
        dve.sync()
        return MASK, dve.did(nc.vector.tensor_tensor(MASK, MASK, core.causal, ALU.add))
    rest = (IH - n_banks) // 2
    return [turn_queries, turn_key_and_score, lambda: score(n_banks, n_banks + rest), lambda: score(n_banks + rest, IH)], begin_choice, end_choice


Q_COL, KV_COL, GATE_COL = 0, N2 * HD, N2 * HD + 6 * 2 * HD
DN_COL = GATE_COL + 3 * N2
Z_COL = DN_COL + 3 * DH * HD
AB_COL = Z_COL + DH * HD
MERGE_COL = AB_COL + 2 * DH
HQ = 4
LEVELS = 6
PADC = 32


def deltanet_gates(core, AB, ready, DN):
    nc, prog = core.nc, core.prog
    pe, act, dve = prog.pe, prog.act, prog.dve
    V, TT, TS, MM = nc.vector, nc.vector.tensor_tensor, nc.vector.tensor_scalar, nc.tensor.matmul
    tri, same = DN["tri"], DN["same"]
    G, B, GC, GL, E1, EG, EKD, BEG = (core.small_tables[:, n * TB * DH:(n + 1) * TB * DH] for n in range(8))
    by = lambda ap: ap.rearrange("p (t h) -> p t h", t=TB)
    dt = DN["dt"].unsqueeze(1).to_broadcast([P, TB, DH])

    def strengths():
        act.wait(DN["ready"])
        dve.wait(ready, DN["ready"])
        dve.did(TT(by(G), AB[:, :, 0:DH], dt, ALU.add))
        act.after(dve)
        act.did(nc.scalar.activation(E1, G, ACT.Abs))
        act.sync()
        act.did(nc.scalar.activation(E1, E1, ACT.Exp, scale=-1.0))
        dve.after(act)
        dve.did(TS(E1, E1, 1.0, None, ALU.add))
        act.after(dve)
        act.did(nc.scalar.activation(E1, E1, ACT.Ln))
        act.did(nc.scalar.activation(DN["alog"], DN["alog"], ACT.Exp))
        dve.after(act)
        dve.did(V.scalar_tensor_tensor(G, G, 0.0, E1, ALU.max, ALU.add))
        dve.sync()
        dve.did(TT(by(G), by(G), DN["alog"].unsqueeze(1).to_broadcast([P, TB, DH]), ALU.mult))
        dve.sync()
        dve.did(TS(G, G, -1.0, None, ALU.mult))
        act.did(nc.scalar.activation(by(B), AB[:, :, DH:2 * DH], ACT.Sigmoid))

    def sums():
        pe.after(dve)
        pe.wait(core.tp_taken.now())
        pe.did(MM(core.TP[0][:, 0:TB * DH], tri, G, start=True, stop=True))
        pe.did(MM(core.TP[0][:, TB * DH:2 * TB * DH], same, G, start=True, stop=True))
        act.after(pe)
        act.did(nc.scalar.activation(GC, core.TP[0][:, 0:TB * DH], ACT.Copy))
        act.did(nc.scalar.activation(GL, core.TP[0][:, TB * DH:2 * TB * DH], ACT.Copy))
        dve.after(act)
        dve.did(TT(EKD, GL, GC, ALU.subtract))
        act.after(dve)
        act.did(nc.scalar.activation(EKD, EKD, ACT.Exp))
        act.did(nc.scalar.activation(EG, GC, ACT.Exp))
        dve.after(act)
        dve.did(TT(BEG, B, EG, ALU.mult))
    return [strengths, sums], (GC, G, B, EKD, BEG)


def deltanet(core, a, QKV, tables, O, ready, DN):
    nc, prog = core.nc, core.prog
    pe, act, dve, pool = prog.pe, prog.act, prog.dve, prog.pool
    V, TT, TS, MM = nc.vector, nc.vector.tensor_tensor, nc.vector.tensor_scalar, nc.tensor.matmul
    pairs = lambda ap: ap.rearrange("p (h w) -> p h w", h=PH)
    flat = lambda ap: ap.rearrange("p h w -> p (h w)")
    over_heads = lambda m: m.unsqueeze(1).to_broadcast([P, PH, P])
    per_head = lambda s: s.unsqueeze(2).to_broadcast([P, PH, P])
    ones, tri, same, lower = DN["ones"], DN["tri"], DN["same"], DN["lower"]
    masks = DN["levels"].rearrange("p (l w) -> p l w", l=LEVELS)
    GC, G, B, EKD, BEG = tables
    by = lambda ap: ap.rearrange("p (t h) -> p t h", t=TB)
    dve.wait(ready)
    act.wait(ready)
    own = places(core, DN["memory"])
    STG = core.TMP[:, 0:TB * CH].rearrange("p (t w) -> p t w", t=TB)
    SQ = core.TMP[:, TB * CH:2 * TB * CH]
    YT = [own(HQ * T).rearrange("p (h t) -> p h t", h=HQ) for c in range(3)]
    m4 = {n: own(HQ * P).rearrange("p (h w) -> p h w", h=HQ) for n in "R D L S TI Y QD EGR KBG KD VB STATE".split()}
    m4.update(M=m4["R"], DT=m4["D"], VN=m4["L"], WT=m4["TI"], U=m4["Y"])
    cw4 = own(3 * HQ * 4).rearrange("p (c n) -> p c n", c=3)
    h4 = {n: own(TB * HQ).rearrange("p (t h) -> p t h", t=TB) for n in ("G", "B", "GC", "EKD", "BEG")}
    src = dict(G=G, B=B, GC=GC, EKD=EKD, BEG=BEG)

    def two_heads(i, s):
        last = {e.name: e.line.now() for e in (pe, act, dve, pool)}

        def did(e, ins):
            last[e.name] = e.did(ins)

        def after(e, *others):
            e.wait(*(last[o.name] for o in others))
        pair = slice(s * PH, (s + 1) * PH)
        TP, SC, PV, ACC = core.TP[s], core.SC[s], core.PV[s], core.ACC[s]
        lo, hi = slice(0, PH * P), slice(PH * P, 2 * PH * P)
        sq = SQ[:, s * CH:(s + 1) * CH]
        y3 = [y[:, pair, :] for y in YT]
        m = {n: v[:, pair, :] for n, v in m4.items()}
        small = {n: v[:, :, pair] for n, v in h4.items()}
        cw = cw4[:, :, s * PH * 4:(s + 1) * PH * 4]
        for c in range(3):
            stg = STG[:, :, s * PH * HD:(s + 1) * PH * HD]
            bank = (TP, ACC)[c % 2]
            after(pool, pe)
            did(pool, nc.gpsimd.tensor_copy(stg, QKV[:, :, bass.ds(i * CH + c * DH * HD + s * PH * HD, PH * HD)]))
            after(pe, pool, dve)
            for h in range(PH):
                for t in range(TB):
                    did(pe, nc.tensor.transpose(bank[:, (h * TB + t) * P:(h * TB + t + 1) * P], stg[:, t, h * HD:(h + 1) * HD], core.ident))
            yield
            after(dve, pe)
            tap = lambda h, back: cw[:, c, h * 4 + 3 - back:h * 4 + 4 - back]
            for back in range(4):
                if back:
                    after(dve, dve)
                for h in range(PH):
                    x, y = bank[:, h * T:(h + 1) * T], y3[c][:, h, :]
                    if back == 0:
                        did(dve, TS(y, x, tap(h, 0), None, ALU.mult))
                    else:
                        did(dve, V.scalar_tensor_tensor(y[:, back:T], x[:, 0:T - back], tap(h, back), y[:, back:T], ALU.mult, ALU.add))
            after(act, dve)
            did(act, nc.scalar.activation(flat(y3[c]), flat(y3[c]), ACT.Silu))
            yield
        for c in range(2):
            after(act, act, dve)
            did(act, nc.scalar.activation(sq, flat(y3[c]), ACT.Square))
            after(pe, act)
            did(pe, MM(SC[:, :], ones, sq, start=True, stop=True))
            yield
            after(dve, pe)
            did(dve, TS(sq, SC[:, :], EPS, None, ALU.add))
            after(act, dve)
            did(act, nc.scalar.activation(sq, sq, ACT.Sqrt))
            yield
            after(dve, act)
            did(dve, V.reciprocal(sq, sq))
            after(dve, dve)
            y = flat(y3[c])
            if c == 0:
                did(dve, V.scalar_tensor_tensor(y, y, HD ** -0.5, sq, ALU.mult, ALU.mult))
            else:
                did(dve, TT(y, y, sq, ALU.mult))
            yield
        did(dve, V.memset(m["STATE"], 0.0))
        for t in range(TB):
            block = lambda c, h: y3[c][:, h, t * P:(t + 1) * P]
            after(pe, dve, act)
            for h in range(PH):
                nc.tensor.transpose(TP[:, h * P:(h + 1) * P], block(1, h), core.ident)
                did(pe, nc.tensor.transpose(TP[:, (PH + h) * P:(PH + h + 1) * P], block(2, h), core.ident))
            did(dve, TT(m["R"], over_heads(tri), per_head(small["G"][:, t, :]), ALU.mult))
            after(dve, pe)
            after(pe, dve)
            did(pe, MM(SC[:, lo], ones, flat(m["R"]), start=True, stop=True))
            for h in range(PH):
                nc.tensor.matmul(PV[:, h * P:(h + 1) * P], block(1, h), block(1, h), start=True, stop=True)
            yield
            did(dve, TT(m["KBG"], pairs(TP[:, lo]), per_head(small["BEG"][:, t, :]), ALU.mult))
            did(dve, TT(m["KD"], pairs(TP[:, lo]), per_head(small["EKD"][:, t, :]), ALU.mult))
            did(dve, TT(m["VB"], pairs(TP[:, hi]), per_head(small["B"][:, t, :]), ALU.mult))
            after(act, pe)
            did(act, nc.scalar.activation(flat(m["EGR"]), SC[:, lo], ACT.Exp))
            yield
            after(dve, act)
            did(dve, TT(m["D"], over_heads(lower), pairs(SC[:, lo]), ALU.subtract))
            after(dve, dve)
            did(dve, TT(m["D"], m["D"], per_head(small["GC"][:, t, :]), ALU.add))
            after(act, dve)
            did(act, nc.scalar.activation(flat(m["D"]), flat(m["D"]), ACT.Exp))
            after(pe, dve)
            for h in range(PH):
                did(pe, MM(TP[:, (PH + h) * P:(PH + h + 1) * P], block(1, h), block(0, h), start=True, stop=True))
            yield
            after(dve, pe, act)
            did(dve, TT(m["L"], pairs(PV[:, lo]), m["D"], ALU.mult))
            did(dve, TT(m["QD"], y3[0][:, :, t * P:(t + 1) * P], m["EGR"], ALU.mult))
            after(dve, dve)
            did(dve, TT(m["L"], m["L"], per_head(small["B"][:, t, :]), ALU.mult))
            did(dve, V.tensor_copy(m["TI"], over_heads(core.ident)))
            did(dve, V.tensor_copy(m["S"], over_heads(core.ident)))
            after(pe, act)
            for h in range(PH):
                did(pe, nc.tensor.transpose(TP[:, h * P:(h + 1) * P], m["D"][:, h, :], core.ident))
            yield
            mask = lambda level: did(dve, TT(m["M"], m["L"], over_heads(masks[:, level, :]), ALU.mult))
            after(dve, dve)
            mask(0)
            after(act, pe, dve)
            did(act, nc.scalar.activation(flat(m["DT"]), TP[:, lo], ACT.Copy))
            for level in range(LEVELS):
                after(pe, dve)
                for h in range(PH):
                    did(pe, MM(SC[:, h * P:(h + 1) * P], m["M"][:, h, :], m["S"][:, h, :], start=True, stop=True))
                yield
                after(act, pe)
                did(act, nc.scalar.activation(flat(m["Y"]), SC[:, lo], ACT.Copy))
                after(dve, pe)
                if level == 0:
                    after(dve, act)
                    did(dve, TT(m["DT"], pairs(TP[:, hi]), m["DT"], ALU.mult))
                if level < LEVELS - 1:
                    mask(level + 1)
                after(pe, act)
                for h in range(PH):
                    did(pe, MM(PV[:, h * P:(h + 1) * P], m["TI"][:, h, :], m["Y"][:, h, :], start=True, stop=True))
                if level < LEVELS - 1:
                    for h in range(PH):
                        did(pe, MM(PV[:, (PH + h) * P:(PH + h + 1) * P], m["Y"][:, h, :], m["TI"][:, h, :], start=True, stop=True))
                yield
                after(dve, pe)
                did(dve, TT(m["S"], m["S"], pairs(PV[:, lo]), ALU.subtract))
                if level < LEVELS - 1:
                    did(dve, TT(m["TI"], m["TI"], pairs(PV[:, hi]), ALU.subtract))
            after(pe, dve)
            for h in range(PH):
                did(pe, MM(SC[:, h * P:(h + 1) * P], m["S"][:, h, :], m["VB"][:, h, :], start=True, stop=True))
                did(pe, MM(SC[:, (PH + h) * P:(PH + h + 1) * P], m["KBG"][:, h, :], m["S"][:, h, :], start=True, stop=True))
            yield
            after(act, pe)
            did(act, nc.scalar.activation(flat(m["U"]), SC[:, lo], ACT.Copy))
            did(act, nc.scalar.activation(flat(m["WT"]), SC[:, hi], ACT.Copy))
            yield
            for c in range(P // DC):
                r = slice(c * DC, (c + 1) * DC)
                after(pe, dve, act)
                pe.constant_wait()
                for h in range(PH):
                    did(pe, MM(SC[r, h * P:(h + 1) * P], m["WT"][:, h, r], m["STATE"][:, h, :], start=True, stop=True))
                yield
                after(dve, pe)
                did(dve, TT(m["VN"][r], m["U"][r], pairs(SC[:, lo])[r], ALU.subtract))
                after(pe, dve)
                pe.constant_wait()
                for h in range(PH):
                    hs = slice(h * P, (h + 1) * P)
                    MM(ACC[r, hs], m["QD"][:, h, r], m["STATE"][:, h, :], start=True, stop=False)
                    MM(ACC[r, hs], m["DT"][r, h, r], m["VN"][r, h, :], start=False, stop=True)
                    did(pe, MM(PV[:, hs], m["KD"][r, h, :], m["VN"][r, h, :], start=True, stop=True))
                yield
                at = c * DC + DC - 1
                after(dve, pe)
                for h in range(PH):
                    did(dve, V.scalar_tensor_tensor(m["STATE"][:, h, :], m["STATE"][:, h, :], m["EGR"][:, h, at:at + 1],
                                                    PV[:, h * P:(h + 1) * P], ALU.mult, ALU.add))
            after(act, pe)
            act.constant_wait()
            did(act, nc.scalar.activation(O[:, t, bass.ds(i * CH + s * PH * HD, PH * HD)], ACC[:, lo], ACT.Copy))
            yield
    with prog.turns("deltanet", DH // HQ) as i:
        dve.after(pe, act)
        dve.sync()
        for n, v in h4.items():
            dve.did(V.tensor_copy(v, by(src[n])[:, :, bass.ds(i * HQ, HQ)]))
        dve.did(V.tensor_copy(cw4, DN["conv"].rearrange("p (c n) -> p c n", c=3)[:, :, bass.ds(i * HQ * 4, HQ * 4)]))
        dve.sync()
        pool.after(pe)
        steps = [two_heads(i, s) for s in range(HQ // PH)]
        while steps:
            for g in list(steps):
                if next(g, "over") == "over":
                    steps.remove(g)
    pe.after(act, dve)
    return act.line.now()


def third_layer(core, a, stop):
    nc, prog = core.nc, core.prog
    pe, act, dve, pool = prog.pe, prog.act, prog.dve, prog.pool
    w = a["w_in_2"][0]
    core.at = 0
    MG0, Q2, KV, Z = arena(core, "MG0", [TB, D]), arena(core, "Q2", [TB, N2 * HD]), arena(core, "KV", [TB, 6 * 2 * HD]), arena(core, "Z", [TB, DH * HD])
    MG1 = cut(core, core.arena, 4096, [TB, D])[0]
    rest = core.at
    own = places(core, [(core.arena, rest, ARENA)])
    QKV = cut(core, core.arena, 0, [TB, 3 * DH * HD])[0]
    GT, AB = core.GT, core.AB
    DN, at = {}, 6144
    sizes = dict(ones=P, tri=P, same=P, lower=P, levels=LEVELS * P, conv=24 * 4, dt=DH, alog=DH)
    dn_at = at
    for n, size in sizes.items():
        DN[n], at = cut(core, core.arena, at, [size])
    DN["memory"] = [(core.fixed, 0, core.fixed.shape[1]), (core.arena, at, 9216), (core.arena, rest, ARENA)]
    nc.gpsimd.wait_ge(act.line.sem, act.line.now().value())
    nc.gpsimd.wait_ge(dve.line.sem, dve.line.now().value())
    nc.gpsimd.wait_ge(pe.line.sem, pe.line.now().value())
    nc.gpsimd.wait_ge(core.quad_done.sem, core.quad_done.now().value())
    core.late.tick(nc.gpsimd.dma_start(core.arena[:, dn_at:dn_at + 10 * P], a["dn_consts"]))
    core.late.tick(nc.gpsimd.dma_start(DN["conv"], a["dn_conv"]))
    core.late.tick(nc.gpsimd.dma_start(DN["dt"], a["dt_bias_2"][0].partition_broadcast(P)))
    DN["ready"] = core.late.tick(nc.gpsimd.dma_start(DN["alog"], a["a_log_2"][0].partition_broadcast(P)))
    x_ready = token_norm(core, core.gains[:, 2, :], cut(core, core.arena, rest, [TB, D])[0])
    take = lambda buf, i: copy_to(core, lambda t: buf[:, t, bass.ds(i * CH, CH)])
    gt_quads, ab_quads = quads_of(w, GATE_COL, width=3 * N2), quads_of(w, AB_COL, width=2 * DH)
    dn_quads = lambda c: quads_of(w, DN_COL + c * CH)
    z_quads, q_quads, kv_quads, mg_quads = (lambda c, col=col: quads_of(w, col + c * CH) for col in (Z_COL, Q_COL, KV_COL, MERGE_COL))
    pe.wait(x_ready[-1])
    project(core, gt_quads, copy_to(core, lambda t: GT[:, t, :]), then=ab_quads)
    ab_ready = project(core, ab_quads, copy_to(core, lambda t: AB[:, t, :]), then=dn_quads(0))
    steps, tables = deltanet_gates(core, AB, ab_ready, DN)
    last_chunk = 3 * DH * HD // CH - 1
    qkv_ready = stream(core, "dn_in", last_chunk + 1, dn_quads, lambda i, then: project(
        core, dn_quads(i), take(QKV, i), then=then,
        between=lambda q: steps[q]() if type(i) is int and i == last_chunk and q < len(steps) else None), z_quads(0))
    for e in (pool, dve, pe, act):
        e.wait(qkv_ready, ab_ready)
        e.wait(core.tp_taken.now())
    o_ready = deltanet(core, a, QKV, tables, Z, qkv_ready, DN)
    O, SQ = Z, cut(core, core.fixed, 0, [TB, DH * HD])[0]
    ZG = core.TMP[:, :].rearrange("p (t w) -> p t w", t=TB)
    act.after(pe, dve, pool)
    W1 = cut(core, core.arena, 0, [32, HD])[0]
    CW = own(2 * (HD + 32)).rearrange("p (j w) -> p j w", j=2)
    MC = own(TB * HQ * PADC + HQ + TB)
    KS, BD = own(4 * T).rearrange("p (j t) -> p j t", j=4), own(2 * HQ * HD).rearrange("p (g h d) -> p g h d", g=2, h=HQ)
    KC = own(4 * T).rearrange("p (j t) -> p j t", j=4)
    NG = own(HD)
    GB = own(3 * TB * N2).rearrange("p (b t h) -> p b t h", b=3, t=TB)
    GBS, CS = own(TB * HQ).rearrange("p (t h) -> p t h", t=TB), own(TB * HQ)
    for e in (dve, pe, act):
        nc.gpsimd.wait_ge(e.line.sem, e.line.now().value())
    w1_ready = core.late.tick(nc.gpsimd.dma_start(W1, a["cmp_w1_k_2"][0].rearrange("(i d) e -> d i e", d=HD)))
    for n_j, n in enumerate("kv"):
        core.late.tick(nc.gpsimd.dma_start(CW[:, n_j, 0:HD], a[f"cmp_w2_{n}_2"][0]))
        core.late.tick(nc.gpsimd.dma_start(CW[:, n_j, HD:], a[f"cmp_pe_{n}_2"]))
    core.late.tick(nc.gpsimd.dma_start(NG, a["dn_norm_w_2"][0].partition_broadcast(P)))
    cmp_ready = core.late.tick(nc.gpsimd.dma_start(MC, a["cmp_masks"]))
    cmp_mask = MC[:, 0:TB * HQ * PADC].rearrange("p (t n) -> p t n", t=TB)
    head_of, any_valid = MC[:, TB * HQ * PADC:TB * HQ * PADC + HQ], MC[:, TB * HQ * PADC + HQ:]
    o16 = O.rearrange("p t (h w) -> p (t h) w", w=HD)
    heads = lambda ap: ap.rearrange("p t (h w) -> p t h w", w=HD)
    att, point = core.att, {}

    def with_steps(buf, i, quads, then, steps):
        return project(core, quads(i), take(buf, i), then=then, between=lambda q: steps[q]() if q < len(steps) else None)

    def squares():
        act.wait(o_ready)
        act.did(nc.scalar.activation(SQ, O, ACT.Square))
        dve.after(act)
        dve.did(nc.vector.tensor_reduce(core.ss[:, 0:16], SQ.rearrange("p t (h w) -> p (t h) w", w=HD), AX.X, ALU.add))

    def roots():
        rstd(core, core.ss[:, 0:16], core.rs[:, 0:16], HD, dve.line.now())

    def normalised():
        dve.sync()
        dve.did(nc.vector.tensor_tensor(o16, o16, core.rs[:, 0:16].unsqueeze(2).to_broadcast([P, 16, HD]), ALU.mult))
        dve.wait(cmp_ready)
        dve.sync()
        dve.did(nc.vector.tensor_tensor(o16, o16, NG.unsqueeze(1).to_broadcast([P, 16, HD]), ALU.mult))
    with_steps(ZG, 0, z_quads, z_quads(1), [squares, roots, normalised])
    z_ready = with_steps(ZG, 1, z_quads, kv_quads(0), [])

    def silu_z():
        act.wait(z_ready)
        act.did(nc.scalar.activation(ZG, ZG, ACT.Silu))

    def gated_z():
        dve.after(act)
        point["dn_out"] = dve.did(nc.vector.tensor_tensor(Z, O, ZG, ALU.mult))
    kv0_ready = with_steps(KV, 0, kv_quads, kv_quads(1), [silu_z, gated_z])

    def rope_keys(kind, ready):
        mine = KV[:, :, kind * 2 * HD:(kind + 1) * 2 * HD]
        dve.after(pe)
        dve.sync()
        rope(core, heads(mine), heads(mine), core.cos, core.sin, 2, HD, core.TMP, ready)

    def turn_keys(dst, kinds):
        for j, kind in enumerate(kinds):
            pe.after(dve)
            pe.wait(core.tp_taken.now())
            for h in range(2):
                for t in range(TB):
                    c = (kind * 2 + h) * HD
                    ins = nc.tensor.transpose(core.TP[j][:, (2 * h + t) * P:(2 * h + t + 1) * P], KV[:, t, c:c + HD], core.ident)
            act.wait(pe.did(ins))
            core.tp_taken.tick(nc.scalar.activation(dst[:, 2 * j:2 * j + 2, :].rearrange("p h t -> p (h t)"), core.TP[j][:, :], ACT.Copy))
    BL = core.TMP[:, 0:32 * 2 * NC2].rearrange("p (i c) -> p i c", i=32)
    H1 = [att.LG[j][:, 0:2 * NC2] for j in range(2)]
    KCT, GV4 = att.PR[0][:, 0:2 * PADC], att.PR[1][:, 0:2 * P]

    def blocks(j):
        dve.wait(cmp_ready, core.tp_taken.now())
        dve.after(pe)
        dve.sync()
        for h in range(2):
            x = KC[:, 2 * j + h, :]
            for half in range(2):
                rows = x[:, 16 * half:16 * half + 16 * NC2].rearrange("p (c i) -> p i c", i=16)
                pe_rows = CW[:, j, HD + 16 * half:HD + 16 * half + 16].unsqueeze(2).to_broadcast([P, 16, NC2])
                dve.did(nc.vector.tensor_tensor(BL[:, 16 * half:16 * half + 16, h * NC2:(h + 1) * NC2], rows, pe_rows, ALU.add))

    def hidden_blocks(j):
        pe.wait(w1_ready)
        pe.after(dve, act)
        for i in range(32):
            ins = nc.tensor.matmul(core.SC[j][:, 0:2 * NC2], W1[:, i, :], BL[:, i, :], start=i == 0, stop=i == 31)
        point["hidden"] = pe.did(ins)

    def gelu(j):
        act.wait(point["hidden"])
        act.did(nc.scalar.activation(H1[j], core.SC[j][:, 0:2 * NC2], ACT.Gelu_apprx_tanh))
    pe.wait(cmp_ready)
    kv1_ready = with_steps(KV, 1, kv_quads, kv_quads(2), [
        lambda: rope_keys(0, kv0_ready), lambda: turn_keys(KC, (0, 1)), lambda: blocks(0), lambda: hidden_blocks(0)])
    nc.gpsimd.wait_ge(pe.line.sem, point["hidden"].value())
    w1_ready = core.late.tick(nc.gpsimd.dma_start(W1, a["cmp_w1_v_2"][0].rearrange("(i d) e -> d i e", d=HD)))

    def gelu_and_selected_keys():
        gelu(0)
        rope_keys(2, kv1_ready)
    kv2_ready = with_steps(KV, 2, kv_quads, q_quads(0), [
        gelu_and_selected_keys, lambda: blocks(1), lambda: None, lambda: hidden_blocks(1)])

    def gelu_and_window_keys():
        gelu(1)
        rope_keys(4, kv2_ready)
        dve.did(nc.vector.memset(KCT, 0.0))
        dve.did(nc.vector.memset(GV4, 0.0))

    def compressed_products():
        dve.sync()
        dve.after(act)
        for g in range(2):
            for h in range(HQ):
                c = g * P + h * PADC
                dve.did(nc.vector.tensor_copy(GV4[:, c:c + NC2], H1[1][:, g * NC2:(g + 1) * NC2]))
        pe.after(act, dve)
        pe.did(nc.tensor.matmul(core.SC[0][:, 0:2 * NC2], CW[:, 0, 0:HD], H1[0], start=True, stop=True))
        for g in range(2):
            pe.did(nc.tensor.matmul(core.SC[1][:, g * HD:(g + 1) * HD], GV4[:, g * P:(g + 1) * P], CW[:, 1, 0:HD], start=True, stop=True))

    def compressed_operands():
        dve.after(pe)
        for g in range(2):
            dve.did(nc.vector.tensor_copy(KCT[:, g * PADC:g * PADC + NC2], core.SC[0][:, g * NC2:(g + 1) * NC2]))
            for h in range(HQ):
                dve.did(nc.vector.tensor_scalar(BD[:, g, h, :], core.SC[1][:, g * HD:(g + 1) * HD], head_of[:, h:h + 1], None, ALU.mult))
        act.did(nc.scalar.activation(GT[:, :, :], GT[:, :, :], ACT.Sigmoid))
        gates = GT[:, :, :].rearrange("p t (h b) -> p t h b", b=3)
        dve.after(act)
        for b in range(3):
            dve.did(nc.vector.tensor_copy(GB[:, b], gates[:, :, :, b]))
    q0_ready = with_steps(Q2, 0, q_quads, q_quads(1), [
        gelu_and_window_keys, compressed_products, compressed_operands, lambda: turn_keys(KS, (2, 4))])
    O = core.TMP[:, :].rearrange("p (t w) -> p t w", t=TB)
    RT = cut(core, core.arena, 0, [TB * CH])[0]
    CP = att.LG[0][:, 0:TB * P].rearrange("p (t n) -> p t n", t=TB)
    CPT = att.LG[1][:, 0:TB * P].rearrange("p (t n) -> p t n", t=TB)
    cp = CP[:, :, :].rearrange("p t (h c) -> p (t h) c", c=PADC)
    wide = lambda s: s.unsqueeze(2).to_broadcast([P, TB * HQ, PADC])

    def rope_queries(g, ready):
        mine = heads(Q2[:, :, g * CH:(g + 1) * CH])
        dve.after(pe, act)
        dve.sync()
        rope(core, mine, mine, core.cos, core.sin, GRP, HD, RT, ready)

    def compressed_scores(g):
        pool.after(dve, act)
        act.after(dve)
        q_ready, _ = group_queries(core, Q2[:, :, g * CH:(g + 1) * CH])
        pe.wait(q_ready)
        pe.after(dve)
        for t in range(TB):
            for h in range(HQ):
                c = (t * HQ + h) * PADC
                ins = nc.tensor.matmul(core.SC[0][:, c:c + PADC], att.QT[:, h, t * P:(t + 1) * P], KCT[:, g * PADC:(g + 1) * PADC], start=True, stop=True)
        att.qt_taken.tick(ins)

    def compressed_softmax(g):
        dve.wait(att.qt_taken.now())
        dve.after(act, pe)
        dve.did(nc.vector.scalar_tensor_tensor(CP[:, :, :], core.SC[0][:, 0:TB * HQ * PADC].rearrange("p (t n) -> p t n", t=TB), HD ** -0.5, cmp_mask, ALU.mult, ALU.add))
        dve.sync()
        dve.did(nc.vector.tensor_reduce(CS, cp, AX.X, ALU.max))
        dve.sync()
        dve.did(nc.vector.tensor_tensor(cp, cp, wide(CS), ALU.subtract))
        act.after(dve)
        act.did(nc.scalar.activation(CP[:, :, :], CP[:, :, :], ACT.Exp))
        dve.after(act)
        dve.did(nc.vector.tensor_reduce(CS, cp, AX.X, ALU.add))
        dve.sync()
        dve.did(nc.vector.reciprocal(CS, CS))
        dve.did(nc.vector.tensor_copy(GBS[:, :, :], GB[:, 0, :, g * HQ:(g + 1) * HQ]))
        dve.sync()
        for t in range(TB):
            dve.did(nc.vector.scalar_tensor_tensor(CS[:, t * HQ:(t + 1) * HQ], CS[:, t * HQ:(t + 1) * HQ], any_valid[:, t:t + 1], GBS[:, t, :], ALU.mult, ALU.mult))
        dve.sync()
        dve.did(nc.vector.tensor_tensor(cp, cp, wide(CS), ALU.mult))

    def compressed_outputs(g):
        pe.after(dve)
        pe.wait(core.tp_taken.now())
        for t in range(TB):
            ins = nc.tensor.transpose(core.TP[0][:, t * P:(t + 1) * P], CP[:, t, :], core.ident)
        act.wait(pe.did(ins))
        core.tp_taken.tick(nc.scalar.activation(CPT[:, :, :].rearrange("p t n -> p (t n)"), core.TP[0][:, 0:T], ACT.Copy))
        pe.wait(core.tp_taken.now())
        pe.after(act)
        for t in range(TB):
            pe.did(nc.tensor.matmul(core.PV[t][:, :], CPT[:, t, :], BD[:, g, :, :].rearrange("p h d -> p (h d)"), start=True, stop=True))
        act.after(pe)
        for t in range(TB):
            act.did(nc.scalar.activation(O[:, t, g * CH:(g + 1) * CH], core.PV[t][:, :], ACT.Copy))
    q1_ready = with_steps(Q2, 1, q_quads, mg_quads(0), [
        lambda: rope_queries(0, q0_ready), lambda: compressed_scores(0), lambda: compressed_softmax(0), lambda: compressed_outputs(0)])
    rope_queries(1, q1_ready)
    compressed_scores(1)
    compressed_softmax(1)
    compressed_outputs(1)
    pool.after(dve, act)
    act.after(dve)
    pe.after(dve)
    dn_out = point["dn_out"]
    dve.after(act, pe)
    dve.wait(core.tp_taken.now())
    for b, kind in ((1, 3), (2, 5)):
        def branch(g, then):
            kt = lambda t0, n: KS[:, bass.ds(2 * (b - 1) + g, 1), t0:t0 + n].rearrange("p a n -> p (a n)")
            vt = lambda t: KV[:, t, bass.ds(kind * 2 * HD + g * HD, HD)]
            dve.wait(att.pv_taken.now())
            dve.did(nc.vector.tensor_copy(GBS[:, :, :], GB[:, b, :, bass.ds(g * HQ, HQ)]))

            def add_to(h, pv, multiplied, sum_ready, src_read):
                dve.wait(multiplied, sum_ready)
                for t in range(TB):
                    dve.did(nc.vector.tensor_tensor(att.SUM[:, h, t:t + 1], att.SUM[:, h, t:t + 1], GBS[:, t, h:h + 1], ALU.mult))
                dve.sync()
                for t in range(TB):
                    o = O[:, t, bass.ds(g * CH + h * HD, HD)]
                    ins = nc.vector.scalar_tensor_tensor(o, pv[:, t * HD:(t + 1) * HD], att.SUM[:, h, t:t + 1], o, ALU.mult, ALU.add)
                    p = att.pv_taken.tick(ins) if t else dve.did(ins)
                return p
            between = attend(core, Q2[:, :, bass.ds(g * CH, CH)], kt, vt, core.causal, add_to)
            m = 2 * (b - 1) + g
            return project(core, mg_quads(m), take(MG0, m), then=then, between=between)
        for g in range(2):
            branch(g, mg_quads(2 * (b - 1) + g + 1))
    act.wait(att.pv_taken.now(), att.qt_taken.now(), att.qr_taken.now(), att.pt_taken.now())
    up0, up1 = (lambda c, w=w: quads_of(w, c * CH, 2) for w in (a["w_up_nsa_2"][0], a["w_up_dn_2"][0]))
    act.wait(core.acc_taken.now())

    def merge_gates(i, then):
        def first(q):
            if q < TB:
                m = MG0[:, q, bass.ds(i * CH, CH)]
                act.constant_wait()
                act.did(nc.scalar.activation(m, m, ACT.Sigmoid))
        sigmoid = lambda t, acc: nc.scalar.activation(MG1[:, t, bass.ds(i * CH, CH)], acc, ACT.Sigmoid)
        return project(core, mg_quads(i + 4), (act, sigmoid), then=then, between=first)
    stream(core, "merge_in", 4, lambda c: mg_quads(c + 4), merge_gates, up0(0))
    turn(core, O, ready=att.pv_taken.now(), k_tiles=8)
    x_ready = turn(core, Z, ready=dn_out, k_tiles=8, k0=8)
    pe.wait(x_ready[-1])
    dve.after(act)

    def up(i, then):
        g0 = lambda t: MG0[:, t, bass.ds(i * CH, CH)]
        g1 = lambda t: MG1[:, t, bass.ds(i * CH, CH)]
        gated0 = lambda t, acc: nc.vector.tensor_tensor(g0(t), acc, g0(t), ALU.mult)
        gated1 = lambda t, acc: nc.vector.tensor_tensor(g1(t), acc, g1(t), ALU.mult)
        project(core, up0(i), (dve, gated0), then=up1(i))
        project(core, up1(i), (dve, gated1), then=then, k0=8)
        dve.wait(core.acc_taken.now())
        for t in range(TB):
            dve.did(nc.vector.tensor_tensor(g0(t), g0(t), g1(t), ALU.add))
    stream(core, "up", D // CH, up0, up, quads_of(a["w_o_2"][0], 0))
    x_ready = turn(core, MG0, ready=dve.line.now())
    return add_projection(core, "w_o", a["w_o_2"][0], x_ready, quads_of(a["w_ffn_gate_2"][0], 0))


def feed_forward(core, a, stop):
    nc, prog = core.nc, core.prog
    pe, act, dve = prog.pe, prog.act, prog.dve
    for e in (act, dve):
        e.after(pe, act, dve, prog.pool)
        e.wait(core.x_ready[-1])
    SG, H = core.sb("SG", [P, TB, CH]), core.sb("H", [P, TB, D])
    hid = [core.sb(n, [P, KT_D, T], F32R) for n in ("HH", "HL")]
    x_ready = token_norm(core, core.gains[:, 3, :], H)
    done = 0
    gate_quads, up_quads = (lambda c, w=a[n][0]: quads_of(w, c * CH) for n in ("w_ffn_gate_2", "w_ffn_up_2"))
    down = a["w_ffn_down_2"][0]
    pe.wait(x_ready[-1])
    for part, n in enumerate((4, 4, 3)):
        def hidden(i, then):
            silu = lambda t, acc: nc.scalar.activation(SG[:, t, :], acc, ACT.Silu)
            product = lambda t, acc: nc.vector.tensor_tensor(H[:, t, bass.ds(i * CH, CH)], acc, SG[:, t, :], ALU.mult)
            act.wait(core.acc_taken.now())
            project(core, gate_quads(done + i), (act, silu), then=up_quads(done + i))
            dve.wait(core.acc_taken.now())
            return project(core, up_quads(done + i), (dve, product), then=then)
        act.after(pe)
        h_ready = stream(core, f"ff{part}", n, lambda c: gate_quads(done + c), hidden, quads_of(down, 0, n, row0=done * CH))
        ready = turn(core, H, ready=h_ready, k_tiles=n * QK, xs=hid)
        add_projection(core, f"down{part}", down, ready, gate_quads(done + n) if part < 2 else (), n, done * CH, hid)
        done += n
    if stop == "d":
        return
    nc.gpsimd.wait_ge(dve.line.sem, dve.line.now().value())
    nc.gpsimd.wait_ge(core.acc_taken.sem, core.acc_taken.now().value())
    nc.gpsimd.wait_ge(core.tp_taken.sem, core.tp_taken.now().value())
    gain = H[:, 0, :]
    squares = hid[0][:, :, :].rearrange("p k t -> p (k t)").rearrange("p (t w) -> p t w", t=TB)
    here = core.late.tick(nc.gpsimd.dma_start(gain, a["norm_f_w_2"].partition_broadcast(P)))
    act.after(dve)
    p = sums_of_squares(core, squares, core.x_ready, core.squared)
    rstd(core, core.ss[:, 0:TB], core.rs[:, 0:TB], D, p)
    dve.wait(here, core.x_ready[-1])
    dve.sync()
    for t in range(TB):
        normalised = dve.did(nc.vector.scalar_tensor_tensor(core.X[:, t, :], core.X[:, t, :], core.rs[:, t:t + 1], gain, ALU.mult, ALU.mult))
        core.x_ready[t] = normalised


A_COLS = (0, 2560, 3072)
INDEX_COL = 5120


def program(nc, counts, a, out, stop=None):
    with ExitStack() as ctx:
        prog = Prog(nc, counts, ctx)
        core = memory(nc, prog)
        core.x_ready, core.squared = [None] * TB, 0
        for t in range(TB):
            landed = Line(prog, f"x_landed{t}", 16)
            core.x_ready[t] = landed.tick(nc.sync.dma_start(core.X[:, t, :], a["x"][0, t * P:(t + 1) * P, :]))
        core.small.tick(nc.scalar.dma_start(core.consts[:, :], a["consts"]))
        core.small.tick(nc.scalar.dma_start(core.gains[:, :, :], a["norm_gains"]))
        QKG = core.QKG
        p = core.small.tick(nc.scalar.dma_start(QKG[:, :], a["a_qk_gains"].partition_broadcast(P)))
        core.gains_ready = p
        prog.pe.wait(p)
        attention_layer(core, "a", a["a_w_in"][0], a["a_w_out"][0], core.gains[:, 0, :], QKG, A_COLS,
                        quads_of(a["b_w_in"][0], A_COLS[0]) if stop != "a" else (), indexer)
        if stop != "a":
            nc.gpsimd.wait_ge(prog.dve.line.sem, prog.dve.line.now().value())
            p = core.late.tick(nc.gpsimd.dma_start(QKG[:, :], a["b_qk_gains"].partition_broadcast(P)))
            prog.dve.wait(p)
            attention_layer(core, "b", a["b_w_in"][0], a["b_w_out"][0], core.gains[:, 1, :], QKG, A_COLS,
                            quads_of(a["w_in_2"][0], GATE_COL, width=3 * N2) if stop != "b" else ())
        if stop not in ("a", "b"):
            third_layer(core, a, stop)
        core.mixers.close()
        if stop not in ("a", "b", "c"):
            feed_forward(core, a, stop)
        stored = Line(prog, "x_stored", 16)
        for t in range(TB):
            nc.sync.wait_ge(core.x_ready[t].line.sem, core.x_ready[t].value())
            stored.tick(nc.sync.dma_start(out[0, t * P:(t + 1) * P, :], core.X[:, t, :]))
        nc.sync.wait_ge(stored.sem, stored.now().value())
    return prog.seen


def laid_out(inputs):
    a = {n: np.ascontiguousarray(v) for n, v in inputs.items()}
    cols = lambda v: v.reshape(KT_D, P).T
    out = {n: a[n] for n in ("x", "a_w_in", "a_w_out", "b_w_in", "b_w_out")}
    out["consts"] = shape_constants()
    out["norm_gains"] = np.ascontiguousarray(np.stack([cols(a[n]) for n in ("a_norm", "b_norm", "norm1_w_2", "norm2_w_2")], 1))
    for n in ("w_in_2", "w_up_nsa_2", "w_up_dn_2", "w_o_2", "w_ffn_gate_2", "w_ffn_up_2", "w_ffn_down_2", "dt_bias_2", "a_log_2",
              "dn_norm_w_2", "cmp_w1_k_2", "cmp_w1_v_2", "cmp_w2_k_2", "cmp_w2_v_2", "norm_f_w_2"):
        out[n] = a[n]
    for n in ("cmp_pe_k_2", "cmp_pe_v_2"):
        out[n] = np.ascontiguousarray(a[n][0].T)
    out["dn_conv"] = np.ascontiguousarray(a["conv_w_2"][0, :, 0, :].reshape(4, 24, P).transpose(2, 1, 0).reshape(P, 96))
    out["dn_consts"], out["cmp_masks"] = more_constants()
    for l in ("a", "b"):
        out[l + "_qk_gains"] = np.concatenate([a[l + "_q_norm"][0]] * (NH // GRP) + [a[l + "_k_norm"][0]])
    return out


def kernel(**inputs):
    import concourse.bacc as bacc
    from concourse.bass_utils import run_bass_kernel_spmd
    arrays = laid_out(inputs)
    counts = {}
    for _ in range(2):
        nc = bacc.Bacc("TRN2", target_bir_lowering=False, num_devices=1)
        a = {n: nc.dram_tensor("in_" + n, v.shape, F32, kind="ExternalInput").ap() for n, v in arrays.items()}
        out = nc.dram_tensor("out_0", (1, T, D), F32, kind="ExternalOutput").ap()
        counts = program(nc, counts, a, out)
    r = run_bass_kernel_spmd(nc, [{"in_" + n: v for n, v in arrays.items()}], core_ids=[0])
    return r.results[0]["out_0"]
```
